# Optimizing a Trainium2 kernel written in Bass

```python
import math
import jax
import jax.numpy as jnp
from jax import lax
import numpy as np
import jax, jax.numpy as jnp

D_MODEL = 1024
BATCH = 1
SEQ = 256
DEPTH = 1

GRID_W = 64
CTX_LEN = 256
MIX_W = D_MODEL
GDN_W = MIX_W // 2
GDN_DK = 128
GDN_DV = 128
GDN_HEADS = GDN_W // GDN_DV
SSM_W = MIX_W - GDN_W
SSM_HEADDIM = 64
SSM_HEADS = SSM_W // SSM_HEADDIM
SSM_GROUPS = 2
SSM_STATE = 128
SHORT_CONV = 3
CHUNK = 64
D_FF = ((8 * D_MODEL // 3 + 127) // 128) * 128
FFN_CONV = 3
EPS = 1e-6

GDN_SPLITS = (GDN_HEADS * GDN_DK, GDN_HEADS * GDN_DK, GDN_HEADS * GDN_DV, GDN_W, 2 * GDN_HEADS, 2 * GDN_HEADS)
SSM_SPLITS = (SSM_W, SSM_W, SSM_GROUPS * SSM_STATE, SSM_GROUPS * SSM_STATE, 2 * SSM_HEADS)
IN_DIM = sum(GDN_SPLITS) + sum(SSM_SPLITS)
GDN_CONV_CH = 2 * GDN_HEADS * GDN_DK + GDN_HEADS * GDN_DV
SSM_CONV_CH = SSM_W + 2 * SSM_GROUPS * SSM_STATE


def _split(t, sizes):
    idx = np.cumsum(sizes)[:-1].tolist()
    return jnp.split(t, idx, axis=-1)

def _flip(t):
    return t[:, ::-1]

def rmsnorm(x, g):
    x32 = x.astype(jnp.float32)
    y = x32 * lax.rsqrt(jnp.mean(x32 * x32, axis=-1, keepdims=True) + EPS)
    return (y * g.astype(jnp.float32)).astype(x.dtype)

def l2norm(t):
    t32 = t.astype(jnp.float32)
    return t32 * lax.rsqrt(jnp.sum(t32 * t32, axis=-1, keepdims=True) + EPS)

def modulate(h, shift, scale):
    return h * (1 + scale) + shift

def dwconv1d(u, w, b=None):
    C = u.shape[-1]
    K = w.shape[0]
    out = lax.conv_general_dilated(u, w.reshape(K, 1, C).astype(u.dtype), window_strides=(1,),
                                   padding=((K // 2, K // 2),), dimension_numbers=('NWC', 'WIO', 'NWC'),
                                   feature_group_count=C)
    if b is not None:
        out = out + b
    return out

def dwconv2d_grid(u, w, b):
    Bsz, L, F = u.shape
    rows = L // GRID_W
    img = u.reshape(Bsz, rows, GRID_W, F)
    out = lax.conv_general_dilated(img, w.reshape(FFN_CONV, FFN_CONV, 1, F).astype(u.dtype), window_strides=(1, 1),
                                   padding=((FFN_CONV // 2, FFN_CONV // 2), (FFN_CONV // 2, FFN_CONV // 2)),
                                   dimension_numbers=('NHWC', 'HWIO', 'NHWC'), feature_group_count=F)
    return out.reshape(Bsz, L, F) + b

def gated_delta_chunked(q, k, v, g, beta, S0):
    Bsz, L, H, DK = q.shape
    DV = v.shape[-1]
    NC = L // CHUNK

    def blocks(t):
        t = jnp.moveaxis(t.astype(jnp.float32), 2, 1)
        return t.reshape(Bsz, H, NC, CHUNK, *t.shape[3:])

    q, k, v, g, beta = (blocks(t) for t in (q, k, v, g, beta))
    gc = jnp.cumsum(g, axis=-1)
    pos = jnp.arange(CHUNK)
    lower = pos[:, None] >= pos[None, :]
    decay = jnp.exp(jnp.where(lower, gc[..., :, None] - gc[..., None, :], -jnp.inf))
    kb = k * beta[..., None]
    kk = jnp.einsum('bhnid,bhnjd->bhnij', kb, k) * decay
    rhs = jnp.concatenate([v * beta[..., None], kb * jnp.exp(gc)[..., None]], axis=-1)
    sol = lax.linalg.triangular_solve(kk, rhs, left_side=True, lower=True, unit_diagonal=True)
    u, w = sol[..., :DV], sol[..., DV:]
    qk = jnp.einsum('bhnid,bhnjd->bhnij', q, k) * decay
    q_dec = q * jnp.exp(gc)[..., None]
    k_dec = k * jnp.exp(gc[..., -1:] - gc)[..., None]
    g_last = jnp.exp(gc[..., -1])
    xs = tuple(jnp.moveaxis(t, 2, 0) for t in (u, w, qk, q_dec, k_dec, g_last))

    def step(S, inp):
        u_c, w_c, qk_c, qd_c, kd_c, gl_c = inp
        v_new = u_c - jnp.einsum('bhcd,bhde->bhce', w_c, S)
        o_c = jnp.einsum('bhcd,bhde->bhce', qd_c, S) + jnp.einsum('bhij,bhje->bhie', qk_c, v_new)
        S = S * gl_c[..., None, None] + jnp.einsum('bhcd,bhce->bhde', kd_c, v_new)
        return S, o_c

    S, o = lax.scan(step, S0.astype(jnp.float32), xs)
    o = jnp.moveaxis(o, 0, 2).reshape(Bsz, H, L, DV)
    return jnp.moveaxis(o, 1, 2), S

def ssd_chunked(x, dt, A, Bm, Cm, h0):
    Bsz, L, H, P = x.shape
    G, N = Bm.shape[2], Bm.shape[3]
    R = H // G
    NC = L // CHUNK
    f32 = jnp.float32
    xc = x.astype(f32).reshape(Bsz, NC, CHUNK, G, R, P)
    dtc = dt.astype(f32).reshape(Bsz, NC, CHUNK, G, R)
    Bc = Bm.astype(f32).reshape(Bsz, NC, CHUNK, G, N)
    Cc = Cm.astype(f32).reshape(Bsz, NC, CHUNK, G, N)
    cum = jnp.cumsum(dtc * A.astype(f32).reshape(G, R), axis=2)
    pos = jnp.arange(CHUNK)
    lower = (pos[:, None] >= pos[None, :])[:, :, None, None]
    seg = jnp.exp(jnp.where(lower, cum[:, :, :, None] - cum[:, :, None, :], -jnp.inf))
    cb = jnp.einsum('bnigs,bnjgs->bnijg', Cc, Bc)
    y_diag = jnp.einsum('bnijg,bnijgr,bnjgrp->bnigrp', cb, seg, dtc[..., None] * xc)
    xdt_end = (jnp.exp(cum[:, :, -1:] - cum) * dtc)[..., None] * xc
    states = jnp.einsum('bnjgs,bnjgrp->bngrps', Bc, xdt_end)
    chunk_decay = jnp.exp(cum[:, :, -1])

    def step(h, inp):
        st, dc = inp
        return h * dc[..., None, None] + st, h

    h_fin, h_in = lax.scan(step, h0.astype(f32).reshape(Bsz, G, R, P, N),
                           (jnp.moveaxis(states, 1, 0), jnp.moveaxis(chunk_decay, 1, 0)))
    h_in = jnp.moveaxis(h_in, 0, 1)
    y_off = jnp.einsum('bnigs,bngrps,bnigr->bnigrp', Cc, h_in, jnp.exp(cum))
    y = (y_diag + y_off).reshape(Bsz, L, H, P)
    return y, h_fin.reshape(Bsz, H, P, N)

def token_mixers(h, w_in, gdn_conv_w, gdn_A_log, gdn_dt_bias, gdn_norm_g, ssm_conv_w, ssm_conv_b,
                 ssm_A_log, ssm_dt_bias, ssm_D, ssm_norm_g, states, with_output):
    f32 = jnp.float32
    Bsz, L = h.shape[0], h.shape[1]
    proj = h @ w_in
    q, k, v, z_g, a_g, b_g, z_s, x_s, B_s, C_s, dt_s = _split(proj, GDN_SPLITS + SSM_SPLITS)
    S_gf0, S_gb0, S_sf0, S_sb0 = states

    qkv = jax.nn.silu(dwconv1d(jnp.concatenate([q, k, v], axis=-1), gdn_conv_w))
    q, k, v = _split(qkv, (GDN_HEADS * GDN_DK, GDN_HEADS * GDN_DK, GDN_HEADS * GDN_DV))
    q = l2norm(q.reshape(Bsz, L, GDN_HEADS, GDN_DK)) * (GDN_DK ** -0.5)
    k = l2norm(k.reshape(Bsz, L, GDN_HEADS, GDN_DK))
    v = v.reshape(Bsz, L, GDN_HEADS, GDN_DV)
    a = a_g.reshape(Bsz, L, 2, GDN_HEADS).astype(f32)
    g_log = -jnp.exp(gdn_A_log.astype(f32)) * jax.nn.softplus(a + gdn_dt_bias.astype(f32))
    beta = jax.nn.sigmoid(b_g.reshape(Bsz, L, 2, GDN_HEADS).astype(f32))
    o_f, S_gf = gated_delta_chunked(q, k, v, g_log[:, :, 0], beta[:, :, 0], S_gf0)
    o_b, S_gb = gated_delta_chunked(_flip(q), _flip(k), _flip(v), _flip(g_log[:, :, 1]), _flip(beta[:, :, 1]), S_gb0)

    xBC = jax.nn.silu(dwconv1d(jnp.concatenate([x_s, B_s, C_s], axis=-1), ssm_conv_w, ssm_conv_b))
    xs, Bm, Cm = _split(xBC, (SSM_W, SSM_GROUPS * SSM_STATE, SSM_GROUPS * SSM_STATE))
    xs = xs.reshape(Bsz, L, SSM_HEADS, SSM_HEADDIM)
    Bm = Bm.reshape(Bsz, L, SSM_GROUPS, SSM_STATE)
    Cm = Cm.reshape(Bsz, L, SSM_GROUPS, SSM_STATE)
    dt = jax.nn.softplus(dt_s.reshape(Bsz, L, 2, SSM_HEADS).astype(f32) + ssm_dt_bias.astype(f32))
    A = -jnp.exp(ssm_A_log.astype(f32))
    y_f, S_sf = ssd_chunked(xs, dt[:, :, 0], A[0], Bm, Cm, S_sf0)
    y_b, S_sb = ssd_chunked(_flip(xs), _flip(dt[:, :, 1]), A[1], _flip(Bm), _flip(Cm), S_sb0)
    new_states = (S_gf, S_gb, S_sf, S_sb)
    if not with_output:
        return None, new_states

    o = o_f + _flip(o_b)
    o = rmsnorm(o, gdn_norm_g) * jax.nn.silu(z_g.reshape(Bsz, L, GDN_HEADS, GDN_DV).astype(f32))
    o = o.reshape(Bsz, L, GDN_W)
    y = y_f + _flip(y_b) + ssm_D.astype(f32)[:, None] * xs.astype(f32)
    y = rmsnorm(y.reshape(Bsz, L, SSM_W) * jax.nn.silu(z_s.astype(f32)), ssm_norm_g)
    mix = jnp.concatenate([o, y.astype(f32)], axis=-1).astype(h.dtype)
    return mix, new_states

def conv_glu(h, w_gate, w_up, conv_w, conv_b, w_down, on_grid):
    a = h @ w_gate
    if on_grid:
        a = dwconv2d_grid(a, conv_w, conv_b)
    else:
        a = dwconv1d(a, conv_w[FFN_CONV // 2], conv_b)
    return (jax.nn.silu(a) * (h @ w_up)) @ w_down

def first_inputs(seed: int = 0) -> dict:
    key = jax.random.key(seed)
    ks = jax.random.split(key, 32)
    f32 = jnp.float32

    def nrm(k, shape, scale):
        return jax.random.normal(k, shape, f32) * scale

    def gain(k, shape):
        return 1.0 + 0.05 * jax.random.normal(k, shape, f32)

    def a_log(k, shape):
        return jnp.log(jax.random.uniform(k, shape, f32, 1.0, 16.0))

    def dt_bias(k, shape):
        dtv = jnp.exp(jax.random.uniform(k, shape, f32, math.log(1e-3), math.log(1e-1)))
        return dtv + jnp.log(-jnp.expm1(-dtv))

    return {
        'x': nrm(ks[0], (BATCH, SEQ, D_MODEL), 1.0),
        'c': nrm(ks[1], (BATCH, D_MODEL), 1.0),
        'ctx': nrm(ks[2], (BATCH, CTX_LEN, D_MODEL), 1.0),
        'c_ctx': nrm(ks[3], (D_MODEL,), 1.0),
        'w_ada': nrm(ks[4], (DEPTH, D_MODEL, 6 * D_MODEL), 0.5 * D_MODEL ** -0.5),
        'b_ada': nrm(ks[5], (DEPTH, 6 * D_MODEL), 0.01),
        'norm1_g': gain(ks[6], (DEPTH, D_MODEL)),
        'w_in': nrm(ks[7], (DEPTH, D_MODEL, IN_DIM), D_MODEL ** -0.5),
        'gdn_conv_w': nrm(ks[8], (DEPTH, SHORT_CONV, GDN_CONV_CH), SHORT_CONV ** -0.5),
        'gdn_A_log': a_log(ks[9], (DEPTH, 2, GDN_HEADS)),
        'gdn_dt_bias': dt_bias(ks[10], (DEPTH, 2, GDN_HEADS)),
        'gdn_norm_g': gain(ks[11], (DEPTH, GDN_DV)),
        'ssm_conv_w': nrm(ks[12], (DEPTH, SHORT_CONV, SSM_CONV_CH), SHORT_CONV ** -0.5),
        'ssm_conv_b': nrm(ks[13], (DEPTH, SSM_CONV_CH), 0.02),
        'ssm_A_log': a_log(ks[14], (DEPTH, 2, SSM_HEADS)),
        'ssm_dt_bias': dt_bias(ks[15], (DEPTH, 2, SSM_HEADS)),
        'ssm_D': 1.0 + 0.1 * jax.random.normal(ks[16], (DEPTH, SSM_HEADS), f32),
        'ssm_norm_g': gain(ks[17], (DEPTH, SSM_W)),
        'w_out': nrm(ks[18], (DEPTH, MIX_W, D_MODEL), MIX_W ** -0.5),
        'norm2_g': gain(ks[19], (DEPTH, D_MODEL)),
        'ffn_w_gate': nrm(ks[20], (DEPTH, D_MODEL, D_FF), D_MODEL ** -0.5),
        'ffn_w_up': nrm(ks[21], (DEPTH, D_MODEL, D_FF), D_MODEL ** -0.5),
        'ffn_conv_w': nrm(ks[22], (DEPTH, FFN_CONV, FFN_CONV, D_FF), 1.0 / FFN_CONV),
        'ffn_conv_b': nrm(ks[23], (DEPTH, D_FF), 0.02),
        'ffn_w_down': nrm(ks[24], (DEPTH, D_FF, D_MODEL), D_FF ** -0.5),
        'final_norm_g': gain(ks[25], (D_MODEL,)),
    }

def first_block(x, c, ctx, c_ctx, w_ada, b_ada, norm1_g, w_in, gdn_conv_w, gdn_A_log, gdn_dt_bias, gdn_norm_g,
              ssm_conv_w, ssm_conv_b, ssm_A_log, ssm_dt_bias, ssm_D, ssm_norm_g, w_out, norm2_g,
              ffn_w_gate, ffn_w_up, ffn_conv_w, ffn_conv_b, ffn_w_down, final_norm_g):
    f32 = jnp.float32
    Bsz = x.shape[0]
    for l in range(DEPTH):
        last = l == DEPTH - 1
        mod = jax.nn.silu(c) @ w_ada[l] + b_ada[l]
        mod_c = jax.nn.silu(c_ctx) @ w_ada[l] + b_ada[l]
        sh1, sc1, g1, sh2, sc2, g2 = jnp.split(mod[:, None, :], 6, axis=-1)
        sh1c, sc1c, g1c, sh2c, sc2c, g2c = jnp.split(mod_c, 6, axis=-1)
        mixer_params = (w_in[l], gdn_conv_w[l], gdn_A_log[l], gdn_dt_bias[l], gdn_norm_g[l], ssm_conv_w[l],
                        ssm_conv_b[l], ssm_A_log[l], ssm_dt_bias[l], ssm_D[l], ssm_norm_g[l])
        ffn_params = (ffn_w_gate[l], ffn_w_up[l], ffn_conv_w[l], ffn_conv_b[l], ffn_w_down[l])
        zero_states = (jnp.zeros((Bsz, GDN_HEADS, GDN_DK, GDN_DV), f32),
                       jnp.zeros((Bsz, GDN_HEADS, GDN_DK, GDN_DV), f32),
                       jnp.zeros((Bsz, SSM_HEADS, SSM_HEADDIM, SSM_STATE), f32),
                       jnp.zeros((Bsz, SSM_HEADS, SSM_HEADDIM, SSM_STATE), f32))
        hc = modulate(rmsnorm(ctx, norm1_g[l]), sh1c, sc1c)
        mix_c, ctx_states = token_mixers(hc, *mixer_params, zero_states, not last)
        hx = modulate(rmsnorm(x, norm1_g[l]), sh1, sc1)
        mix_x, _ = token_mixers(hx, *mixer_params, ctx_states, True)
        x = x + g1 * (mix_x @ w_out[l])
        x = x + g2 * conv_glu(modulate(rmsnorm(x, norm2_g[l]), sh2, sc2), *ffn_params, True)
        if not last:
            ctx = ctx + g1c * (mix_c @ w_out[l])
            ctx = ctx + g2c * conv_glu(modulate(rmsnorm(ctx, norm2_g[l]), sh2c, sc2c), *ffn_params, False)
    return rmsnorm(x, final_norm_g)


HEAD_DIM = 64
MIX_WIDTH = D_MODEL
A_HEADS = MIX_WIDTH // (2 * HEAD_DIM)
A_KV_HEADS = max(1, A_HEADS // 4)
B_HEADS = MIX_WIDTH // HEAD_DIM - A_HEADS
A_WIDTH = A_HEADS * HEAD_DIM
A_KV_WIDTH = A_KV_HEADS * HEAD_DIM
B_WIDTH = B_HEADS * HEAD_DIM
IN_WIDTH = A_WIDTH + 2 * A_KV_WIDTH + 3 * B_WIDTH
IN_SPLITS = (A_WIDTH, A_WIDTH + A_KV_WIDTH, A_WIDTH + 2 * A_KV_WIDTH,
             A_WIDTH + 2 * A_KV_WIDTH + B_WIDTH, A_WIDTH + 2 * A_KV_WIDTH + 2 * B_WIDTH)
ROPE_THETA = 10000.0
Q_BLOCK = 128
DILATED_PATTERNS = ((128, 1), (512, 4), (2048, 16))
SUBSEQ_BLOCK = 64
N_GROUPS = 4
EXPERTS_PER_GROUP = 8
N_EXPERTS = N_GROUPS * EXPERTS_PER_GROUP
TOP_K = 2
D_EXPERT = D_MODEL // 2
MOE_BLOCK = 512
NEG_INF = -1e30


def _rms_norm(x, g):
    xf = x.astype(jnp.float32)
    y = xf * lax.rsqrt(jnp.mean(xf * xf, axis=-1, keepdims=True) + EPS)
    return (y * g.astype(jnp.float32)).astype(x.dtype)

def _rope_inv_freq(dim):
    return 1.0 / (ROPE_THETA ** (jnp.arange(0, dim, 2, dtype=jnp.float32) / dim))

def _apply_rotary(x, angles):
    cos, sin = jnp.cos(angles), jnp.sin(angles)
    xf = x.astype(jnp.float32)
    x1, x2 = jnp.split(xf, 2, axis=-1)
    return jnp.concatenate([x1 * cos - x2 * sin, x2 * cos + x1 * sin], axis=-1).astype(x.dtype)

def _axial_angles(seq_len):
    rows = seq_len // GRID_W
    row = jnp.repeat(jnp.arange(rows, dtype=jnp.float32), GRID_W)
    col = jnp.tile(jnp.arange(GRID_W, dtype=jnp.float32), rows)
    f = _rope_inv_freq(HEAD_DIM // 2)
    return jnp.concatenate([row[:, None] * f, col[:, None] * f], axis=-1)

def _linear_angles(seq_len):
    t = jnp.arange(seq_len, dtype=jnp.float32)
    return t[:, None] * _rope_inv_freq(HEAD_DIM)

def _global_axial_gqa(q, k, v, q_norm_g, k_norm_g):
    b, s, _ = q.shape
    grp = A_HEADS // A_KV_HEADS
    q = q.reshape(b, s, A_KV_HEADS, grp, HEAD_DIM).transpose(0, 2, 3, 1, 4)
    k = k.reshape(b, s, A_KV_HEADS, HEAD_DIM).transpose(0, 2, 1, 3)
    v = v.reshape(b, s, A_KV_HEADS, HEAD_DIM).transpose(0, 2, 1, 3)
    ang = _axial_angles(s)
    q = _apply_rotary(_rms_norm(q, q_norm_g), ang)
    k = _apply_rotary(_rms_norm(k, k_norm_g), ang)
    nq = s // Q_BLOCK
    qb = jnp.moveaxis(q.reshape(b, A_KV_HEADS, grp, nq, Q_BLOCK, HEAD_DIM), 3, 0)
    scale = HEAD_DIM ** -0.5

    def block(qblk):
        sc = jnp.einsum('bkgqd,bksd->bkgqs', qblk, k, preferred_element_type=jnp.float32) * scale
        p = jax.nn.softmax(sc, axis=-1).astype(v.dtype)
        return jnp.einsum('bkgqs,bksd->bkgqd', p, v)

    o = lax.map(block, qb)
    o = jnp.moveaxis(o, 0, 3).reshape(b, A_KV_HEADS, grp, s, HEAD_DIM)
    return o.transpose(0, 3, 1, 2, 4).reshape(b, s, A_WIDTH)

def _dilated_window(q, k, v, window, dilation):
    b, h, s, d = q.shape
    r = window // (2 * dilation)
    L = s // dilation

    def to_sub(t):
        return t.reshape(b, h, L, dilation, d).transpose(0, 1, 3, 2, 4)

    qs, ks, vs = to_sub(q), to_sub(k), to_sub(v)
    nblk = -(-L // SUBSEQ_BLOCK)
    lp = nblk * SUBSEQ_BLOCK
    pad4 = ((0, 0), (0, 0), (0, 0))
    qs = jnp.pad(qs, pad4 + ((0, lp - L), (0, 0)))
    kpad = jnp.pad(ks, pad4 + ((r, lp - L + r), (0, 0)))
    vpad = jnp.pad(vs, pad4 + ((r, lp - L + r), (0, 0)))
    kwin = SUBSEQ_BLOCK + 2 * r
    kidx = jnp.arange(nblk)[:, None] * SUBSEQ_BLOCK + jnp.arange(kwin)[None, :]
    kb = jnp.take(kpad, kidx, axis=3)
    vb = jnp.take(vpad, kidx, axis=3)
    qb = qs.reshape(b, h, dilation, nblk, SUBSEQ_BLOCK, d)
    sc = jnp.einsum('bhrnqd,bhrnkd->bhrnqk', qb, kb, preferred_element_type=jnp.float32) * (d ** -0.5)
    qpos = jnp.arange(lp).reshape(nblk, SUBSEQ_BLOCK)
    kpos = kidx - r
    mask = (jnp.abs(qpos[:, :, None] - kpos[:, None, :]) <= r) & ((kpos >= 0) & (kpos < L))[:, None, :]
    sc = jnp.where(mask, sc, NEG_INF)
    m = jnp.max(sc, axis=-1, keepdims=True)
    p = jnp.exp(sc - m)
    den = jnp.sum(p, axis=-1, keepdims=True)
    o = jnp.einsum('bhrnqk,bhrnkd->bhrnqd', p.astype(vb.dtype), vb,
                   preferred_element_type=jnp.float32) / den
    lse = (m + jnp.log(den))[..., 0]
    o = o.astype(v.dtype).reshape(b, h, dilation, lp, d)[:, :, :, :L]
    o = o.transpose(0, 1, 3, 2, 4).reshape(b, h, s, d)
    lse = lse.reshape(b, h, dilation, lp)[:, :, :, :L].transpose(0, 1, 3, 2).reshape(b, h, s)
    return o, lse

def _longnet_mixture(q, k, v):
    b, s, _ = q.shape
    q = q.reshape(b, s, B_HEADS, HEAD_DIM).transpose(0, 2, 1, 3)
    k = k.reshape(b, s, B_HEADS, HEAD_DIM).transpose(0, 2, 1, 3)
    v = v.reshape(b, s, B_HEADS, HEAD_DIM).transpose(0, 2, 1, 3)
    ang = _linear_angles(s)
    q = _apply_rotary(q, ang)
    k = _apply_rotary(k, ang)
    outs, lses = [], []
    for window, dilation in DILATED_PATTERNS:
        o, lse = _dilated_window(q, k, v, window, dilation)
        outs.append(o)
        lses.append(lse)
    w = jax.nn.softmax(jnp.stack(lses, axis=0), axis=0).astype(v.dtype)
    o = jnp.einsum('pbhs,pbhsd->bhsd', w, jnp.stack(outs, axis=0))
    return o.transpose(0, 2, 1, 3).reshape(b, s, B_WIDTH)

def _hierarchical_moe(x, router_group_w, router_group_b, router_expert_w, router_expert_b,
                      w_gate, w_up, w_down):
    b, s, dm = x.shape
    n = b * s
    xt = x.reshape(n, dm)
    g_logits = (xt @ router_group_w).astype(jnp.float32) + router_group_b.astype(jnp.float32)
    g_prob = jax.nn.softmax(g_logits, axis=-1)
    g_top_p, g_top = lax.top_k(g_prob, 1)
    e_logits = (xt @ router_expert_w).astype(jnp.float32) + router_expert_b.astype(jnp.float32)
    e_logits = e_logits.reshape(n, N_GROUPS, EXPERTS_PER_GROUP)
    e_in_group = jnp.take_along_axis(e_logits, g_top[:, :, None], axis=1)[:, 0]
    e_top_logit, e_top = lax.top_k(e_in_group, TOP_K)
    gates = g_top_p * jax.nn.softmax(e_top_logit, axis=-1)
    expert_id = g_top * EXPERTS_PER_GROUP + e_top

    nk = n * TOP_K
    flat_e = expert_id.reshape(nk).astype(jnp.int32)
    flat_tok = jnp.arange(nk, dtype=jnp.int32) // TOP_K
    flat_gate = gates.reshape(nk)
    order = jnp.argsort(flat_e)
    se = flat_e[order]
    counts = jnp.bincount(flat_e, length=N_EXPERTS)
    start = jnp.cumsum(counts) - counts
    padded = (counts + MOE_BLOCK - 1) // MOE_BLOCK * MOE_BLOCK
    pend = jnp.cumsum(padded)
    pstart = pend - padded
    dest = pstart[se] + (jnp.arange(nk, dtype=jnp.int32) - start[se])
    n_blocks = -(-nk // MOE_BLOCK) + N_EXPERTS
    rows = n_blocks * MOE_BLOCK
    row_tok = jnp.zeros((rows,), jnp.int32).at[dest].set(flat_tok[order])
    row_gate = jnp.zeros((rows,), x.dtype).at[dest].set(flat_gate[order].astype(x.dtype))
    block_e = jnp.minimum(jnp.searchsorted(pend, jnp.arange(n_blocks) * MOE_BLOCK, side='right'),
                          N_EXPERTS - 1).astype(jnp.int32)

    def expert_block(args):
        e, tok = args
        xb = xt[tok]
        hdn = jax.nn.silu(xb @ w_gate[e]) * (xb @ w_up[e])
        return hdn @ w_down[e]

    yb = lax.map(expert_block, (block_e, row_tok.reshape(n_blocks, MOE_BLOCK)))
    y = jnp.zeros((n, dm), x.dtype).at[row_tok].add(yb.reshape(rows, dm) * row_gate[:, None])
    return y.reshape(b, s, dm)

def second_inputs(seed: int = 0) -> dict:
    key = jax.random.key(seed)
    ks = jax.random.split(key, 20)
    f32 = jnp.float32

    def nrm(k, shape, scale):
        return jax.random.normal(k, shape, f32) * scale

    def gain(k, shape):
        return 1.0 + 0.02 * jax.random.normal(k, shape, f32)

    return {
        "x": jax.random.normal(ks[0], (BATCH, SEQ, D_MODEL), f32),
        "norm1_g": gain(ks[1], (DEPTH, D_MODEL)),
        "w_in": nrm(ks[2], (DEPTH, D_MODEL, IN_WIDTH), D_MODEL ** -0.5),
        "q_norm_g": gain(ks[3], (DEPTH, HEAD_DIM)),
        "k_norm_g": gain(ks[4], (DEPTH, HEAD_DIM)),
        "out_norm_a_g": gain(ks[5], (DEPTH, A_WIDTH)),
        "out_norm_b_g": gain(ks[6], (DEPTH, B_WIDTH)),
        "w_out": nrm(ks[7], (DEPTH, MIX_WIDTH, D_MODEL), MIX_WIDTH ** -0.5),
        "norm2_g": gain(ks[8], (DEPTH, D_MODEL)),
        "router_group_w": nrm(ks[9], (DEPTH, D_MODEL, N_GROUPS), D_MODEL ** -0.5),
        "router_group_b": nrm(ks[10], (DEPTH, N_GROUPS), 0.01),
        "router_expert_w": nrm(ks[11], (DEPTH, D_MODEL, N_EXPERTS), D_MODEL ** -0.5),
        "router_expert_b": nrm(ks[12], (DEPTH, N_EXPERTS), 0.01),
        "w_gate": nrm(ks[13], (DEPTH, N_EXPERTS, D_MODEL, D_EXPERT), D_MODEL ** -0.5),
        "w_up": nrm(ks[14], (DEPTH, N_EXPERTS, D_MODEL, D_EXPERT), D_MODEL ** -0.5),
        "w_down": nrm(ks[15], (DEPTH, N_EXPERTS, D_EXPERT, D_MODEL), D_EXPERT ** -0.5),
        "final_norm_g": gain(ks[16], (D_MODEL,)),
    }

def second_block(x, norm1_g, w_in, q_norm_g, k_norm_g, out_norm_a_g, out_norm_b_g, w_out,
              norm2_g, router_group_w, router_group_b, router_expert_w, router_expert_b,
              w_gate, w_up, w_down, final_norm_g):
    h = x
    for l in range(DEPTH):
        u = _rms_norm(h, norm1_g[l])
        proj = u @ w_in[l]
        qa, ka, va, qb, kb, vb = jnp.split(proj, IN_SPLITS, axis=-1)
        oa = _rms_norm(_global_axial_gqa(qa, ka, va, q_norm_g[l], k_norm_g[l]), out_norm_a_g[l])
        ob = _rms_norm(_longnet_mixture(qb, kb, vb), out_norm_b_g[l])
        h = h + jnp.concatenate([oa, ob], axis=-1) @ w_out[l]
        h = h + _hierarchical_moe(_rms_norm(h, norm2_g[l]), router_group_w[l], router_group_b[l],
                                  router_expert_w[l], router_expert_b[l],
                                  w_gate[l], w_up[l], w_down[l])
    return _rms_norm(h, final_norm_g)


def setup_inputs(seed=0):
    out = dict(first_inputs(seed))
    for name, value in second_inputs(seed + 1).items():
        if name != "x":
            out[name + "_2"] = value
    return out


def reference(
    x, c, ctx, c_ctx, w_ada, b_ada, norm1_g, w_in, gdn_conv_w, gdn_A_log, gdn_dt_bias,
    gdn_norm_g, ssm_conv_w, ssm_conv_b, ssm_A_log, ssm_dt_bias, ssm_D, ssm_norm_g, w_out,
    norm2_g, ffn_w_gate, ffn_w_up, ffn_conv_w, ffn_conv_b, ffn_w_down, final_norm_g, norm1_g_2,
    w_in_2, q_norm_g_2, k_norm_g_2, out_norm_a_g_2, out_norm_b_g_2, w_out_2, norm2_g_2,
    router_group_w_2, router_group_b_2, router_expert_w_2, router_expert_b_2, w_gate_2, w_up_2,
    w_down_2, final_norm_g_2,
):
    x = first_block(
        x, c, ctx, c_ctx, w_ada, b_ada, norm1_g, w_in, gdn_conv_w, gdn_A_log, gdn_dt_bias,
        gdn_norm_g, ssm_conv_w, ssm_conv_b, ssm_A_log, ssm_dt_bias, ssm_D, ssm_norm_g, w_out,
        norm2_g, ffn_w_gate, ffn_w_up, ffn_conv_w, ffn_conv_b, ffn_w_down, final_norm_g,
    )
    return second_block(
        x, norm1_g_2, w_in_2, q_norm_g_2, k_norm_g_2, out_norm_a_g_2, out_norm_b_g_2, w_out_2,
        norm2_g_2, router_group_w_2, router_group_b_2, router_expert_w_2, router_expert_b_2,
        w_gate_2, w_up_2, w_down_2, final_norm_g_2,
    )


_drawn_inputs = setup_inputs


def setup_inputs(seed=0):
    import zlib

    import numpy as np

    out = dict(_drawn_inputs(seed))
    spreads = {}
    factors = {'ffn_conv_b': 3.762,
     'q_norm_g_2': 3.066,
     'k_norm_g_2': 4.416,
     'out_norm_a_g_2': 11.465,
     'out_norm_b_g_2': 11.508,
     'router_group_b_2': 12.219,
     'router_expert_b_2': 22.27,
     'final_norm_g_2': 7.333,
     'norm2_g_2': 4.668}
    for name, (base, spread) in spreads.items():
        noise = np.random.default_rng([zlib.crc32(name.encode()), seed]).standard_normal(out[name].shape)
        drawn = base * np.exp(spread * noise) if base else spread * noise
        out[name] = jnp.asarray(drawn.astype(out[name].dtype))
    for name, factor in factors.items():
        out[name] = (out[name] * factor).astype(out[name].dtype)
    return out
```

```python
import math
from contextlib import ExitStack

import concourse.bass as bass
from concourse import mybir

P = 128
D = 1024
L = 256
T = L // P
KD = D // P
EPS = 1e-6
GH, SH, SG, SP_ = 4, 8, 2, 64
FF = 2816
KF = FF // P
ARENA = 28600
NE, DE, SLOT = 32, 512, 64
NPAIR = NE // 2
HD = 64
SCALE = HD ** -0.5
LEVELS = 7
GRID = 64

WQ, WK, WV, WZG = 0, 512, 1024, 1536
WZS, WXS, WBC = 2064, 2576, 3088
ROWS = {}
_at = 0
for _name, _n in (("b_ada", 48), ("norm1", 8), ("norm2", 8), ("gconv", 36), ("sconv", 24), ("sconvb", 8),
                  ("mixg", 8), ("n1b", 8), ("outab", 8), ("n2b", 8), ("fconv", 9 * KF), ("fconvb", KF)):
    ROWS[_name] = _at
    _at += _n
NROWS = 3 * P
assert _at <= NROWS
RV = {}
_at = 0
for _name, _n in (("dtb", 24), ("alog", 24), ("ssmD", 8), ("qn", 64), ("kn", 64), ("rb", 36)):
    RV[_name] = _at
    _at += _n
NRV = _at
CO = {}
_at = 0
for _name, _n in (("ident", P), ("ones", P), ("mf", P), ("mb", P), ("lvl", 2 * LEVELS * P), ("strict", P),
                  ("iota", SLOT), ("desc", NE), ("eps", 4), ("rope", 2 * T * 2 * HD)):
    CO[_name] = _at
    _at += _n
NCO = _at


def build(nc, ap, out):
    f32, i32 = mybir.dt.float32, mybir.dt.int32
    ACT, ALU, AX = mybir.ActivationFunctionType, mybir.AluOpType, mybir.AxisListType.X
    MUL, ADD, SUB = ALU.mult, ALU.add, ALU.subtract
    stack = ExitStack()
    with stack:
        sems = {}

        def S(name):
            if name not in sems:
                sems[name] = stack.enter_context(nc.semaphore(name))
            return sems[name]

        ring = stack.enter_context(nc.sbuf_tensor("ring", [P, 6 * 4096], f32))
        A = stack.enter_context(nc.sbuf_tensor("arena", [P, ARENA], f32))
        niter_t = stack.enter_context(nc.sbuf_tensor("niter", [P, 2], i32))
        ps = [stack.enter_context(nc.psum_tensor(f"bank{i}", [P, 512], f32)) for i in range(8)]

        top = [0]

        def take(n, at=None):
            a = top[0] if at is None else at
            if at is None:
                top[0] += n
            assert a + n <= ARENA, (a, n)
            return A[:, a:a + n]

        co = take(NCO)
        C = lambda k, n: co[:, CO[k]:CO[k] + n]
        ident, ones = C("ident", P), C("ones", P)
        mask = [C("mf", P), C("mb", P)]
        lvl = [[co[:, CO["lvl"] + (d * LEVELS + l) * P:CO["lvl"] + (d * LEVELS + l + 1) * P] for l in range(LEVELS)]
               for d in range(2)]
        col = take(NROWS)
        V = lambda k, i, n=1: col[:, ROWS[k] + i:ROWS[k] + i + n]
        rowv = take(NRV)
        R = lambda k, n: rowv[:, RV[k]:RV[k] + n]
        mod = take(96).rearrange("p (j c) -> p j c", c=2)
        scale1 = take(16).rearrange("p (j c) -> p j c", c=2)
        scale2 = take(8)
        stat = take(32)
        rstd = take(32)
        yoff = take(512)
        x = take(T * D).rearrange("p (t n) -> p t n", t=T)
        F0 = top[0]

        def lay(at, n):
            assert F0 + at + n <= ARENA, (at, n)
            return A[:, F0 + at:F0 + at + n]

        def tiles(v, t):
            return v.rearrange("p (t n) -> p t n", t=t)

        kT, BT = tiles(lay(0, 2048), 4), tiles(lay(2048, 1024), 2)
        CT, qT = tiles(lay(3072, 512), 2), tiles(lay(3584, 1024), 4)
        vN, kN, xsN = tiles(lay(4608, 2048), 4), tiles(lay(6656, 2048), 4), tiles(lay(8704, 2048), 4)
        BN, Z = tiles(lay(10752, 1024), 4), tiles(lay(11776, 2048), 2)
        hT, ctx = tiles(lay(13824, 4096), KD), tiles(lay(17920, 2048), 2)
        St = lay(13824, 1024).rearrange("p (d h e) -> p d h e", d=2, h=4)
        ht = tiles(lay(14848, 1024), 2)
        vnew = [tiles(lay(15872 + 512 * d, 512), 4) for d in range(2)]
        xdt, xde = lay(16896, 512), lay(17408, 512)
        Ws = tiles(lay(17920, 1024), 8)
        CBs = lay(18944, 512).rearrange("p (t g i) -> p t g i", t=T, g=2)
        gx = tiles(lay(19968, 128), 4)
        G, dtv, gtmp, gc, egc, kd, etot, dtkd = (tiles(lay(20096 + 96 * i, 96), 4) for i in range(8))
        beta, nbeta, nega = tiles(lay(20864, 32), 4), tiles(lay(20896, 32), 4), lay(20928, 24)
        oacc, yacc = kN[:, 2:4, :], vN[:, 2:4, :]

        def scratch(at, n):
            return ring[:, 4 * 4096 + at:4 * 4096 + at + n]

        xn = tiles(scratch(0, 4096), 4)
        cconv = [scratch(4096 + 512 * i, 512) for i in range(2)]
        csilu = [scratch(5120 + 512 * i, 512) for i in range(3)]
        sqb = [scratch(6656 + 512 * i, 512) for i in range(2)]
        vecs = scratch(6656, 3 * P)
        craw = scratch(7680, 16).rearrange("p (k c) -> p k c", c=2)
        csil = scratch(7696, 16).rearrange("p (k c) -> p k c", c=2)
        wsm = tiles(scratch(7712, 256), KD)
        junk0 = scratch(4096, 1024)
        E, NT, PT, Pv, X, XT, Mn0, Mn1 = ([tiles(scratch(4096 * d + 512 * i, 512), 4) for d in range(2)]
                                          for i in range(8))
        Mn = [[Mn0[d], Mn1[d]] for d in range(2)]
        pA, pB, pC, pD = [ps[0], ps[4]], [ps[1], ps[5]], [ps[2], ps[6]], [ps[3], ps[7]]

        mixT, g1r, g2r = tiles(lay(0, 2048), KD), lay(2048, D), lay(3072, D)
        dg = [lay(4096 + P * i, P) for i in range(2)]
        hid = tiles(lay(4608, KF * L), KF)
        fng = [lay(10240, D), lay(11264, 512)]
        tmpx = [lay(12288 + 512 * i, 512) for i in range(2)]
        xh, hT2 = tiles(lay(13824, 2048), 2), tiles(lay(15872, 2048), KD)
        fa, fs = [lay(17920 + L * i, L) for i in range(2)], [lay(18432 + L * i, L) for i in range(2)]
        junk = lay(18944, 1024)
        n2row = lay(19968, D)
        fng2 = lay(20992, D)
        fng1 = lay(10240, D)

        pj = tiles(lay(0, 4608), 2)
        rotb = tiles(lay(4608, 2048), 2)
        rota = tiles(lay(6656, 1280), 2)
        on = tiles(lay(4608, 2048), 2)
        sc = [tiles(lay(7936 + 512 * i, 512), 2) for i in range(2)]
        pr = [tiles(lay(8960 + 512 * i, 512), 2) for i in range(2)]
        mx, sm = (lay(9984 + 32 * i, 32).rearrange("p (h t) -> p h t", t=2) for i in range(2))
        prT = [lay(12288 + 512 * i, 512).rearrange("p (k t q) -> p k t q", k=2, t=2) for i in range(2)]
        bias = tiles(lay(13312, 512), 2)
        sqo = tiles(lay(6656, 1024), 2)
        qkT = tiles(scratch(0, 26 * L), 26)
        uT = hT2

        u2, u2T = tiles(lay(0, 2048), 2), hT2
        rw, lg = tiles(lay(2048, 288), KD), tiles(lay(2336, 72), 2)
        ra = [tiles(lay(2408 + 64 * i, 64), 2) for i in range(6)]
        rs = lay(2792, 32).rearrange("p (j t) -> p j t", t=2)
        SL, GT = tiles(lay(2824, 264), 2), tiles(lay(3088, 264), 2)
        cur = lay(3352, 8).rearrange("p (c t e) -> p c t e", c=2, t=2)
        sel, gsel = tiles(lay(3360, 256), 2), tiles(lay(3616, 256), 2)
        sg, gselT = tiles(lay(3872, 256), 4), lay(4128, 256)
        cnt = lay(4384, 40)
        xsel, hide = tiles(lay(4608, 1024), KD), [tiles(lay(5632 + 256 * i, 256), 4) for i in range(2)]
        ysb, yN = tiles(lay(6144, 1024), KD), lay(7168, D)

        def item(i):
            g, s = ROWS["gconv"], ROWS["sconv"]
            if i < 4:
                return 512, [g + 12 * a + 4 + i for a in range(3)], None, kT[:, i, :]
            if i < 8:
                return 512, [g + 12 * a + 4 + i for a in range(3)], None, csilu[i % 3]
            if i < 12:
                return 512, [s + 8 * a + i - 8 for a in range(3)], ROWS["sconvb"] + i - 8, csilu[i % 3]
            if i < 14:
                return 512, [s + 8 * a + i - 8 for a in range(3)], ROWS["sconvb"] + i - 8, BT[:, i - 12, :]
            if i < 16:
                return L, [s + 8 * a + i - 8 for a in range(3)], ROWS["sconvb"] + i - 8, CT[:, i - 14, :]
            return L, [g + 12 * a + i - 16 for a in range(3)], None, qT[:, i - 16, :]

        def tile_of(u, d):
            step = u % 2
            return (step if d == 0 else 1 - step) + (2 if u < 2 else 0)

        def pieces(u, l):
            if u < 2:
                return {1: [(0, "e")], 3: [(1, "e")]}.get(l, [])
            return {1: [(0, "a")], 2: [(0, "b")], 3: [(0, "e"), (0, "c")], 4: [(1, "a")], 5: [(1, "b")],
                    6: [(1, "e"), (1, "c")]}.get(l, [])

        def heads(v, n, e):
            return v.rearrange("p (h e) -> p h e", h=n, e=e)

        def wide(v, n):
            return v.unsqueeze(2).to_broadcast([P, v.shape[1], n])

        def each(v, h):
            return v.unsqueeze(1).to_broadcast([P, h, v.shape[1]])

        def rope(kind, t):
            at = CO["rope"] + (kind * T + t) * 2 * HD
            return co[:, at:at + HD], co[:, at + HD:at + 2 * HD]

        def slot(s):
            return ring[:, s * 4096:(s + 1) * 4096]

        chunks = []

        def cols(w, c0, n):
            return (lambda s: slot(s)[:, 0:KD * n].rearrange("p (k n) -> p k n", k=KD),
                    w[:, c0:c0 + n].rearrange("(k p) n -> p k n", p=P))

        def rows(w, k0, nk):
            return (lambda s: slot(s)[:, 0:nk * D].rearrange("p (k n) -> p k n", k=nk),
                    w[k0 * P:(k0 + nk) * P, :].rearrange("(k p) n -> p k n", p=P))

        def add(view, done, value):
            chunks.append((view, done, value))
            return len(chunks) - 1

        ada_ch = [add(cols(ap["w_ada"], 512 * i, 512), "ada_ps", i + 1) for i in range(4)]
        proj_ch = []
        PROJ = (WK, WV, WXS, WBC, WQ, WZG, WZS)
        PEND = (4, 8, 12, 16, 20, 22, 24)
        for i, c0 in enumerate(PROJ):
            proj_ch.append(add(cols(ap["w_in"], c0, 512), "item_ps", PEND[i]))
            ada_ch.append(add(cols(ap["w_ada"], 512 * (4 + i), 512), "ada_ps", 5 + i))
        ada_ch.append(add(cols(ap["w_ada"], 512 * 11, 512), "ada_ps", 12))
        wo_ch = [add(cols(ap["w_out"], 512 * c, 512), "wo_ps", 2 * c + 2) for c in range(2)]
        ga_ch, up_ch = [], []
        for c in range(6):
            n = min(512, FF - 512 * c)
            ga_ch.append(add(cols(ap["w_gate"], 512 * c, n), "gate_ps", min(4 * c + 4, KF)))
            up_ch.append(add(cols(ap["w_up"], 512 * c, n), "up_ps", min(4 * c + 4, KF)))
        dn_ch = [add(rows(ap["w_down"], 4 * c, min(4, KF - 4 * c)), "down_ps", c + 1) for c in range(6)]
        IN2 = ((0, 512), (512, 256), (768, 512), (1280, 512), (1792, 512))
        in2_ch = [add(cols(ap["w_in2"], c0, n), "in2_ps", 2 * i + 2) for i, (c0, n) in enumerate(IN2)]
        wo2_ch = [add(cols(ap["w_out2"], 512 * c, 512), "wo2_ps", 2 * c + 2) for c in range(2)]
        NCH = len(chunks)
        base = [len(range(s, NCH, 4)) for s in range(4)] + [0, 0]

        def arrived(pe, n):
            pe.wait_ge(S(f"loaded{n % 4}"), 16 * (n // 4 + 1))
            return chunks[n][0][0](n % 4)

        block = stack.enter_context(nc.Block())

        @block.sync
        def _(sp):
            for n, ((view, dram), done, value) in enumerate(chunks):
                if n >= 4:
                    sp.wait_ge(S(chunks[n - 4][1]), chunks[n - 4][2])
                sp.dma_start(view(n % 4), dram).then_inc(S(f"loaded{n % 4}"), 16)

            ORDER = (("e_gate", 0), ("e_up", 0), ("e_gate", 1), ("e_up", 1), ("e_down", 0), ("e_down", 1))

            def expert(e, s):
                name, j = ORDER[s]
                nk = 4 if name == "e_down" else KD
                sp.dma_start(slot(s).rearrange("p (o k n) -> p o k n", o=1, k=nk),
                             ap[name][bass.ds(2 * e + j, 1), :, :].rearrange("o (k p) n -> p o k n", p=P)) \
                    .then_inc(S(f"loaded{s}"), 16)

            sp.wait_ge(S("pv_ps"), 16)
            expert(0, 4)
            expert(0, 5)
            for last in range(NCH - 4, NCH):
                sp.wait_ge(S(chunks[last][1]), chunks[last][2])
                expert(0, last % 4)
            sp.wait_ge(S("count_ready"), 1)
            npairs = sp.value_load(niter_t[0:1, 0:1], min_val=NPAIR, max_val=4 * NPAIR)
            with sp.Fori(1, npairs) as p:
                for s, sem in enumerate(("gate_rd", "gu_ps", "gate_rd", "gu_ps", "yt_ps", "yt_ps")):
                    sp.wait_ge(S(sem), 2 * p - 1 + ORDER[s][1])
                    expert(p % NPAIR, s)
            sp.wait_ge(S("out_ready"), 1)
            sp.dma_start(out.rearrange("(t p) n -> p t n", p=P), x).then_inc(S("out_done"), 16)
            sp.wait_ge(S("out_done"), 16)

        @block.gpsimd
        def _(g):
            def mul(o_, a, b):
                return nc.gpsimd.tensor_tensor(o_, a, b, MUL)

            g.wait_ge(S("item_silu"), 20)
            for i in range(6):
                src = kT[:, i, :] if i < 4 else qT[:, 2 * i - 8:2 * i - 6, :].rearrange("p h t -> p (h t)")
                if i >= 2:
                    g.wait_ge(S("sq_ps"), i - 1)
                mul(sqb[i % 2], src, src).then_inc(S("sq_ready"), 1)
            g.wait_ge(S("item_ps"), 24)
            nc.gpsimd.memset(St[:, :, :, :], 0.0)
            nc.gpsimd.memset(ht[:, :, :], 0.0).then_inc(S("state0"), 1)
            g.wait_ge(S("gates"), 1)

            def piece(u, d, kind):
                t = tile_of(u, d)
                if kind == "c":
                    n = 2 * (u - 2) + d + 1
                    g.wait_ge(S("ws_exp"), n)
                    mul(Ws[:, :, :], Ws[:, :, :], each(mask[d], 8)).then_inc(S("ws_mask"), 1)
                    if n > 1:
                        g.wait_ge(S("yd_ps"), n - 1)
                    mul(heads(xdt, 8, SP_), heads(xsN[:, t, :], 8, SP_),
                        wide(dtv[:, t, 12 * d + 4:12 * d + 12], SP_)).then_inc(S("xdt_ready"), 1)
                if kind == "e":
                    n = 2 * u + d + 1
                    if n > 1:
                        g.wait_ge(S("hs_ps"), n - 1)
                    mul(heads(xde, 8, SP_), heads(xsN[:, t, :], 8, SP_),
                        wide(dtkd[:, t, 12 * d + 4:12 * d + 12], SP_)).then_inc(S("xde_ready"), 1)

            for u in range(4):
                for d in range(2):
                    g.wait_ge(S(f"nt{d}"), u + 1)
                    if u:
                        g.wait_ge(S(f"vn_ps{d}"), u)
                    for l in range(2):
                        mul(Mn[d][l], NT[d], each(lvl[d][l], 4)).then_inc(S(f"mn{d}"), 1)
                    if u >= 2:
                        mul(PT[d], PT[d], each(mask[d], 4)).then_inc(S(f"pt{d}"), 1)
                for l in range(1, LEVELS):
                    if l + 1 < LEVELS:
                        for d in range(2):
                            g.wait_ge(S(f"p_ps{d}"), u * LEVELS + l)
                            if l == 1:
                                g.wait_ge(S(f"x{d}"), u * LEVELS + 1)
                            mul(Mn[d][(l + 1) % 2], NT[d], each(lvl[d][l + 1], 4)).then_inc(S(f"mn{d}"), 1)
                    for d, kind in pieces(u, l):
                        piece(u, d, kind)
                for d in range(2 if u < 3 else 0):
                    t = tile_of(u, d)
                    g.wait_ge(S(f"mn{d}"), LEVELS * (u + 1))
                    mul(NT[d], heads(kN[:, t, :], 4, P), wide(kd[:, t, 12 * d:12 * d + 4], P)) \
                        .then_inc(S(f"kd{d}"), 1)
            for t in range(T):
                g.wait_ge(S("in2_ev"), 8 + t + 1)
            link_n = 0
            for t in range(T):
                src = pj[:, t, 768:1792]
                s4, r4 = src.rearrange("p (h a e) -> p h a e", h=16, a=2), \
                    rotb[:, t, :].rearrange("p (h a e) -> p h a e", h=16, a=2)
                cos, sin = rope(1, t)
                for a in range(2):
                    mul(r4[:, :, a, :], s4[:, :, 1 - a, :], each(sin[:, 32 * a:32 * a + 32], 16)) \
                        .then_inc(S("pool_rot"), 1)
                link_n += 2
                g.wait_ge(S("pool_rot"), link_n)
                mul(heads(src, 16, HD), heads(src, 16, HD), each(cos, 16)).then_inc(S("pool_rot"), 1)
                link_n += 1
                g.wait_ge(S("pool_rot"), link_n)
                nc.gpsimd.tensor_tensor(src, src, rotb[:, t, :], ADD).then_inc(S("rot_b"), 1)

        @block.scalar
        def _(a):
            act = nc.scalar.activation
            a.dma_start(co, ap["consts"]).then_inc(S("in_first"), 16)
            a.dma_start(craw, ap["cc"]).then_inc(S("in_first"), 16)
            a.dma_start(tiles(vecs, 3), ap["vec_rows"].rearrange("(i p) n -> p i n", p=P)).then_inc(S("in_first"), 16)
            a.dma_start(x, ap["x"].rearrange("(t p) n -> p t n", p=P)).then_inc(S("in_rest"), 16)
            a.dma_start(ctx, ap["ctx"].rearrange("(t p) n -> p t n", p=P)).then_inc(S("in_rest"), 16)
            a.dma_start(rowv, ap["rowv"].to_broadcast([P, NRV])).then_inc(S("in_rest"), 16)
            a.dma_start(wsm, ap["w_small"].rearrange("(k p) n -> p k n", p=P)).then_inc(S("in_rest"), 16)
            a.wait_ge(S("in_first"), 48)
            act(csil, craw, ACT.Silu).then_inc(S("c_silu"), 1)

            def rms(k, srcs, space):
                for i, s in enumerate(srcs):
                    if k or i:
                        a.wait_ge(S("rms_sq"), (2 + 2 * k if k else 0) + i)
                    act(space, s, ACT.Square, accum_out=stat[:, i:i + 1]).then_inc(S("rms_sq"), 1)
                a.wait_ge(S("rms_mean"), k + 1)
                act(rstd[:, 0:len(srcs)], stat[:, 0:len(srcs)], ACT.Sqrt).then_inc(S("rms_root"), 1)

            a.wait_ge(S("in_rest"), 64)
            rms(0, [x[:, 0, :], x[:, 1, :], ctx[:, 0, :], ctx[:, 1, :]], junk0)
            a.wait_ge(S("mod"), 1)
            for k in range(KD):
                a.wait_ge(S("ht_ps"), k + 1)
                b = ps[2 + k % 2]
                act(hT[:, k, 0:L], b[:, 0:L], ACT.Identity, scale=scale1[:, k, 0:1], bias=mod[:, k, 0:1])
                act(hT[:, k, L:2 * L], b[:, L:2 * L], ACT.Identity, scale=scale1[:, k, 1:2],
                    bias=mod[:, k, 1:2]).then_inc(S("ht_ev"), 1)

            def silu_item(i):
                n, _, _, dest = item(i)
                a.wait_ge(S("conv_v"), i + 1)
                if 7 <= i < 12:
                    a.wait_ge(S("tr_ps"), i - 6)
                act(dest, cconv[i % 2][:, 0:n], ACT.Silu).then_inc(S("item_silu"), 1)

            for i in range(24):
                b = ps[4 + i % 2]
                if i < 20:
                    n, taps, wb, _ = item(i)
                    if i >= 2:
                        a.wait_ge(S("item_silu"), i - 1)
                    a.wait_ge(S("item_ps"), i + 1)
                    act(cconv[i % 2][:, 0:n], b[:, 0:n], ACT.Identity, scale=col[:, taps[1]:taps[1] + 1],
                        bias=0.0 if wb is None else col[:, wb:wb + 1]).then_inc(S("conv_a"), 1)
                    if i >= 1:
                        silu_item(i - 1)
                    if i == 19:
                        silu_item(19)
                else:
                    j = i - 20
                    a.wait_ge(S("item_ps"), i + 1)
                    act(Z[:, j % 2, 512 * (j // 2):512 * (j // 2) + 512], b[:, :], ACT.Silu).then_inc(S("z_ev"), 1)

            def k_rows(i):
                a.wait_ge(S("tr_ps"), 10 + i + 1)
                act(kN[:, :, i * P:(i + 1) * P], tiles(ps[6 + i % 2][:, :], 4), ACT.Copy).then_inc(S("kn_ev"), 1)

            a.wait_ge(S("item_silu"), 20)
            for i in range(6):
                a.wait_ge(S("sq_ps"), i + 1)
                if i >= 2:
                    a.wait_ge(S("kq_norm"), i - 1)
                act(cconv[i % 2], ps[2 + i % 2][:, :], ACT.Sqrt, scale=1.0 if i < 4 else float(P),
                    bias=C("eps", 4)[:, 0:1] if i < 4 else C("eps", 4)[:, 1:2]).then_inc(S("kq_root"), 1)
            for i in range(4):
                k_rows(i)
            a.wait_ge(S("exp_arg"), 1)
            act(gtmp[:, :, :], gtmp[:, :, :], ACT.Exp).then_inc(S("exp_done"), 1)
            a.wait_ge(S("exp_done"), 1)
            act(beta[:, :, :], beta[:, :, :], ACT.Exp)
            act(nega, R("alog", 24), ACT.Exp)
            act(gtmp[:, :, :], gtmp[:, :, :], ACT.Ln, bias=C("eps", 4)[:, 2:3]).then_inc(S("exp_done"), 1)
            a.wait_ge(S("exp_arg"), 2)
            act(egc[:, :, :], gc[:, :, :], ACT.Exp)
            act(etot[:, :, :], etot[:, :, :], ACT.Exp)
            act(kd[:, :, :], kd[:, :, :], ACT.Exp).then_inc(S("exp_done"), 1)
            for u in range(4):
                for d in range(2):
                    a.wait_ge(S(f"e_arg{d}"), u + 1)
                    act(E[d], E[d], ACT.Exp).then_inc(S(f"e_exp{d}"), 1)
                for l in range(1, LEVELS):
                    for d in range(2):
                        a.wait_ge(S(f"p_ps{d}"), u * LEVELS + l + 1)
                        act(Pv[d], tiles(pA[d][:, :], 4), ACT.Copy).then_inc(S(f"p_ev{d}"), 1)
                    for d, kind in pieces(u, l):
                        if kind == "c":
                            a.wait_ge(S("ws_arg"), 2 * (2 * (u - 2) + d + 1))
                            act(Ws[:, :, :], Ws[:, :, :], ACT.Exp).then_inc(S("ws_exp"), 1)
            for n in range(2):
                a.wait_ge(S("mean"), n + 1)
                act(rstd[:, 8 * n:8 * n + (8 if n == 0 else 2)], stat[:, 8 * n:8 * n + (8 if n == 0 else 2)],
                    ACT.Sqrt).then_inc(S("root"), 1)

            def columns(nth, dest, scale, bias=None):
                for k in range(KD):
                    a.wait_ge(S("cols_ps"), nth * KD + k + 1)
                    act(dest[:, k, :], ps[2 + k % 2][:, 0:L], ACT.Identity, scale=scale(k),
                        bias=0.0 if bias is None else bias(k)).then_inc(S("cols_ev"), 1)

            columns(0, mixT, lambda k: V("mixg", k))
            a.wait_ge(S("x_step"), 4)
            rms(1, [x[:, 0, :], x[:, 1, :]], junk)
            columns(1, hT2, lambda k: scale2[:, k:k + 1], lambda k: mod[:, 24 + k, 0:1])
            a.dma_start(fng1, ap["fng"].to_broadcast([P, D])).then_inc(S("in_rows"), 16)
            a.dma_start(fng2, ap["fng2"].to_broadcast([P, D])).then_inc(S("in_rows"), 16)
            a.dma_start(n2row, ap["n2row"].to_broadcast([P, D])).then_inc(S("in_rows"), 16)
            a.dma_start(bias, ap["bias"].rearrange("(t p) n -> p t n", p=P)).then_inc(S("in_rows"), 16)

            def ffn_silu(b):
                a.wait_ge(S("f_taps"), b + 1)
                if b >= 2:
                    a.wait_ge(S("f_hid"), b - 1)
                act(fs[b % 2], fa[b % 2], ACT.Silu).then_inc(S("f_silu"), 1)

            for b in range(KF):
                if b >= 2:
                    a.wait_ge(S("f_silu"), b - 1)
                a.wait_ge(S("gate_ps"), b + 1)
                act(fa[b % 2], ps[b % 2][:, 0:L], ACT.Identity, scale=V("fconv", 4 * KF + b),
                    bias=V("fconvb", b)).then_inc(S("f_mid"), 1)
                if b >= 1:
                    ffn_silu(b - 1)
            ffn_silu(KF - 1)
            a.wait_ge(S("x_step"), 8)
            rms(2, [x[:, 0, :], x[:, 1, :]], junk)
            a.wait_ge(S("x_step"), 9)
            rms(3, [x[:, 0, :], x[:, 1, :]], junk)
            columns(2, uT, lambda k: V("n1b", k))
            for i, (c0, n) in enumerate(IN2):
                for t in range(T):
                    j = 2 * i + t
                    a.wait_ge(S("in2_ps"), j + 1)
                    act(pj[:, t, c0:c0 + n], ps[4 + j % 4][:, 0:n], ACT.Copy).then_inc(S("in2_ev"), 1)
            a.wait_ge(S("mean"), 3)
            act(rstd[:, 0:20], stat[:, 0:20], ACT.Sqrt).then_inc(S("root"), 1)
            for i in range(13):
                a.wait_ge(S("qt_ps"), i + 1)
                act(qkT[0:HD, 2 * i:2 * i + 2, :], ps[i % 2][0:HD, :].rearrange("p (h t) -> p h t", h=2),
                    ACT.Copy).then_inc(S("qt_ev"), 1)

            def prob_rows(h):
                a.wait_ge(S("pt_ps"), h + 1)
                if h >= 2:
                    a.wait_ge(S("pv_ps"), h - 1)
                act(prT[h % 2], ps[2 + h % 2][:, :].rearrange("p (k t q) -> p k t q", k=2, t=2),
                    ACT.Copy).then_inc(S("pt_ev"), 1)

            for h in range(16):
                a.wait_ge(S("s_max"), h + 1)
                if h >= 2:
                    a.wait_ge(S("pt_ps"), h - 1)
                for t in range(T):
                    src = ps[h % 2][:, t * L:(t + 1) * L] if h < 8 else sc[h % 2][:, t, :]
                    act(pr[h % 2][:, t, :], src, ACT.Exp, scale=SCALE if h < 8 else 1.0,
                        bias=mx[:, h, t:t + 1], accum_out=sm[:, h, t:t + 1]).then_inc(S("s_exp"), 1)
                if h >= 1:
                    prob_rows(h - 1)
            prob_rows(15)
            a.wait_ge(S("mean"), 4)
            act(rstd[:, 0:4], stat[:, 0:4], ACT.Sqrt).then_inc(S("root"), 1)
            columns(3, uT, lambda k: V("outab", k))
            a.dma_start(rw, ap["rw"].rearrange("(k p) n -> p k n", p=P)).then_inc(S("in_rw"), 16)
            a.wait_ge(S("x_step"), 13)
            rms(4, [x[:, 0, :], x[:, 1, :]], junk)
            columns(4, u2T, lambda k: V("n2b", k))
            a.wait_ge(S("exp_arg"), 3)
            act(ra[0][:, :, 0:4], ra[0][:, :, 0:4], ACT.Exp)
            act(rs[:, 5, :], rs[:, 5, :], ACT.Exp).then_inc(S("exp_done"), 1)
            a.wait_ge(S("count_ready"), 1)
            npairs = a.value_load(niter_t[0:1, 0:1], min_val=NPAIR, max_val=4 * NPAIR)
            a.wait_ge(S("gather_ps"), 1)
            act(xsel[:, 0:4, :], tiles(ps[4][:, :], 4), ACT.Copy).then_inc(S("xsel_a"), 1)
            with a.Fori(0, npairs) as p:
                for j in range(2):
                    a.wait_ge(S("gu_ps"), 2 * p + j + 1)
                    a.wait_ge(S("hid"), 2 * p + j + 2)
                    act(sg, tiles(ps[6][:, 0:256], 4), ACT.Silu).then_inc(S("sg"), 1)
                    if j == 0:
                        a.wait_ge(S("yn_ps"), p + 1)
                        a.wait_ge(S("sc_ps"), p + 1)
                        act(yN[:, 0:512], ps[4][:, :], ACT.Copy).then_inc(S("yn_a"), 1)
                a.wait_ge(S("gather_ps"), p + 2)
                act(xsel[:, 0:4, :], tiles(ps[4][:, :], 4), ACT.Copy).then_inc(S("xsel_a"), 1)
            a.wait_ge(S("yn_ps"), npairs + 1)
            a.wait_ge(S("sc_ps"), npairs + 1)
            act(yN[:, 0:512], ps[4][:, :], ACT.Copy).then_inc(S("yn_a"), 1)
            a.wait_ge(S("x_step"), 17)
            rms(5, [x[:, 0, :], x[:, 1, :]], junk)

        @block.vector
        def _(v):
            tt, ts, stt = nc.vector.tensor_tensor, nc.vector.tensor_scalar, nc.vector.scalar_tensor_tensor
            n = [0]

            def link(ins):
                n[0] += 1
                ins.then_inc(S("dve"), 1)
                v.wait_ge(S("dve"), n[0])

            def rms(k, width=2):
                v.wait_ge(S("rms_sq"), 4 + 2 * k)
                ts(stat[:, 0:width], stat[:, 0:width], 1.0 / D, EPS, MUL, ADD).then_inc(S("rms_mean"), 1)
                v.wait_ge(S("rms_root"), k + 1)
                link(nc.vector.reciprocal(rstd[:, 0:width], rstd[:, 0:width]))

            v.wait_ge(S("one_ps"), 1)
            link(nc.vector.tensor_copy(col, ps[0][:, 0:NROWS]))
            rms(0, 4)
            for t in range(4):
                ts(xn[:, t, :], x[:, t, :] if t < 2 else ctx[:, t - 2, :], rstd[:, t:t + 1], None,
                   MUL).then_inc(S("xh"), 1)
            v.wait_ge(S("ada_ps"), 4)
            link(tt(mod[:, 0:16, :], ps[1][:, 0:32].rearrange("p (j c) -> p j c", c=2),
                    wide(V("b_ada", 0, 16), 2), ADD))
            link(ts(scale1[:, :, :], mod[:, 8:16, :], 1.0, None, ADD))
            tt(scale1[:, :, :], scale1[:, :, :], wide(V("norm1", 0, 8), 2), MUL).then_inc(S("mod"), 1)

            def rows_out(r):
                v.wait_ge(S("tr_ps"), r + 1)
                dest = vN[:, :, r * P:(r + 1) * P] if r < 4 else xsN[:, :, (r - 4) * P:(r - 3) * P] if r < 8 \
                    else BN[:, :, (r - 8) * P:(r - 7) * P]
                nc.vector.tensor_copy(dest, tiles(ps[6 + r % 2][:, :], 4)).then_inc(S("tr_ev"), 1)

            for i in range(20):
                w, taps, _, _ = item(i)
                segs = w // L
                v.wait_ge(S("conv_a"), i + 1)
                b = ps[4 + i % 2][:, 0:w].rearrange("p (s t) -> p s t", s=segs)
                o_ = cconv[i % 2][:, 0:w].rearrange("p (s t) -> p s t", s=segs)
                link(stt(o_[:, :, 1:L], b[:, :, 0:L - 1], col[:, taps[0]:taps[0] + 1], o_[:, :, 1:L], MUL, ADD))
                stt(o_[:, :, 0:L - 1], b[:, :, 1:L], col[:, taps[2]:taps[2] + 1], o_[:, :, 0:L - 1], MUL,
                    ADD).then_inc(S("conv_v"), 1)
                if 7 <= i < 17:
                    rows_out(i - 7)
            v.wait_ge(S("one_ps"), 2)
            v.wait_ge(S("in_rest"), 64)
            sp4 = ps[3][:, 0:128].rearrange("p (t n) -> p t n", t=4)
            nc.vector.tensor_copy(gx, sp4).then_inc(S("small_rd"), 1)
            v.wait_ge(S("small_rd"), 1)
            link(tt(gx[:, :, 0:24], gx[:, :, 0:24], each(R("dtb", 24), 4), ADD))
            link(ts(gtmp[:, :, :], gx[:, :, 0:24], -1.0, None, MUL))
            link(tt(gtmp[:, :, :], gtmp[:, :, :], gx[:, :, 0:24], ALU.min))
            ts(beta[:, :, :], gx[:, :, 24:32], -1.0, None, MUL).then_inc(S("exp_arg"), 1)
            for i in range(6):
                v.wait_ge(S("kq_root"), i + 1)
                dest = kT[:, i, :] if i < 4 else qT[:, 2 * i - 8:2 * i - 6, :].rearrange("p h t -> p (h t)")
                link(nc.vector.reciprocal(cconv[i % 2], cconv[i % 2]))
                tt(dest, dest, cconv[i % 2], MUL).then_inc(S("kq_norm"), 1)
            v.wait_ge(S("exp_done"), 2)
            link(ts(gx[:, :, 0:24], gx[:, :, 0:24], 0.0, None, ALU.max))
            link(tt(dtv[:, :, :], gx[:, :, 0:24], gtmp[:, :, :], ADD))
            link(ts(nega, nega, -1.0, None, MUL))
            tt(G[:, :, :], dtv[:, :, :], each(nega, 4), MUL).then_inc(S("g_ready"), 1)
            link(ts(beta[:, :, :], beta[:, :, :], 1.0, None, ADD))
            link(nc.vector.reciprocal(beta[:, :, :], beta[:, :, :]))
            link(ts(nbeta[:, :, :], beta[:, :, :], -1.0, None, MUL))
            v.wait_ge(S("one_ps"), 3)
            link(nc.vector.tensor_copy(gc[:, :, :], tiles(ps[2][:, 0:96], 4)))
            link(nc.vector.tensor_copy(etot[:, :, :], tiles(ps[2][:, 128:224], 4)))
            tt(kd[:, :, :], etot[:, :, :], gc[:, :, :], SUB).then_inc(S("exp_arg"), 1)
            v.wait_ge(S("exp_done"), 3)
            link(tt(dtkd[:, :, :], dtv[:, :, :], kd[:, :, :], MUL))
            v.wait_ge(S("one_ps"), 4)
            nc.vector.tensor_copy(CBs, pD[0][:, :].rearrange("p (t g i) -> p t g i", t=T, g=2)) \
                .then_inc(S("gates"), 1)
            v.wait_ge(S("ada_ps"), 12)
            link(tt(mod[:, 16:48, :], ps[1][:, 32:96].rearrange("p (j c) -> p j c", c=2),
                    wide(V("b_ada", 16, 32), 2), ADD))
            link(ts(scale2, mod[:, 32:40, 0], 1.0, None, ADD))
            tt(scale2, scale2, V("norm2", 0, 8), MUL).then_inc(S("mod"), 1)
            v.wait_ge(S("gates"), 1)
            v.wait_ge(S("state0"), 1)

            def piece(u, d, kind):
                t, c = tile_of(u, d), 12 * d + 4
                if kind in "ab":
                    k = 0 if kind == "a" else 4
                    m = 2 * (2 * (u - 2) + d) + (1 if kind == "b" else 0)
                    v.wait_ge(S("wg_ps"), m + 1)
                    for h in range(4):
                        ins = ts(Ws[:, k + h, :], pD[d][:, h * P:(h + 1) * P], gc[:, t, c + k + h:c + k + h + 1], 0.0,
                                 SUB, ALU.min)
                    ins.then_inc(S("ws_arg"), 1)
                elif kind == "e":
                    m = 2 * u + d
                    if u >= 2:
                        v.wait_ge(S("yo_ps"), 2 * (u - 2) + d + 1)
                        tt(heads(yoff, 8, SP_), heads(pD[d][:, :], 8, SP_), wide(egc[:, t, c:c + 8], SP_), MUL) \
                            .then_inc(S("yo_rd"), 1)
                        v.wait_ge(S("yo_rd"), 2 * (u - 2) + d + 1)
                        if first(u, d):
                            link(tt(heads(yacc[:, t, :], 8, SP_), heads(xsN[:, t, :], 8, SP_),
                                    wide(R("ssmD", 8), SP_), MUL))
                        link(tt(yacc[:, t, :], yacc[:, t, :], yoff, ADD))
                    link(tt(heads(ht[:, d, :], 8, SP_), heads(ht[:, d, :], 8, SP_), wide(etot[:, t, c:c + 8], SP_),
                            MUL))
                    v.wait_ge(S("hs_ps"), m + 1)
                    tt(ht[:, d, :], ht[:, d, :], pD[d][:, :], ADD).then_inc(S("h_ready"), 1)
                else:
                    m = 2 * (u - 2) + d
                    v.wait_ge(S("ws_mask"), m + 1)
                    for k in range(2):
                        ins = tt(Ws[:, 4 * k:4 * k + 4, :], Ws[:, 4 * k:4 * k + 4, :], each(CBs[:, t, k, :], 4), MUL)
                    ins.then_inc(S("ws_ready"), 1)
                    v.wait_ge(S("yd_ps"), m + 1)
                    tt(yacc[:, t, :], yacc[:, t, :], pD[d][:, :], ADD).then_inc(S("yd_rd"), 1)
                    v.wait_ge(S("yd_rd"), m + 1)

            def first(u, d):
                return u == 2

            for u in range(4):
                for d in range(2):
                    t = tile_of(u, d)
                    v.wait_ge(S(f"pre{d}"), u + 1)
                    for h in range(4):
                        ins = ts(E[d][:, h, :], pB[d][:, h * P:(h + 1) * P], gc[:, t, 12 * d + h:12 * d + h + 1], 0.0,
                                 SUB, ALU.min)
                    ins.then_inc(S(f"e_arg{d}"), 1)
                for d in range(2):
                    t = tile_of(u, d)
                    v.wait_ge(S(f"e_exp{d}"), u + 1)
                    if u:
                        v.wait_ge(S(f"s_ps{d}"), u)
                    if u >= 2:
                        if u == 3:
                            v.wait_ge(S(f"o_ps{d}"), 1)
                        tt(PT[d], tiles(pC[d][:, :], 4), E[d], MUL)
                    for h in range(4):
                        ins = stt(NT[d][:, h, :], pA[d][:, h * P:(h + 1) * P], nbeta[:, t, 4 * d + h:4 * d + h + 1],
                                  E[d][:, h, :], MUL, MUL)
                    ins.then_inc(S(f"nt{d}"), 1)
                for d in range(2):
                    v.wait_ge(S(f"mn{d}"), u * LEVELS + 1)
                    v.wait_ge(S(f"p_ps{d}"), u * LEVELS + 1)
                    tt(X[d], tiles(pA[d][:, :], 4), each(ident, 4), ADD)
                    tt(XT[d], Mn[d][0], each(ident, 4), ADD).then_inc(S(f"x{d}"), 1)
                for l in range(1, LEVELS):
                    for d, kind in pieces(u, l):
                        piece(u, d, kind)
                    for d in range(2):
                        v.wait_ge(S(f"x{d}"), u * LEVELS + l)
                        v.wait_ge(S(f"q_ps{d}"), u * (LEVELS - 1) + l)
                        if l < LEVELS - 1:
                            tt(X[d], X[d], tiles(pB[d][:, :], 4), ADD)
                        tt(XT[d], XT[d], tiles(pC[d][:, :], 4), ADD).then_inc(S(f"x{d}"), 1)
                for d in range(2):
                    t = tile_of(u, d)
                    v.wait_ge(S(f"ks_ps{d}"), u + 1)
                    link(tt(E[d], tiles(pA[d][:, :], 4), wide(egc[:, t, 12 * d:12 * d + 4], P), MUL))
                    v.wait_ge(S(f"mn{d}"), u * LEVELS + LEVELS)
                    tt(Mn[d][1], heads(vN[:, t, :], 4, P), E[d], SUB).then_inc(S(f"r{d}"), 1)
                for d in range(2):
                    t = tile_of(u, d)
                    v.wait_ge(S(f"vn_ps{d}"), u + 1)
                    tt(vnew[d], tiles(pB[d][:, :], 4), wide(beta[:, t, 4 * d:4 * d + 4], P), MUL) \
                        .then_inc(S(f"vnew{d}"), 1)
                for d in range(2):
                    t = tile_of(u, d)
                    v.wait_ge(S(f"ks_ps{d}"), u + 1)
                    if u >= 2:
                        v.wait_ge(S(f"o_ps{d}"), u - 1)
                        link(tt(E[d], tiles(pC[d][:, :], 4), wide(egc[:, t, 12 * d:12 * d + 4], P), MUL))
                        o4 = heads(oacc[:, t, :], 4, P)
                        if first(u, d):
                            link(tt(o4, E[d], tiles(pA[d][:, :], 4), ADD))
                        else:
                            link(tt(E[d], E[d], tiles(pA[d][:, :], 4), ADD))
                            link(tt(o4, o4, E[d], ADD))
                    if u < 3:
                        link(tt(St[:, d, :, :], St[:, d, :, :], wide(etot[:, t, 12 * d:12 * d + 4], P), MUL))
                        v.wait_ge(S(f"s_ps{d}"), u + 1)
                        tt(St[:, d, :, :], St[:, d, :, :], tiles(pB[d][:, :], 4), ADD).then_inc(S(f"s{d}"), 1)
            sq = tiles(scratch(0, 1024), 2)
            v.wait_ge(S("o_ps0"), 2)
            v.wait_ge(S("o_ps1"), 2)
            for t in range(T):
                link(tt(sq[:, t, :], oacc[:, t, :], oacc[:, t, :], MUL))
            link(nc.vector.tensor_reduce(stat[:, 0:8], sq.rearrange("p t (h e) -> p (t h) e", h=4), AX, ADD))
            ts(stat[:, 0:8], stat[:, 0:8], 1.0 / P, EPS, MUL, ADD).then_inc(S("mean"), 1)
            for t in range(T):
                link(tt(yacc[:, t, :], yacc[:, t, :], Z[:, t, 512:1024], MUL))
                link(tt(sq[:, t, :], yacc[:, t, :], yacc[:, t, :], MUL))
            link(nc.vector.tensor_reduce(stat[:, 8:10], sq, AX, ADD))
            ts(stat[:, 8:10], stat[:, 8:10], 1.0 / 512, EPS, MUL, ADD).then_inc(S("mean"), 1)
            v.wait_ge(S("root"), 2)
            link(nc.vector.reciprocal(rstd[:, 0:10], rstd[:, 0:10]))
            for t in range(T):
                link(tt(heads(oacc[:, t, :], 4, P), heads(oacc[:, t, :], 4, P), wide(rstd[:, 4 * t:4 * t + 4], P), MUL))
                tt(oacc[:, t, :], oacc[:, t, :], Z[:, t, 0:512], MUL).then_inc(S("normed"), 1)
                ts(yacc[:, t, :], yacc[:, t, :], rstd[:, 8 + t:9 + t], None, MUL).then_inc(S("normed"), 1)
            for i in range(16):
                if i >= 2:
                    v.wait_ge(S("dg_ps"), i - 1)
                ts(dg[i % 2], ident, mod[:, (16 if i < 8 else 32) + i, 0:1], None, MUL).then_inc(S("dg"), 1)
            for i in range(4):
                v.wait_ge(S("dg_ps"), 4 * i + 4)
                nc.vector.tensor_copy((g1r if i < 2 else g2r)[:, 512 * (i % 2):512 * (i % 2) + 512],
                                      ps[4 + i][:, :]).then_inc(S("gain_rows"), 1)
            v.wait_ge(S("gain_rows"), 4)

            def residual(name, order, gain, done):
                for i, (bank, t, c) in enumerate(order):
                    v.wait_ge(S(name), (i + 1) if done else 6)
                    xs = x[:, t, 512 * c:512 * c + 512]
                    if gain is None:
                        tt(xs, xs, ps[bank][:, :], ADD).then_inc(S("x_step"), 1)
                    else:
                        link(tt(tmpx[i % 2], ps[bank][:, :], gain[:, 512 * c:512 * c + 512], MUL))
                        tt(xs, xs, tmpx[i % 2], ADD).then_inc(S("x_step"), 1)

            residual("wo_ps", [(4 + 2 * c + t, t, c) for c in range(2) for t in range(2)], g1r, True)
            rms(1)
            for t in range(T):
                ts(xh[:, t, :], x[:, t, :], rstd[:, t:t + 1], None, MUL).then_inc(S("xh"), 1)

            def ffn_hid(b):
                v.wait_ge(S("f_silu"), b + 1)
                v.wait_ge(S("up_ps"), b + 1)
                tt(hid[:, b, :], fs[b % 2], ps[2 + b % 2][:, 0:L], MUL).then_inc(S("f_hid"), 1)

            for b in range(KF):
                v.wait_ge(S("f_mid"), b + 1)
                src = ps[b % 2][:, 0:L].rearrange("p (r c) -> p r c", c=GRID)
                dst = fa[b % 2].rearrange("p (r c) -> p r c", c=GRID)
                nr = L // GRID
                for j in range(9):
                    if j == 4:
                        continue
                    dy, dx = j // 3 - 1, j % 3 - 1
                    r0, r1, c0, c1 = max(0, -dy), nr - max(0, dy), max(0, -dx), GRID - max(0, dx)
                    o_ = dst[:, r0:r1, c0:c1]
                    ins = stt(o_, src[:, r0 + dy:r1 + dy, c0 + dx:c1 + dx], V("fconv", j * KF + b), o_, MUL, ADD)
                    if j < 8:
                        link(ins)
                    else:
                        ins.then_inc(S("f_taps"), 1)
                if b >= 1:
                    ffn_hid(b - 1)
            ffn_hid(KF - 1)
            residual("down_ps", [(4 + 2 * t + c, t, c) for t in range(2) for c in range(2)], g2r, False)
            rms(2)
            v.wait_ge(S("x_step"), 8)
            v.wait_ge(S("in_rows"), 64)
            for t in range(T):
                link(ts(x[:, t, :], x[:, t, :], rstd[:, t:t + 1], None, MUL))
            link(tt(x[:, 0, :], x[:, 0, :], fng1, MUL))
            tt(x[:, 1, :], x[:, 1, :], fng1, MUL).then_inc(S("x_step"), 1)
            rms(3)
            v.wait_ge(S("x_step"), 9)
            for t in range(T):
                ts(xh[:, t, :], x[:, t, :], rstd[:, t:t + 1], None, MUL).then_inc(S("xh"), 1)
            v.wait_ge(S("in2_ev"), 4)
            for t in range(T):
                link(tt(rota[:, t, :], pj[:, t, 0:640], pj[:, t, 0:640], MUL))
                link(nc.vector.tensor_reduce(stat[:, 10 * t:10 * t + 10], heads(rota[:, t, :], 10, HD), AX, ADD))
            ts(stat[:, 0:20], stat[:, 0:20], 1.0 / HD, EPS, MUL, ADD).then_inc(S("mean"), 1)
            v.wait_ge(S("root"), 3)
            link(nc.vector.reciprocal(rstd[:, 0:20], rstd[:, 0:20]))
            for t in range(T):
                qa, ka = heads(pj[:, t, 0:512], 8, HD), heads(pj[:, t, 512:640], 2, HD)
                all_ = pj[:, t, 0:640]
                link(tt(heads(all_, 10, HD), heads(all_, 10, HD), wide(rstd[:, 10 * t:10 * t + 10], HD), MUL))
                link(tt(qa, qa, each(R("qn", HD), 8), MUL))
                link(tt(ka, ka, each(R("kn", HD), 2), MUL))
                s4 = all_.rearrange("p (h a e) -> p h a e", h=10, a=2)
                r4 = rota[:, t, :].rearrange("p (h a e) -> p h a e", h=10, a=2)
                cos, sin = rope(0, t)
                for a in range(2):
                    link(tt(r4[:, :, a, :], s4[:, :, 1 - a, :], each(sin[:, 32 * a:32 * a + 32], 10), MUL))
                link(tt(heads(all_, 10, HD), heads(all_, 10, HD), each(cos, 10), MUL))
                tt(all_, all_, rota[:, t, :], ADD).then_inc(S("rot_a"), 1)
            v.wait_ge(S("in_rows"), 64)
            for h in range(16):
                v.wait_ge(S("s_ps"), h + 1)
                if h < 8:
                    link(nc.vector.tensor_reduce(mx[:, h, :], tiles(ps[h % 2][:, :], 2), AX, ALU.max, negate=True))
                    ts(mx[:, h, :], mx[:, h, :], SCALE, None, MUL).then_inc(S("s_max"), 1)
                else:
                    v.wait_ge(S("s_exp"), 2 * h - 2)
                    link(stt(sc[h % 2], tiles(ps[h % 2][:, :], 2), SCALE, bias, MUL, ADD))
                    nc.vector.tensor_reduce(mx[:, h, :], sc[h % 2], AX, ALU.max, negate=True) \
                        .then_inc(S("s_max"), 1)
            v.wait_ge(S("pv_ps"), 16)
            v.wait_ge(S("s_exp"), 32)
            link(nc.vector.reciprocal(sm[:, :, :], sm[:, :, :]))
            for t in range(T):
                for m in range(2):
                    o_ = on[:, t, 512 * m:512 * m + 512]
                    link(tt(heads(o_, 8, HD), heads(ps[4 + 2 * m + t][:, :], 8, HD),
                            wide(sm[:, 8 * m:8 * m + 8, t], HD), MUL))
                    link(tt(tmpx[0], o_, o_, MUL))
                    link(nc.vector.tensor_reduce(stat[:, 2 * m + t:2 * m + t + 1], tmpx[0], AX, ADD))
            ts(stat[:, 0:4], stat[:, 0:4], 1.0 / 512, EPS, MUL, ADD).then_inc(S("mean"), 1)
            v.wait_ge(S("root"), 4)
            link(nc.vector.reciprocal(rstd[:, 0:4], rstd[:, 0:4]))
            for t in range(T):
                for m in range(2):
                    o_ = on[:, t, 512 * m:512 * m + 512]
                    ts(o_, o_, rstd[:, 2 * m + t:2 * m + t + 1], None, MUL).then_inc(S("normed"), 1)
            residual("wo2_ps", [(4 + 2 * c + t, t, c) for c in range(2) for t in range(2)], None, True)
            rms(4)
            v.wait_ge(S("x_step"), 13)
            for t in range(T):
                ts(xh[:, t, :], x[:, t, :], rstd[:, t:t + 1], None, MUL).then_inc(S("xh"), 1)
            v.wait_ge(S("xh"), 10)
            v.wait_ge(S("in_rows"), 64)
            for t in range(T):
                tt(u2[:, t, :], xh[:, t, :], n2row, MUL).then_inc(S("u2"), 1)
            desc = C("desc", NE)

            def one_hot(dst, src, top, w):
                e1 = ra[4][:, :, 0:w]
                link(nc.vector.tensor_reduce(top, src, AX, ALU.max))
                link(tt(e1, src, wide(top, w), ALU.is_equal))
                link(tt(e1, e1, each2(desc[:, 0:w]), MUL))
                link(nc.vector.tensor_reduce(rs[:, 7, :], e1, AX, ALU.max))
                link(tt(dst, e1, wide(rs[:, 7, :], w), ALU.is_equal))

            def each2(row):
                return row.unsqueeze(1).to_broadcast([P, 2, row.shape[1]])

            v.wait_ge(S("one_ps"), 5)
            link(tt(lg[:, :, :], tiles(ps[0][:, 0:72], 2), each2(R("rb", 36)), ADD))
            gm, el, oh1, oh2 = ra[1][:, :, 0:4], ra[2], ra[3], ra[5]
            one_hot(gm, lg[:, :, 0:4], rs[:, 0, :], 4)
            link(tt(ra[0][:, :, 0:4], lg[:, :, 0:4], wide(rs[:, 0, :], 4), SUB))
            for t in range(T):
                link(tt(heads(el[:, t, :], 4, 8), heads(lg[:, t, 4:36], 4, 8), wide(gm[:, t, :], 8), MUL))
            link(ts(gm, gm, -1.0, 1e30, ADD, MUL))
            for t in range(T):
                link(tt(heads(el[:, t, :], 4, 8), heads(el[:, t, :], 4, 8), wide(gm[:, t, :], 8), ADD))
            one_hot(oh1, el, rs[:, 1, :], NE)
            link(stt(el.rearrange("p t n -> p (t n)"), oh1.rearrange("p t n -> p (t n)"), -3e38,
                     el.rearrange("p t n -> p (t n)"), MUL, ADD))
            one_hot(oh2, el, rs[:, 2, :], NE)
            tt(rs[:, 5, :], rs[:, 2, :], rs[:, 1, :], SUB).then_inc(S("exp_arg"), 1)
            v.wait_ge(S("exp_done"), 4)
            link(nc.vector.tensor_reduce(rs[:, 3, :], ra[0][:, :, 0:4], AX, ADD))
            link(ts(rs[:, 4, :], rs[:, 5, :], 1.0, None, ADD))
            link(tt(rs[:, 3, :], rs[:, 3, :], rs[:, 4, :], MUL))
            link(nc.vector.reciprocal(rs[:, 3, :], rs[:, 3, :]))
            link(tt(rs[:, 4, :], rs[:, 3, :], rs[:, 5, :], MUL))
            flag = ra[4]
            tt(flag, oh1, oh2, ADD).then_inc(S("flag"), 1)
            link(nc.vector.memset(SL[:, :, :], -1.0))
            link(nc.vector.memset(GT[:, :, :], 0.0))
            link(tt(oh1, oh1, wide(rs[:, 3, :], NE), MUL))
            link(tt(oh2, oh2, wide(rs[:, 4, :], NE), MUL))
            v.wait_ge(S("flag"), 1)
            v.wait_ge(S("one_ps"), 6)
            link(ts(el, tiles(ps[1][:, 0:64], 2), 1.0, None, ADD))
            link(tt(el, el, flag, MUL))
            for r in range(4):
                link(ts(SL[:, :, 2 + NE * r:2 + NE * r + NE], el, -1.0 - SLOT * r, None, ADD))
                link(tt(GT[:, :, 2 + NE * r:2 + NE * r + NE], oh1, oh2, ADD))
            link(nc.vector.tensor_copy(cnt[:, 0:32], ps[1][:, 64:96]))
            link(nc.vector.tensor_reduce(cnt[:, 32:33], cnt[:, 0:32], AX, ALU.max))
            for r in range(3):
                link(ts(cnt[:, 33 + r:34 + r], cnt[:, 32:33], float(SLOT * (r + 1)), float(NPAIR), ALU.is_gt, MUL))
            link(nc.vector.tensor_reduce(cnt[:, 36:37], cnt[:, 33:36], AX, ADD))
            for e in range(2):
                nc.vector.memset(ysb[:, :, e * SLOT:(e + 1) * SLOT], 0.0).then_inc(S("ysb"), 1)
                nc.vector.memset(hide[e], 0.0).then_inc(S("hid"), 1)
            ts(niter_t[:, 0:1], cnt[:, 36:37], float(NPAIR), None, ADD).then_inc(S("count_ready"), 1)
            iota = C("iota", SLOT)

            def selection(chain, at, with_gate, name):
                chain(nc.vector.tensor_copy(cur[:, 0, :, :], SL[:, :, bass.ds(at, 2)]))
                if with_gate:
                    chain(nc.vector.tensor_copy(cur[:, 1, :, :], GT[:, :, bass.ds(at, 2)]))
                for t in range(T):
                    for e in range(2):
                        if with_gate:
                            ins = ts(gsel[:, t, e * SLOT:(e + 1) * SLOT], iota, cur[:, 0, t, e:e + 1],
                                     cur[:, 1, t, e:e + 1], ALU.is_equal, MUL)
                        else:
                            ins = ts(sel[:, t, e * SLOT:(e + 1) * SLOT], iota, cur[:, 0, t, e:e + 1], None,
                                     ALU.is_equal)
                ins.then_inc(S(name), 1)

            v.wait_ge(S("count_ready"), 1)
            npairs = v.value_load(niter_t[0:1, 0:1], min_val=NPAIR, max_val=4 * NPAIR)
            selection(link, 2, False, "sel")
            v.wait_ge(S("gather_ps"), 1)
            nc.vector.tensor_copy(xsel[:, 4:8, :], tiles(ps[5][:, :], 4)).then_inc(S("xsel_v"), 1)
            LINKS = 3

            def before(p, chain):
                selection(chain, 2 * p, True, "gsel")

            def rows_before(p):
                v.wait_ge(S("yn_ps"), p + 1)
                nc.vector.tensor_copy(yN[:, 512:1024], ps[5][:, :]).then_inc(S("yn_v"), 1)
                v.wait_ge(S("gt_ps"), p + 1)
                nc.vector.tensor_copy(gselT, ps[7][:, 0:256]).then_inc(S("gt_ev"), 1)

            with v.Fori(0, npairs) as p:
                m = [0]

                def chain(ins):
                    m[0] += 1
                    ins.then_inc(S("dve_loop"), 1)
                    v.wait_ge(S("dve_loop"), p * LINKS + m[0])

                v.wait_ge(S("sel"), p + 1)
                before(p, chain)
                v.wait_ge(S("sc_ps"), p + 1)
                v.wait_ge(S("sg"), 2 * p + 1)
                tt(hide[0], sg, tiles(ps[6][:, 256:512], 4), MUL).then_inc(S("hid"), 1)
                rows_before(p)
                v.wait_ge(S("gather_ps"), p + 1)
                v.wait_ge(S("gsel"), p + 1)
                selection(chain, 2 * p + 4, False, "sel")
                v.wait_ge(S("yt_ps"), 2 * p + 1)
                v.wait_ge(S("sg"), 2 * p + 2)
                tt(hide[1], sg, tiles(ps[6][:, 256:512], 4), MUL).then_inc(S("hid"), 1)
                nc.vector.tensor_copy(ysb[:, :, 0:SLOT], tiles(ps[7][:, :], KD)).then_inc(S("ysb"), 1)
                v.wait_ge(S("gather_ps"), p + 2)
                nc.vector.tensor_copy(xsel[:, 4:8, :], tiles(ps[5][:, :], 4)).then_inc(S("xsel_v"), 1)
                v.wait_ge(S("yt_ps"), 2 * p + 2)
                nc.vector.tensor_copy(ysb[:, :, SLOT:P], tiles(ps[7][:, :], KD)).then_inc(S("ysb"), 1)
                assert m[0] == LINKS
            v.wait_ge(S("sel"), npairs + 1)
            before(npairs, link)
            v.wait_ge(S("sc_ps"), npairs + 1)
            rows_before(npairs)
            v.wait_ge(S("sc_ps"), npairs + 2)
            for t in range(T):
                for c in range(2):
                    xs = x[:, t, 512 * c:512 * c + 512]
                    tt(xs, xs, ps[2 * t + c][:, :], ADD).then_inc(S("x_step"), 1)
            rms(5)
            v.wait_ge(S("x_step"), 17)
            for t in range(T):
                link(ts(x[:, t, :], x[:, t, :], rstd[:, t:t + 1], None, MUL))
            link(tt(x[:, 0, :], x[:, 0, :], fng2, MUL))
            tt(x[:, 1, :], x[:, 1, :], fng2, MUL).then_inc(S("out_ready"), 1)

        @block.tensor
        def _(pe):
            mm, tr = nc.tensor.matmul, nc.tensor.transpose
            pe.wait_ge(S("in_first"), 48)
            for i in range(3):
                ins = tr(ps[0][:, i * P:(i + 1) * P], vecs[:, i * P:(i + 1) * P], ident)
            ins.then_inc(S("one_ps"), 1)

            def ada(i):
                w = arrived(pe, ada_ch[i])
                for j in range(4):
                    for k in range(KD):
                        ins = mm(ps[1][:, 2 * (4 * i + j):2 * (4 * i + j) + 2], w[:, k, j * P:(j + 1) * P],
                                 csil[:, k, :], start=(k == 0), stop=(k == KD - 1))
                ins.then_inc(S("ada_ps"), 1)

            pe.wait_ge(S("c_silu"), 1)
            for i in range(4):
                ada(i)
            pe.wait_ge(S("xh"), 4)
            for k in range(KD):
                if k >= 2:
                    pe.wait_ge(S("ht_ev"), k - 1)
                for t in range(4):
                    ins = tr(ps[2 + k % 2][:, t * P:(t + 1) * P], xn[:, t, k * P:(k + 1) * P], ident)
                ins.then_inc(S("ht_ps"), 1)
            pe.wait_ge(S("ht_ev"), KD)
            pe.wait_ge(S("mod"), 1)
            pe.wait_ge(S("in_rest"), 64)
            for t in range(4):
                for k in range(KD):
                    ins = mm(ps[3][:, t * 32:(t + 1) * 32], hT[:, k, t * P:(t + 1) * P], wsm[:, k, :],
                             start=(k == 0), stop=(k == KD - 1))
            ins.then_inc(S("one_ps"), 1)

            def rows_in(i):
                r = i - 4
                pe.wait_ge(S("item_silu"), i + 1)
                if r >= 2:
                    pe.wait_ge(S("tr_ev"), r - 1)
                src = item(i)[3]
                for t in range(4):
                    ins = tr(ps[6 + r % 2][:, t * P:(t + 1) * P], src[:, t * P:(t + 1) * P], ident)
                ins.then_inc(S("tr_ps"), 1)

            for i in range(24):
                if i in (0, 4, 8, 12, 16, 20, 22):
                    c = PEND.index(min(e for e in PEND if e > i))
                    if i:
                        ada(3 + c)
                    w = arrived(pe, proj_ch[c])
                    first_item = i
                if 2 <= i < 22:
                    pe.wait_ge(S("conv_v"), i - 1)
                elif i >= 22:
                    pe.wait_ge(S("z_ev"), i - 21)
                if i < 20:
                    n = item(i)[0]
                    j = i - first_item
                    if PROJ[c] == WBC:
                        j = i - 12
                    for k in range(KD):
                        ins = mm(ps[4 + i % 2][:, 0:n], w[:, k, j * P:(j + 1) * P], hT[:, k, 0:n],
                                 start=(k == 0), stop=(k == KD - 1))
                else:
                    t = i % 2
                    for k in range(KD):
                        ins = mm(ps[4 + i % 2][:, :], hT[:, k, t * P:(t + 1) * P], w[:, k, :],
                                 start=(k == 0), stop=(k == KD - 1))
                ins.then_inc(S("item_ps"), 1)
                if 6 <= i < 16:
                    rows_in(i - 2)
            ada(10)
            ada(11)
            pe.wait_ge(S("small_rd"), 1)
            for i in range(6):
                pe.wait_ge(S("sq_ready"), i + 1)
                if i >= 2:
                    pe.wait_ge(S("kq_root"), i - 1)
                mm(ps[2 + i % 2][:, :], ones, sqb[i % 2], start=True, stop=True).then_inc(S("sq_ps"), 1)
            pe.wait_ge(S("tr_ev"), 10)
            for i in range(4):
                pe.wait_ge(S("kq_norm"), i + 1)
                if i >= 2:
                    pe.wait_ge(S("kn_ev"), i - 1)
                for t in range(4):
                    ins = tr(ps[6 + i % 2][:, t * P:(t + 1) * P], kT[:, i, t * P:(t + 1) * P], ident)
                ins.then_inc(S("tr_ps"), 1)
            pe.wait_ge(S("g_ready"), 1)
            pe.wait_ge(S("kq_root"), 6)
            for t in range(4):
                for d in range(2):
                    mm(ps[2][:, t * 24 + d * 12:t * 24 + d * 12 + 12], mask[d], G[:, t, d * 12:d * 12 + 12],
                       start=True, stop=True)
            mm(ps[2][:, 128:224], ones, G[:, :, :].rearrange("p t n -> p (t n)"), start=True, stop=True) \
                .then_inc(S("one_ps"), 1)
            for t in range(T):
                for g in range(2):
                    ins = mm(pD[0][:, (2 * t + g) * P:(2 * t + g + 1) * P], BT[:, g, t * P:(t + 1) * P],
                             CT[:, g, t * P:(t + 1) * P], start=True, stop=True)
            ins.then_inc(S("one_ps"), 1)
            pe.wait_ge(S("gates"), 1)
            pe.wait_ge(S("mod"), 2)
            pe.wait_ge(S("state0"), 1)
            pe.wait_ge(S("kn_ev"), 4)
            pe.wait_ge(S("kq_norm"), 6)

            def sums_over(bank, t, c):
                d = 0 if c < 12 else 1
                for h in range(4):
                    ins = mm(bank[:, h * P:(h + 1) * P], G[:, t, c + h:c + h + 1].to_broadcast([P, P]), mask[d],
                             start=True, stop=True)
                return ins

            def piece(u, d, kind):
                t, c = tile_of(u, d), 12 * d + 4
                if kind in "ab":
                    m = 2 * (2 * (u - 2) + d) + (1 if kind == "b" else 0)
                    if kind == "a" and m:
                        pe.wait_ge(S("yd_rd"), 2 * (u - 2) + d)
                    if kind == "a":
                        pe.wait_ge(S("h_ready"), 2 * u + (0 if d == 0 else 1))
                    else:
                        pe.wait_ge(S("ws_arg"), m)
                    sums_over(pD[d], t, c + (4 if kind == "b" else 0)).then_inc(S("wg_ps"), 1)
                elif kind == "e":
                    m = 2 * u + d
                    if m >= 2:
                        pe.wait_ge(S("h_ready"), m - 1 if u < 2 else m)
                    if u >= 2:
                        pe.wait_ge(S("ws_arg"), 2 * (2 * (u - 2) + d + 1))
                        for g in range(2):
                            ins = mm(pD[d][:, g * L:(g + 1) * L], CT[:, g, t * P:(t + 1) * P],
                                     ht[:, d, g * L:(g + 1) * L], start=True, stop=True)
                        ins.then_inc(S("yo_ps"), 1)
                        pe.wait_ge(S("yo_rd"), 2 * (u - 2) + d + 1)
                    pe.wait_ge(S("xde_ready"), m + 1)
                    for g in range(2):
                        ins = mm(pD[d][:, g * L:(g + 1) * L], BN[:, t, g * P:(g + 1) * P],
                                 xde[:, g * L:(g + 1) * L], start=True, stop=True)
                    ins.then_inc(S("hs_ps"), 1)
                else:
                    pe.wait_ge(S("h_ready"), 2 * u + d + 1)
                    pe.wait_ge(S("ws_ready"), 2 * (u - 2) + d + 1)
                    pe.wait_ge(S("xdt_ready"), 2 * (u - 2) + d + 1)
                    for h in range(8):
                        ins = mm(pD[d][:, h * SP_:(h + 1) * SP_], Ws[:, h, :], xdt[:, h * SP_:(h + 1) * SP_],
                                 start=True, stop=True)
                    ins.then_inc(S("yd_ps"), 1)

            def four(bank, left, right):
                for h in range(4):
                    ins = mm(bank[:, h * P:(h + 1) * P], left(h), right(h), start=True, stop=True)
                return ins

            for u in range(4):
                for d in range(2):
                    t = tile_of(u, d)
                    at = slice(t * P, (t + 1) * P)
                    if u >= 1:
                        pe.wait_ge(S(f"s{d}"), u)
                    four(pA[d], lambda h: kT[:, h, at], lambda h: kT[:, h, at])
                    if u >= 2:
                        four(pC[d], lambda h: kT[:, h, at], lambda h: qT[:, h, at])
                    sums_over(pB[d], t, 12 * d).then_inc(S(f"pre{d}"), 1)
                for d in range(2):
                    pe.wait_ge(S(f"mn{d}"), u * LEVELS + 1)
                    four(pA[d], lambda h: Mn[d][0][:, h, :], lambda h: ident).then_inc(S(f"p_ps{d}"), 1)
                for l in range(1, LEVELS):
                    for d in range(2):
                        pe.wait_ge(S(f"mn{d}"), u * LEVELS + l + 1)
                        pe.wait_ge(S(f"x{d}"), u * LEVELS + l)
                        four(pA[d], lambda h: Mn[d][l % 2][:, h, :], lambda h: X[d][:, h, :]) \
                            .then_inc(S(f"p_ps{d}"), 1)
                    for d, kind in pieces(u, l):
                        piece(u, d, kind)
                    for d in range(2):
                        pe.wait_ge(S(f"p_ev{d}"), u * (LEVELS - 1) + l)
                        if l < LEVELS - 1:
                            four(pB[d], lambda h: XT[d][:, h, :], lambda h: Pv[d][:, h, :])
                        four(pC[d], lambda h: Pv[d][:, h, :], lambda h: XT[d][:, h, :]) \
                            .then_inc(S(f"q_ps{d}"), 1)
                for d in range(2):
                    t = tile_of(u, d)
                    at = slice(t * P, (t + 1) * P)
                    four(pA[d], lambda h: kT[:, h, at], lambda h: St[:, d, h, :]).then_inc(S(f"ks_ps{d}"), 1)
                for d in range(2):
                    pe.wait_ge(S(f"r{d}"), u + 1)
                    pe.wait_ge(S(f"x{d}"), LEVELS * (u + 1))
                    four(pB[d], lambda h: XT[d][:, h, :], lambda h: Mn[d][1][:, h, :]).then_inc(S(f"vn_ps{d}"), 1)
                for d in range(2):
                    t = tile_of(u, d)
                    at = slice(t * P, (t + 1) * P)
                    pe.wait_ge(S(f"vnew{d}"), u + 1)
                    if u >= 2:
                        pe.wait_ge(S(f"pt{d}"), u - 1)
                        four(pC[d], lambda h: qT[:, h, at], lambda h: St[:, d, h, :])
                        four(pA[d], lambda h: PT[d][:, h, :], lambda h: vnew[d][:, h, :]).then_inc(S(f"o_ps{d}"), 1)
                    if u < 3:
                        pe.wait_ge(S(f"kd{d}"), u + 1)
                        four(pB[d], lambda h: NT[d][:, h, :], lambda h: vnew[d][:, h, :]).then_inc(S(f"s_ps{d}"), 1)
            pe.wait_ge(S("normed"), 4)

            def columns(nth, src):
                for k in range(KD):
                    if k >= 2:
                        pe.wait_ge(S("cols_ev"), nth * KD + k - 1)
                    for t in range(T):
                        ins = tr(ps[2 + k % 2][:, t * P:(t + 1) * P], src(k, t), ident)
                    ins.then_inc(S("cols_ps"), 1)

            columns(0, lambda k, t: (oacc if k < 4 else yacc)[:, t, (k % 4) * P:(k % 4 + 1) * P])
            for i in range(16):
                pe.wait_ge(S("dg"), i + 1)
                mm(ps[4 + i // 4][:, (i % 4) * P:(i % 4 + 1) * P], ones, dg[i % 2], start=True,
                   stop=True).then_inc(S("dg_ps"), 1)
            pe.wait_ge(S("cols_ev"), 8)
            pe.wait_ge(S("gain_rows"), 4)

            def token_rows(bank, w, src, t, n, name):
                for k in range(KD):
                    ins = mm(ps[bank][:, 0:n], src[:, k, t * P:(t + 1) * P], w[:, k, :], start=(k == 0),
                             stop=(k == KD - 1))
                ins.then_inc(S(name), 1)

            for c in range(2):
                w = arrived(pe, wo_ch[c])
                for t in range(T):
                    token_rows(4 + 2 * c + t, w, mixT, t, 512, "wo_ps")
            pe.wait_ge(S("xh"), 6)
            columns(1, lambda k, t: xh[:, t, k * P:(k + 1) * P])
            pe.wait_ge(S("cols_ev"), 16)
            for b in range(KF):
                if b % 4 == 0:
                    wg = arrived(pe, ga_ch[b // 4])
                at = slice((b % 4) * P, (b % 4 + 1) * P)
                if b >= 2:
                    pe.wait_ge(S("f_taps"), b - 1)
                for k in range(KD):
                    ins = mm(ps[b % 2][:, 0:L], wg[:, k, at], hT2[:, k, :], start=(k == 0), stop=(k == KD - 1))
                ins.then_inc(S("gate_ps"), 1)
                if b % 4 == 0:
                    wu = arrived(pe, up_ch[b // 4])
                if b >= 2:
                    pe.wait_ge(S("f_hid"), b - 1)
                for k in range(KD):
                    ins = mm(ps[2 + b % 2][:, 0:L], wu[:, k, at], hT2[:, k, :], start=(k == 0), stop=(k == KD - 1))
                ins.then_inc(S("up_ps"), 1)
            pe.wait_ge(S("x_step"), 4)
            for c in range(6):
                w = arrived(pe, dn_ch[c])
                for kk in range(min(4, KF - 4 * c)):
                    k = 4 * c + kk
                    if c == 5 or kk == 0:
                        pe.wait_ge(S("f_hid"), min(k + 4, KF))
                    for t in range(T):
                        for h in range(2):
                            ins = mm(ps[4 + 2 * t + h][:, :], hid[:, k, t * P:(t + 1) * P],
                                     w[:, kk, 512 * h:512 * h + 512], start=(k == 0), stop=(k == KF - 1))
                ins.then_inc(S("down_ps"), 1)
            pe.wait_ge(S("xh"), 8)
            columns(2, lambda k, t: xh[:, t, k * P:(k + 1) * P])
            pe.wait_ge(S("cols_ev"), 24)
            for i, (c0, n) in enumerate(IN2):
                w = arrived(pe, in2_ch[i])
                for t in range(T):
                    j = 2 * i + t
                    if j >= 4:
                        pe.wait_ge(S("in2_ev"), j - 3)
                    token_rows(4 + j % 4, w, uT, t, n, "in2_ps")
            for i in range(13):
                if i == 0:
                    pe.wait_ge(S("rot_a"), 2)
                if i == 5:
                    pe.wait_ge(S("rot_b"), 2)
                if i >= 2:
                    pe.wait_ge(S("qt_ev"), i - 1)
                for hh in range(2):
                    head = 2 * i + hh
                    c0 = head * HD if head < 10 else 768 + (head - 10) * HD
                    for t in range(T):
                        ins = tr(ps[i % 2][0:HD, hh * L + t * P:hh * L + (t + 1) * P], pj[:, t, c0:c0 + HD], ident)
                ins.then_inc(S("qt_ps"), 1)
            pe.wait_ge(S("qt_ev"), 13)
            pe.wait_ge(S("in2_ev"), 10)

            def scores(h):
                qi, ki = (h, 8 + h // 4) if h < 8 else (2 + h, 10 + h)
                if h >= 2:
                    pe.wait_ge(S("s_exp"), 2 * (h - 1))
                for t in range(T):
                    ins = mm(ps[h % 2][:, t * L:(t + 1) * L], qkT[0:HD, qi, t * P:(t + 1) * P], qkT[0:HD, ki, :],
                             start=True, stop=True)
                ins.then_inc(S("s_ps"), 1)

            def prob_rows(h):
                pe.wait_ge(S("s_exp"), 2 * h + 2)
                if h >= 2:
                    pe.wait_ge(S("pt_ev"), h - 1)
                for kt in range(2):
                    for t in range(T):
                        ins = tr(ps[2 + h % 2][:, (2 * kt + t) * P:(2 * kt + t + 1) * P],
                                 pr[h % 2][:, t, kt * P:(kt + 1) * P], ident)
                ins.then_inc(S("pt_ps"), 1)

            def values(h):
                vc = 640 + HD * (h // 4) if h < 8 else 1792 + HD * (h - 8)
                pe.wait_ge(S("pt_ev"), h + 1)
                for t in range(T):
                    for kt in range(2):
                        ins = mm(ps[4 + 2 * (h // 8) + t][:, (h % 8) * HD:(h % 8 + 1) * HD], prT[h % 2][:, kt, t, :],
                                 pj[:, kt, vc:vc + HD], start=(kt == 0), stop=(kt == 1))
                ins.then_inc(S("pv_ps"), 1)

            for h in range(18):
                if h < 16:
                    scores(h)
                if 1 <= h < 17:
                    prob_rows(h - 1)
                if h >= 2:
                    values(h - 2)
            pe.wait_ge(S("normed"), 8)
            columns(3, lambda k, t: on[:, t, k * P:(k + 1) * P])
            pe.wait_ge(S("cols_ev"), 32)
            for c in range(2):
                w = arrived(pe, wo2_ch[c])
                for t in range(T):
                    token_rows(4 + 2 * c + t, w, uT, t, 512, "wo2_ps")
            pe.wait_ge(S("xh"), 10)
            columns(4, lambda k, t: xh[:, t, k * P:(k + 1) * P])
            pe.wait_ge(S("cols_ev"), 40)
            pe.wait_ge(S("in_rw"), 16)
            for t in range(T):
                for k in range(KD):
                    ins = mm(ps[0][:, t * 36:(t + 1) * 36], u2T[:, k, t * P:(t + 1) * P], rw[:, k, :],
                             start=(k == 0), stop=(k == KD - 1))
            ins.then_inc(S("one_ps"), 1)
            pe.wait_ge(S("flag"), 1)
            flag = ra[4]
            mm(ps[1][:, 0:NE], C("strict", P), flag[:, 0, :], start=True, stop=True)
            mm(ps[1][:, NE:2 * NE], ones, flag[:, 0, :], start=True, stop=False)
            mm(ps[1][:, NE:2 * NE], C("strict", P), flag[:, 1, :], start=False, stop=True)
            mm(ps[1][:, 2 * NE:3 * NE], ones, flag[:, 0, :], start=True, stop=False)
            mm(ps[1][:, 2 * NE:3 * NE], ones, flag[:, 1, :], start=False, stop=True).then_inc(S("one_ps"), 1)
            pe.wait_ge(S("count_ready"), 1)
            npairs = pe.value_load(niter_t[0:1, 0:1], min_val=NPAIR, max_val=4 * NPAIR)

            def gather(n):
                pe.wait_ge(S("sel"), n)
                for k in range(KD):
                    for t in range(T):
                        ins = mm(ps[4 + k // 4][:, (k % 4) * P:(k % 4 + 1) * P], u2[:, t, k * P:(k + 1) * P],
                                 sel[:, t, :], start=(t == 0), stop=(t == 1))
                ins.then_inc(S("gather_ps"), 1)

            def gate_up(p, j):
                pe.wait_ge(S(f"loaded{2 * j}"), p * 16 + 16 * (base[2 * j] + 1))
                wg = slot(2 * j).rearrange("p (k n) -> p k n", k=KD)
                wu = slot(2 * j + 1).rearrange("p (k n) -> p k n", k=KD)
                for w, at, name in ((wg, 0, "gate_rd"), (wu, 256, "gu_ps")):
                    if at:
                        pe.wait_ge(S(f"loaded{2 * j + 1}"), p * 16 + 16 * (base[2 * j + 1] + 1))
                    for f in range(4):
                        for k in range(KD):
                            ins = mm(ps[6][:, at + f * SLOT:at + (f + 1) * SLOT], w[:, k, f * P:(f + 1) * P],
                                     xsel[:, k, j * SLOT:(j + 1) * SLOT], start=(k == 0), stop=(k == KD - 1))
                    ins.then_inc(S(name), 1)

            def down(p, j):
                pe.wait_ge(S(f"loaded{4 + j}"), p * 16 + 16)
                w = slot(4 + j).rearrange("p (k n) -> p k n", k=4)
                for k in range(KD):
                    for f in range(4):
                        ins = mm(ps[7][:, k * SLOT:(k + 1) * SLOT], w[:, f, k * P:(k + 1) * P], hide[j][:, f, :],
                                 start=(f == 0), stop=(f == 3))
                ins.then_inc(S("yt_ps"), 1)

            def out_rows(p):
                pe.wait_ge(S("ysb"), 2 * p + 2)
                for k in range(KD):
                    ins = tr(ps[4 + k // 4][:, (k % 4) * P:(k % 4 + 1) * P], ysb[:, k, :], ident)
                ins.then_inc(S("yn_ps"), 1)
                pe.wait_ge(S("gsel"), p + 1)
                for t in range(T):
                    ins = tr(ps[7][:, t * P:(t + 1) * P], gsel[:, t, :], ident)
                ins.then_inc(S("gt_ps"), 1)

            def scatter(p, last):
                pe.wait_ge(S("yn_a"), p + 1)
                pe.wait_ge(S("yn_v"), p + 1)
                pe.wait_ge(S("gt_ev"), p + 1)
                for t in range(T):
                    for c in range(2):
                        ins = mm(ps[2 * t + c][:, :], gselT[:, t * P:(t + 1) * P], yN[:, 512 * c:512 * c + 512],
                                 start=False, stop=last)
                ins.then_inc(S("sc_ps"), 1)

            for t in range(T):
                for c in range(2):
                    ins = mm(ps[2 * t + c][:, :], ysb[:, 0, :], u2[:, 0, 0:512], start=True, stop=False)
            ins.then_inc(S("sc_ps"), 1)
            gather(1)
            pe.wait_ge(S("xsel_a"), 1)
            with pe.Fori(0, npairs) as p:
                pe.wait_ge(S("xsel_a"), p + 1)
                pe.wait_ge(S("xsel_v"), p + 1)
                pe.wait_ge(S("hid"), 2 * p + 2)
                gate_up(p, 0)
                out_rows(p)
                pe.wait_ge(S("hid"), 2 * p + 3)
                gate_up(p, 1)
                scatter(p, False)
                down(p, 0)
                gather(p + 2)
                pe.wait_ge(S("hid"), 2 * p + 4)
                pe.wait_ge(S("ysb"), 2 * p + 3)
                down(p, 1)
            pe.wait_ge(S("xsel_a"), npairs + 1)
            pe.wait_ge(S("xsel_v"), npairs + 1)
            out_rows(npairs)
            scatter(npairs, True)


def constants():
    import numpy as np
    c = np.zeros((P, NCO), np.float32)
    j, i = np.arange(P)[:, None], np.arange(P)[None, :]
    c[:, CO["ident"]:CO["ident"] + P] = i == j
    c[:, CO["ones"]:CO["ones"] + P] = 1
    c[:, CO["mf"]:CO["mf"] + P] = i >= j
    c[:, CO["mb"]:CO["mb"] + P] = i <= j
    c[:, CO["strict"]:CO["strict"] + P] = i > j
    for lv in range(LEVELS):
        s = 2 ** lv
        m = (i // (2 * s) == j // (2 * s)) & (j % (2 * s) < s) & (i % (2 * s) >= s)
        c[:, CO["lvl"] + lv * P:CO["lvl"] + (lv + 1) * P] = m
        c[:, CO["lvl"] + (LEVELS + lv) * P:CO["lvl"] + (LEVELS + lv + 1) * P] = m.T
    c[:, CO["iota"]:CO["iota"] + SLOT] = np.arange(SLOT)
    c[:, CO["desc"]:CO["desc"] + NE] = NE - np.arange(NE)
    c[:, CO["eps"]:CO["eps"] + 4] = (EPS, EPS * P, 1.0, 0.0)

    def inv(dim):
        e = np.arange(0, dim, 2, dtype=np.float32) / np.float32(dim)
        return (np.float32(1.0) / (np.float32(10000.0) ** e)).astype(np.float32)

    tok = np.arange(L)
    row, colm = (tok // GRID).astype(np.float32), (tok % GRID).astype(np.float32)
    axial = np.concatenate([row[:, None] * inv(HD // 2), colm[:, None] * inv(HD // 2)], axis=1)
    linear = tok.astype(np.float32)[:, None] * inv(HD)
    for kind, ang in enumerate((axial, linear)):
        cos, sin = np.cos(ang.astype(np.float64)), np.sin(ang.astype(np.float64))
        tab = np.concatenate([cos, cos, -sin, sin], axis=1).astype(np.float32)
        for t in range(T):
            at = CO["rope"] + (kind * T + t) * 2 * HD
            c[:, at:at + 2 * HD] = tab[t * P:(t + 1) * P]
    q, k = tok[:, None], tok[None, :]
    count = np.zeros((L, L))
    for window, dil in ((128, 1), (512, 4), (2048, 16)):
        count += (q % dil == k % dil) & (np.abs(q // dil - k // dil) <= window // (2 * dil))
    bias = np.where(count > 0, np.log(np.maximum(count, 1)), -1e30).astype(np.float32)
    return c, bias


def kernel(**inputs):
    import numpy as np
    import concourse.bacc as _bacc
    from concourse.bass_utils import run_bass_kernel_spmd as _run

    v = {n: np.asarray(a) for n, a in inputs.items()}
    r = lambda n: v[n].reshape(-1, P)
    w_in = v["w_in"][0]
    vec = np.concatenate([
        r("b_ada"), r("norm1_g"), r("norm2_g"), r("gdn_conv_w"), r("ssm_conv_w"), r("ssm_conv_b"),
        np.repeat(r("gdn_norm_g"), 4, axis=0), r("ssm_norm_g"), r("norm1_g_2"), r("out_norm_a_g_2"),
        r("out_norm_b_g_2"), r("norm2_g_2"), r("ffn_conv_w"), r("ffn_conv_b")], axis=0)
    vec = np.concatenate([vec, np.zeros((NROWS - vec.shape[0], P), np.float32)], axis=0)
    both = lambda a, b: np.concatenate([a[0, 0], b[0, 0], a[0, 1], b[0, 1]])
    rowv = np.concatenate([
        both(v["gdn_dt_bias"], v["ssm_dt_bias"]), both(v["gdn_A_log"], v["ssm_A_log"]), v["ssm_D"][0],
        v["q_norm_g_2"][0], v["k_norm_g_2"][0], v["router_group_b_2"][0], v["router_expert_b_2"][0]])
    small = np.concatenate([w_in[:, 2048:2052], w_in[:, 3600:3608], w_in[:, 2052:2056], w_in[:, 3608:3616],
                            w_in[:, 2056:2064]], axis=1)
    consts, bias = constants()
    cc = np.stack([v["c"].reshape(KD, P).T, v["c_ctx"].reshape(KD, P).T], axis=2)
    arrays = {
        "x": v["x"][0], "ctx": v["ctx"][0], "cc": cc, "vec_rows": vec, "rowv": rowv[None, :], "w_small": small,
        "consts": consts, "bias": bias, "w_ada": v["w_ada"][0], "w_in": w_in, "w_out": v["w_out"][0],
        "w_gate": v["ffn_w_gate"][0], "w_up": v["ffn_w_up"][0], "w_down": v["ffn_w_down"][0],
        "fng": v["final_norm_g"][None, :], "fng2": v["final_norm_g_2"][None, :], "n2row": v["norm2_g_2"],
        "w_in2": v["w_in_2"][0], "w_out2": v["w_out_2"][0],
        "rw": np.concatenate([v["router_group_w_2"][0], v["router_expert_w_2"][0]], axis=1),
        "e_gate": v["w_gate_2"][0], "e_up": v["w_up_2"][0], "e_down": v["w_down_2"][0],
    }
    arrays = {n: np.ascontiguousarray(a) for n, a in arrays.items()}
    nc = _bacc.Bacc("TRN2", target_bir_lowering=False, num_devices=1)
    ap = {n: nc.dram_tensor("in_" + n, a.shape, mybir.dt.from_np(a.dtype), kind="ExternalInput").ap()
          for n, a in arrays.items()}
    out = nc.dram_tensor("out", (L, D), mybir.dt.float32, kind="ExternalOutput").ap()
    build(nc, ap, out)
    got = _run(nc, [{"in_" + n: a for n, a in arrays.items()}], core_ids=[0])
    return got.results[0]["out"].reshape(1, L, D)
```

```python
import math
from contextlib import ExitStack

import concourse.bass as bass
from concourse import mybir

P = 128
D = 1024
L = 256
T = L // P
KD = D // P
EPS = 1e-6
GH, SH, SG, SP_ = 4, 8, 2, 64
FF = 2816
KF = FF // P
ARENA = 28560
NE, DE, SLOT = 32, 512, 64
NPAIR = NE // 2
EXTRA = 8
NU = NE + EXTRA
HD = 64
SCALE = HD ** -0.5
LEVELS = 7
GRID = 64

WQ, WK, WV, WZG = 0, 512, 1024, 1536
WZS, WXS, WBC = 2064, 2576, 3088
ROWS = {}
_at = 0
for _name, _n in (("b_ada", 48), ("norm1", 8), ("norm2", 8), ("gconv", 36), ("sconv", 24), ("sconvb", 8),
                  ("mixg", 8), ("n1b", 8), ("outab", 8), ("n2b", 8), ("fconv", 9 * KF), ("fconvb", KF)):
    ROWS[_name] = _at
    _at += _n
NROWS = 3 * P
assert _at <= NROWS
RV = {}
_at = 0
for _name, _n in (("dtb", 24), ("alog", 24), ("ssmD", 8), ("qn", 64), ("kn", 64), ("rb", 36)):
    RV[_name] = _at
    _at += _n
NRV = _at
CO = {}
_at = 0
for _name, _n in (("ident", P), ("ones", P), ("mf", P), ("mb", P), ("lvl", 2 * LEVELS * P), ("strict", P),
                  ("iota", SLOT), ("desc", NE), ("eps", 4), ("fold", 32), ("rope", 2 * T * 2 * HD)):
    CO[_name] = _at
    _at += _n
NCO = _at


def build(nc, ap, out):
    f32, i32 = mybir.dt.float32, mybir.dt.int32
    ACT, ALU, AX = mybir.ActivationFunctionType, mybir.AluOpType, mybir.AxisListType.X
    MUL, ADD, SUB = ALU.mult, ALU.add, ALU.subtract
    stack = ExitStack()
    with stack:
        sems = {}

        def S(name):
            if name not in sems:
                sems[name] = stack.enter_context(nc.semaphore(name))
            return sems[name]

        ring = stack.enter_context(nc.sbuf_tensor("ring", [P, 6 * 4096], f32))
        A = stack.enter_context(nc.sbuf_tensor("arena", [P, ARENA], f32))
        units = stack.enter_context(nc.sbuf_tensor("units", [P, NU + 2], i32))
        ps = [stack.enter_context(nc.psum_tensor(f"bank{i}", [P, 512], f32)) for i in range(8)]

        top = [0]

        def take(n, at=None):
            a = top[0] if at is None else at
            if at is None:
                top[0] += n
            assert a + n <= ARENA, (a, n)
            return A[:, a:a + n]

        co = take(NCO)
        C = lambda k, n: co[:, CO[k]:CO[k] + n]
        ident, ones = C("ident", P), C("ones", P)
        mask = [C("mf", P), C("mb", P)]
        lvl = [[co[:, CO["lvl"] + (d * LEVELS + l) * P:CO["lvl"] + (d * LEVELS + l + 1) * P] for l in range(LEVELS)]
               for d in range(2)]
        col = take(NROWS)
        V = lambda k, i, n=1: col[:, ROWS[k] + i:ROWS[k] + i + n]
        rowv = take(NRV)
        R = lambda k, n: rowv[:, RV[k]:RV[k] + n]
        mod = take(96).rearrange("p (j c) -> p j c", c=2)
        scale1 = take(16).rearrange("p (j c) -> p j c", c=2)
        scale2 = take(8)
        stat = take(32)
        rstd = take(32)
        yoff = take(512)
        x = take(T * D).rearrange("p (t n) -> p t n", t=T)
        F0 = top[0]

        def lay(at, n):
            assert F0 + at + n <= ARENA, (at, n)
            return A[:, F0 + at:F0 + at + n]

        def tiles(v, t):
            return v.rearrange("p (t n) -> p t n", t=t)

        kT, BT = tiles(lay(0, 2048), 4), tiles(lay(2048, 1024), 2)
        CT, qT = tiles(lay(3072, 512), 2), tiles(lay(3584, 1024), 4)
        vN, kN, xsN = tiles(lay(4608, 2048), 4), tiles(lay(6656, 2048), 4), tiles(lay(8704, 2048), 4)
        BN, Z = tiles(lay(10752, 1024), 4), tiles(lay(11776, 2048), 2)
        hT, ctx = tiles(lay(13824, 4096), KD), tiles(lay(17920, 2048), 2)
        St = lay(13824, 1024).rearrange("p (d h e) -> p d h e", d=2, h=4)
        ht = tiles(lay(14848, 1024), 2)
        vnew = [tiles(lay(15872 + 512 * d, 512), 4) for d in range(2)]
        xdt, xde = lay(16896, 512), lay(17408, 512)
        Ws = tiles(lay(17920, 1024), 8)
        CBs = lay(18944, 512).rearrange("p (t g i) -> p t g i", t=T, g=2)
        gx = tiles(lay(19968, 128), 4)
        G, dtv, gtmp, gc, egc, kd, etot, dtkd = (tiles(lay(20096 + 96 * i, 96), 4) for i in range(8))
        beta, nbeta, nega = tiles(lay(20864, 32), 4), tiles(lay(20896, 32), 4), lay(20928, 24)
        oacc, yacc = kN[:, 2:4, :], vN[:, 2:4, :]

        def scratch(at, n):
            return ring[:, 4 * 4096 + at:4 * 4096 + at + n]

        xn = tiles(scratch(0, 4096), 4)
        cconv = [scratch(4096 + 512 * i, 512) for i in range(2)]
        csilu = [scratch(5120 + 512 * i, 512) for i in range(3)]
        sqb = [scratch(6656 + 512 * i, 512) for i in range(2)]
        root = [scratch(512 * i, 512) for i in range(2)]
        vecs = scratch(6656, 3 * P)
        craw = scratch(7680, 16).rearrange("p (k c) -> p k c", c=2)
        csil = tiles(scratch(7696, 256), KD)
        wsm = tiles(lay(20960, 256), KD)
        arow = [lay(21216, 512), yoff]
        junk0 = scratch(4096, 1024)
        E, NT, PT, Pv, X, XT, Mn0, Mn1 = ([tiles(scratch(4096 * d + 512 * i, 512), 4) for d in range(2)]
                                          for i in range(8))
        Mn = [[Mn0[d], Mn1[d]] for d in range(2)]
        pA, pB, pC, pD = [ps[0], ps[4]], [ps[1], ps[5]], [ps[2], ps[6]], [ps[3], ps[7]]

        mixT, g1r, g2r = tiles(lay(0, 2048), KD), lay(2048, D), lay(3072, D)
        dg = [lay(4096 + P * i, P) for i in range(2)]
        hid = tiles(lay(4608, KF * L), KF)
        fng = [lay(10240, D), lay(11264, 512)]
        tmpx = [lay(12288 + 512 * i, 512) for i in range(2)]
        xh, hT2 = tiles(lay(13824, 2048), 2), tiles(lay(15872, 2048), KD)
        fa, fs = [lay(17920 + L * i, L) for i in range(2)], [lay(18432 + L * i, L) for i in range(2)]
        junk = lay(18944, 1024)
        n2row = lay(19968, D)
        fng2 = lay(20992, D)
        fng1 = lay(10240, D)

        pj = tiles(lay(0, 4608), 2)
        rotb = tiles(lay(4608, 2048), 2)
        rota = tiles(lay(6656, 1280), 2)
        sqT = lay(4608, 2048)
        sc = [tiles(lay(7936 + 512 * i, 512), 2) for i in range(2)]
        pr = [tiles(lay(8960 + 512 * i, 512), 2) for i in range(2)]
        mx, sm = (lay(9984 + 32 * i, 32).rearrange("p (h t) -> p h t", t=2) for i in range(2))
        prT = [lay(12288 + 512 * i, 512).rearrange("p (k t q) -> p k t q", k=2, t=2) for i in range(2)]
        bias = tiles(lay(13312, 512), 2)
        qkT = tiles(scratch(0, 26 * L), 26)
        uT = hT2

        u2, u2T = tiles(lay(0, 2048), 2), hT2
        rw, lg = tiles(lay(2048, 288), KD), tiles(lay(2336, 72), 2)
        ra = [tiles(lay(2408 + 64 * i, 64), 2) for i in range(6)]
        rs = lay(2792, 32).rearrange("p (j t) -> p j t", t=2)
        SL, GT = tiles(lay(2824, 2 * (NU + 2)), 2), tiles(lay(2912, 2 * (NU + 2)), 2)
        cur = lay(3352, 8).rearrange("p (c t e) -> p c t e", c=2, t=2)
        sel, gsel = tiles(lay(3360, 256), 2), tiles(lay(3616, 256), 2)
        gselT = lay(4128, 256)
        xsel, hidN, sg, hidT = tiles(lay(4608, 1024), KD), lay(5632, 512), lay(6144, 512), tiles(lay(6656, 512), 4)
        yN = lay(7168, D)
        over, scanA, scanB = (lay(8192 + 96 * i, 96) for i in range(3))
        cnt = lay(8480, 40)
        blk, unitE, unitB = tiles(lay(8520, 24), EXTRA), lay(8544, EXTRA), lay(8552, EXTRA)
        place = lay(12288, EXTRA * 96)
        ofexp, pick = tiles(lay(13056, EXTRA * NE), EXTRA), tiles(lay(8576, EXTRA * NE), EXTRA)

        def item(i):
            g, s = ROWS["gconv"], ROWS["sconv"]
            if i < 4:
                return 512, [g + 12 * a + 4 + i for a in range(3)], None, kT[:, i, :]
            if i < 8:
                return 512, [g + 12 * a + 4 + i for a in range(3)], None, csilu[i % 3]
            if i < 12:
                return 512, [s + 8 * a + i - 8 for a in range(3)], ROWS["sconvb"] + i - 8, csilu[i % 3]
            if i < 14:
                return 512, [s + 8 * a + i - 8 for a in range(3)], ROWS["sconvb"] + i - 8, BT[:, i - 12, :]
            if i < 16:
                return L, [s + 8 * a + i - 8 for a in range(3)], ROWS["sconvb"] + i - 8, CT[:, i - 14, :]
            return L, [g + 12 * a + i - 16 for a in range(3)], None, qT[:, i - 16, :]

        SQ_AT = (5, 7, 9, 11, 20, 21)

        def kq_block(n):
            return kT[:, n, :] if n < 4 else qT[:, 2 * n - 8:2 * n - 6, :].rearrange("p h t -> p (h t)")

        def tile_of(u, d):
            step = u % 2
            return (step if d == 0 else 1 - step) + (2 if u < 2 else 0)

        def pieces(u, l):
            if u < 2:
                return {1: [(0, "e")], 3: [(1, "e")]}.get(l, [])
            return {1: [(0, "a")], 2: [(0, "b")], 3: [(0, "e"), (0, "c")], 4: [(1, "a")], 5: [(1, "b")],
                    6: [(1, "e"), (1, "c")]}.get(l, [])

        def heads(v, n, e):
            return v.rearrange("p (h e) -> p h e", h=n, e=e)

        def wide(v, n):
            return v.unsqueeze(2).to_broadcast([P, v.shape[1], n])

        def each(v, h):
            return v.unsqueeze(1).to_broadcast([P, h, v.shape[1]])

        def rope(kind, t):
            at = CO["rope"] + (kind * T + t) * 2 * HD
            return co[:, at:at + HD], co[:, at + HD:at + 2 * HD]

        def slot(s):
            return ring[:, s * 4096:(s + 1) * 4096]

        chunks = []

        def cols(w, c0, n):
            return (lambda s: slot(s)[:, 0:KD * n].rearrange("p (k n) -> p k n", k=KD),
                    w[:, c0:c0 + n].rearrange("(k p) n -> p k n", p=P))

        def rows(w, k0, nk):
            return (lambda s: slot(s)[:, 0:nk * D].rearrange("p (k n) -> p k n", k=nk),
                    w[k0 * P:(k0 + nk) * P, :].rearrange("(k p) n -> p k n", p=P))

        def add(view, done, value):
            chunks.append((view, done, value))
            return len(chunks) - 1

        ada_ch = [add(cols(ap["w_ada"], 512 * i, 512), "rows_ps", i + 1) for i in range(4)]
        proj_ch = []
        PROJ = (WK, WV, WXS, WBC, WQ, WZG, WZS)
        PEND = (4, 8, 12, 16, 20, 22, 24)
        for i, c0 in enumerate(PROJ):
            proj_ch.append(add(cols(ap["w_in"], c0, 512), "item_ps", PEND[i]))
            ada_ch.append(add(cols(ap["w_ada"], 512 * (4 + i), 512), "rows_ps", 6 + i))
        ada_ch.append(add(cols(ap["w_ada"], 512 * 11, 512), "rows_ps", 13))
        wo_ch = [add(cols(ap["w_out"], 512 * c, 512), "wo_ps", 2 * c + 2) for c in range(2)]
        ga_ch, up_ch = [], []
        for c in range(6):
            n = min(512, FF - 512 * c)
            ga_ch.append(add(cols(ap["w_gate"], 512 * c, n), "gate_ps", min(4 * c + 4, KF)))
            up_ch.append(add(cols(ap["w_up"], 512 * c, n), "up_ps", min(4 * c + 4, KF)))
        dn_ch = [add(rows(ap["w_down"], 4 * c, min(4, KF - 4 * c)), "down_ps", c + 1) for c in range(6)]
        IN2 = ((0, 512), (512, 256), (768, 512), (1280, 512), (1792, 512))
        in2_ch = [add(cols(ap["w_in2"], c0, n), "in2_ps", 2 * i + 2) for i, (c0, n) in enumerate(IN2)]
        wo2_ch = [add(cols(ap["w_out2"], 512 * c, 512), "wo2_ps", 2 * c + 2) for c in range(2)]
        NCH = len(chunks)
        base = [len(range(s, NCH, 4)) for s in range(4)] + [0, 0]

        def arrived(pe, n):
            pe.wait_ge(S(f"loaded{n % 4}"), 16 * (n // 4 + 1))
            return chunks[n][0][0](n % 4)

        block = stack.enter_context(nc.Block())

        @block.sync
        def _(sp):
            for n, ((view, dram), done, value) in enumerate(chunks):
                if n >= 4:
                    sp.wait_ge(S(chunks[n - 4][1]), chunks[n - 4][2])
                sp.dma_start(view(n % 4), dram).then_inc(S(f"loaded{n % 4}"), 16)
                if n == 2:
                    sp.dma_start(ctx, ap["ctx"].rearrange("(t p) n -> p t n", p=P)).then_inc(S("in_ctx"), 16)

            ORDER = (("e_gate", 0), ("e_gate", 1), ("e_up", 0), ("e_up", 1), ("e_down", 0), ("e_down", 1))

            def expert(e, s):
                name = ORDER[s][0]
                nk = 4 if name == "e_down" else KD
                sp.dma_start(slot(s).rearrange("p (o k n) -> p o k n", o=1, k=nk),
                             ap[name][bass.ds(e, 1), :, :].rearrange("o (k p) n -> p o k n", p=P)) \
                    .then_inc(S(f"loaded{s}"), 16)

            sp.wait_ge(S("pv_ps"), 16)
            expert(0, 4)
            expert(1, 5)
            for last in range(NCH - 4, NCH):
                sp.wait_ge(S(chunks[last][1]), chunks[last][2])
                expert(ORDER[last % 4][1], last % 4)
            sp.wait_ge(S("count_ready"), 1)
            npairs = sp.value_load(units[0:1, NU:NU + 1], min_val=NPAIR, max_val=NU // 2)
            with sp.Fori(1, npairs) as p:
                e = [sp.value_load(units[0:1, bass.ds(2 * p + j, 1)], min_val=0, max_val=NE - 1) for j in range(2)]
                for s, (sem, n) in enumerate((("eg_ps", 1), ("eg_ps", 1), ("eu_ps", 1), ("eu_ps", 1),
                                              ("yn_ps", 2), ("yn_ps", 2))):
                    sp.wait_ge(S(sem), n * p)
                    expert(e[ORDER[s][1]], s)
            sp.wait_ge(S("out_ready"), 1)
            sp.dma_start(out.rearrange("(t p) n -> p t n", p=P), x).then_inc(S("out_done"), 16)
            sp.wait_ge(S("out_done"), 16)

        @block.gpsimd
        def _(g):
            def mul(o_, a, b):
                return nc.gpsimd.tensor_tensor(o_, a, b, MUL)

            for n in range(6):
                g.wait_ge(S("item_silu"), n + 1 if n < 4 else 20)
                if n >= 2:
                    g.wait_ge(S("sq_ps"), n - 1)
                mul(sqb[n % 2], kq_block(n), kq_block(n)).then_inc(S("sq_ready"), 1)
            g.wait_ge(S("item_ps"), 24)
            nc.gpsimd.memset(St[:, :, :, :], 0.0)
            nc.gpsimd.memset(ht[:, :, :], 0.0).then_inc(S("state0"), 1)
            g.wait_ge(S("gates"), 1)

            def piece(u, d, kind):
                t = tile_of(u, d)
                if kind == "c":
                    n = 2 * (u - 2) + d + 1
                    g.wait_ge(S("ws_exp"), n)
                    mul(Ws[:, :, :], Ws[:, :, :], each(mask[d], 8)).then_inc(S("ws_mask"), 1)
                    if n > 1:
                        g.wait_ge(S("yd_ps"), n - 1)
                    mul(heads(xdt, 8, SP_), heads(xsN[:, t, :], 8, SP_),
                        wide(dtv[:, t, 12 * d + 4:12 * d + 12], SP_)).then_inc(S("xdt_ready"), 1)
                if kind == "e":
                    n = 2 * u + d + 1
                    if n > 1:
                        g.wait_ge(S("hs_ps"), n - 1)
                    mul(heads(xde, 8, SP_), heads(xsN[:, t, :], 8, SP_),
                        wide(dtkd[:, t, 12 * d + 4:12 * d + 12], SP_)).then_inc(S("xde_ready"), 1)

            for u in range(4):
                for d in range(2):
                    g.wait_ge(S(f"nt{d}"), u + 1)
                    if u:
                        g.wait_ge(S(f"vn_ps{d}"), u)
                    for l in range(2):
                        mul(Mn[d][l], NT[d], each(lvl[d][l], 4)).then_inc(S(f"mn{d}"), 1)
                    if u >= 2:
                        mul(PT[d], PT[d], each(mask[d], 4)).then_inc(S(f"pt{d}"), 1)
                for l in range(1, LEVELS):
                    if l + 1 < LEVELS:
                        for d in range(2):
                            g.wait_ge(S(f"p_ps{d}"), u * LEVELS + l)
                            if l == 1:
                                g.wait_ge(S(f"x{d}"), u * LEVELS + 1)
                            mul(Mn[d][(l + 1) % 2], NT[d], each(lvl[d][l + 1], 4)).then_inc(S(f"mn{d}"), 1)
                    for d, kind in pieces(u, l):
                        piece(u, d, kind)
                for d in range(2 if u < 3 else 0):
                    t = tile_of(u, d)
                    g.wait_ge(S(f"mn{d}"), LEVELS * (u + 1))
                    mul(NT[d], heads(kN[:, t, :], 4, P), wide(kd[:, t, 12 * d:12 * d + 4], P)) \
                        .then_inc(S(f"kd{d}"), 1)
            for t in range(T):
                g.wait_ge(S("in2_ev"), 8 + t + 1)
            link_n = 0
            for t in range(T):
                src = pj[:, t, 768:1792]
                s4, r4 = src.rearrange("p (h a e) -> p h a e", h=16, a=2), \
                    rotb[:, t, :].rearrange("p (h a e) -> p h a e", h=16, a=2)
                cos, sin = rope(1, t)
                for a in range(2):
                    mul(r4[:, :, a, :], s4[:, :, 1 - a, :], each(sin[:, 32 * a:32 * a + 32], 16)) \
                        .then_inc(S("pool_rot"), 1)
                link_n += 2
                g.wait_ge(S("pool_rot"), link_n)
                mul(heads(src, 16, HD), heads(src, 16, HD), each(cos, 16)).then_inc(S("pool_rot"), 1)
                link_n += 1
                g.wait_ge(S("pool_rot"), link_n)
                nc.gpsimd.tensor_tensor(src, src, rotb[:, t, :], ADD).then_inc(S("rot_b"), 1)

        @block.scalar
        def _(a):
            act = nc.scalar.activation
            a.dma_start(craw, ap["cc"]).then_inc(S("in_c"), 16)
            a.dma_start(co, ap["consts"]).then_inc(S("in_consts"), 16)
            a.dma_start(x, ap["x"].rearrange("(t p) n -> p t n", p=P)).then_inc(S("in_x"), 16)
            a.dma_start(tiles(vecs, 3), ap["vec_rows"].rearrange("(i p) n -> p i n", p=P)).then_inc(S("in_vecs"), 16)
            a.dma_start(wsm, ap["w_small"].rearrange("(k p) n -> p k n", p=P)).then_inc(S("in_rest"), 16)
            a.dma_start(rowv, ap["rowv"].to_broadcast([P, NRV])).then_inc(S("in_rest"), 16)
            a.wait_ge(S("in_c"), 16)
            a.wait_ge(S("v_early"), 1)
            act(csil[:, :, 0:2], craw, ACT.Silu).then_inc(S("c_silu"), 1)

            def rows_copy(j):
                a.wait_ge(S("rows_ps"), j + 1)
                if j >= 2:
                    a.wait_ge(S("fold_ps"), j - 1)
                act(arow[j % 2], ps[2 * (j % 2)][:, :], ACT.Copy).then_inc(S("rows_ev"), 1)

            for j in range(3):
                rows_copy(j)

            def rms(k, srcs, space):
                for i, s in enumerate(srcs):
                    if k == 0 and i in (0, 2):
                        a.wait_ge(S("in_ctx" if i else "in_x"), 16)
                    if k or i:
                        a.wait_ge(S("rms_sq"), (2 + 2 * k if k else 0) + i)
                    act(space, s, ACT.Square, accum_out=stat[:, i:i + 1]).then_inc(S("rms_sq"), 1)
                a.wait_ge(S("rms_mean"), k + 1)
                act(rstd[:, 0:len(srcs)], stat[:, 0:len(srcs)], ACT.Sqrt).then_inc(S("rms_root"), 1)

            rms(0, [x[:, 0, :], x[:, 1, :], ctx[:, 0, :], ctx[:, 1, :]], junk0)
            rows_copy(3)
            a.wait_ge(S("mod"), 1)
            for k in range(0, KD, 2):
                a.wait_ge(S("ht_ps"), k + 1)
                b = ps[4 + k % 4]
                act(hT[:, k, 0:L], b[:, 0:L], ACT.Identity, scale=scale1[:, k, 0:1], bias=mod[:, k, 0:1])
                act(hT[:, k, L:2 * L], b[:, L:2 * L], ACT.Identity, scale=scale1[:, k, 1:2],
                    bias=mod[:, k, 1:2]).then_inc(S("ht_ev"), 1)

            def silu_item(i):
                n, _, _, dest = item(i)
                a.wait_ge(S("conv_v"), i + 1)
                if 7 <= i < 12:
                    a.wait_ge(S("tr_ps"), i - 6)
                act(dest, cconv[i % 2][:, 0:n], ACT.Silu).then_inc(S("item_silu"), 1)

            def k_rows(i):
                a.wait_ge(S("tr_ps"), 10 + i + 1)
                act(kN[:, :, i * P:(i + 1) * P], tiles(ps[6 + i % 2][:, :], 4), ACT.Copy).then_inc(S("kn_ev"), 1)

            rows_copy(4)
            for i in range(24):
                b = ps[4 + i % 2]
                if i in (4, 8, 12, 16, 20, 22):
                    rows_copy(4 + (4, 8, 12, 16, 20, 22).index(i) + 1)
                if i < 20:
                    n, taps, wb, _ = item(i)
                    if i >= 2:
                        a.wait_ge(S("item_silu"), i - 1)
                    a.wait_ge(S("item_ps"), i + 1)
                    act(cconv[i % 2][:, 0:n], b[:, 0:n], ACT.Identity, scale=col[:, taps[1]:taps[1] + 1],
                        bias=0.0 if wb is None else col[:, wb:wb + 1]).then_inc(S("conv_a"), 1)
                    if i >= 1:
                        silu_item(i - 1)
                    if i == 19:
                        silu_item(19)
                else:
                    j = i - 20
                    a.wait_ge(S("item_ps"), i + 1)
                    act(Z[:, j % 2, 512 * (j // 2):512 * (j // 2) + 512], b[:, :], ACT.Silu).then_inc(S("z_ev"), 1)
                    k_rows(j)
                if i in SQ_AT:
                    n = SQ_AT.index(i)
                    a.wait_ge(S("sq_ps"), n + 1)
                    if n >= 2:
                        a.wait_ge(S("kq_norm"), n - 1)
                    act(root[n % 2], ps[3][:, :], ACT.Sqrt, scale=1.0 if n < 4 else float(P),
                        bias=C("eps", 4)[:, 0:1] if n < 4 else C("eps", 4)[:, 1:2]).then_inc(S("kq_root"), 1)
                if i == 21:
                    a.wait_ge(S("exp_arg"), 1)
                    act(gtmp[:, :, :], gtmp[:, :, :], ACT.Exp).then_inc(S("exp_done"), 1)
                    a.wait_ge(S("exp_done"), 1)
                    act(beta[:, :, :], beta[:, :, :], ACT.Exp)
                    act(nega, R("alog", 24), ACT.Exp)
                    act(gtmp[:, :, :], gtmp[:, :, :], ACT.Ln, bias=C("eps", 4)[:, 2:3]).then_inc(S("exp_done"), 1)

            rows_copy(11)
            rows_copy(12)
            a.wait_ge(S("exp_arg"), 2)
            act(egc[:, :, :], gc[:, :, :], ACT.Exp)
            act(etot[:, :, :], etot[:, :, :], ACT.Exp)
            act(kd[:, :, :], kd[:, :, :], ACT.Exp).then_inc(S("exp_done"), 1)
            for u in range(4):
                for d in range(2):
                    a.wait_ge(S(f"e_arg{d}"), u + 1)
                    act(E[d], E[d], ACT.Exp).then_inc(S(f"e_exp{d}"), 1)
                for l in range(1, LEVELS):
                    for d in range(2):
                        a.wait_ge(S(f"p_ps{d}"), u * LEVELS + l + 1)
                        act(Pv[d], tiles(pA[d][:, :], 4), ACT.Copy).then_inc(S(f"p_ev{d}"), 1)
                        if l >= 2:
                            a.wait_ge(S(f"xt_ps{d}"), u * (LEVELS - 2) + l - 1)
                            act(XT[d], tiles(pC[d][:, :], 4), ACT.Copy).then_inc(S(f"xt_ev{d}"), 1)
                    for d, kind in pieces(u, l):
                        if kind == "c":
                            a.wait_ge(S("ws_arg"), 2 * (2 * (u - 2) + d + 1))
                            act(Ws[:, :, :], Ws[:, :, :], ACT.Exp).then_inc(S("ws_exp"), 1)
            for n in range(2):
                a.wait_ge(S("mean"), n + 1)
                act(rstd[:, 8 * n:8 * n + (8 if n == 0 else 2)], stat[:, 8 * n:8 * n + (8 if n == 0 else 2)],
                    ACT.Sqrt).then_inc(S("root"), 1)

            def columns(nth, dest, scale, bias=None):
                for k in range(KD):
                    a.wait_ge(S("cols_ps"), nth * KD + k + 1)
                    act(dest[:, k, :], ps[2 + k % 2][:, 0:L], ACT.Identity, scale=scale(k),
                        bias=0.0 if bias is None else bias(k)).then_inc(S("cols_ev"), 1)

            columns(0, mixT, lambda k: V("mixg", k))
            a.wait_ge(S("x_step"), 4)
            rms(1, [x[:, 0, :], x[:, 1, :]], junk)
            columns(1, hT2, lambda k: scale2[:, k:k + 1], lambda k: mod[:, 24 + k, 0:1])
            a.dma_start(fng1, ap["fng"].to_broadcast([P, D])).then_inc(S("in_rows"), 16)
            a.dma_start(fng2, ap["fng2"].to_broadcast([P, D])).then_inc(S("in_rows"), 16)
            a.dma_start(n2row, ap["n2row"].to_broadcast([P, D])).then_inc(S("in_rows"), 16)
            a.dma_start(bias, ap["bias"].rearrange("(t p) n -> p t n", p=P)).then_inc(S("in_rows"), 16)

            def ffn_silu(b):
                a.wait_ge(S("f_taps"), b + 1)
                if b >= 2:
                    a.wait_ge(S("f_hid"), b - 1)
                act(fs[b % 2], fa[b % 2], ACT.Silu).then_inc(S("f_silu"), 1)

            for b in range(KF):
                if b >= 2:
                    a.wait_ge(S("f_silu"), b - 1)
                a.wait_ge(S("gate_ps"), b + 1)
                act(fa[b % 2], ps[b % 2][:, 0:L], ACT.Identity, scale=V("fconv", 4 * KF + b),
                    bias=V("fconvb", b)).then_inc(S("f_mid"), 1)
                if b >= 1:
                    ffn_silu(b - 1)
            ffn_silu(KF - 1)
            a.wait_ge(S("x_step"), 8)
            rms(2, [x[:, 0, :], x[:, 1, :]], junk)
            a.wait_ge(S("x_step"), 9)
            rms(3, [x[:, 0, :], x[:, 1, :]], junk)
            columns(2, uT, lambda k: V("n1b", k))
            for i, (c0, n) in enumerate(IN2):
                for t in range(T):
                    j = 2 * i + t
                    a.wait_ge(S("in2_ps"), j + 1)
                    act(pj[:, t, c0:c0 + n], ps[4 + j % 4][:, 0:n], ACT.Copy).then_inc(S("in2_ev"), 1)
            a.wait_ge(S("mean"), 3)
            act(rstd[:, 0:20], stat[:, 0:20], ACT.Sqrt).then_inc(S("root"), 1)
            for i in range(13):
                a.wait_ge(S("qt_ps"), i + 1)
                act(qkT[0:HD, 2 * i:2 * i + 2, :], ps[i % 2][0:HD, :].rearrange("p (h t) -> p h t", h=2),
                    ACT.Copy).then_inc(S("qt_ev"), 1)

            def prob_rows(h):
                a.wait_ge(S("pt_ps"), h + 1)
                if h >= 2:
                    a.wait_ge(S("pv_ps"), h - 1)
                act(prT[h % 2], ps[2 + h % 2][:, :].rearrange("p (k t q) -> p k t q", k=2, t=2),
                    ACT.Copy).then_inc(S("pt_ev"), 1)

            for h in range(16):
                a.wait_ge(S("s_max"), h + 1)
                if h >= 2:
                    a.wait_ge(S("pt_ps"), h - 1)
                for t in range(T):
                    src = ps[h % 2][:, t * L:(t + 1) * L] if h < 8 else sc[h % 2][:, t, :]
                    act(pr[h % 2][:, t, :], src, ACT.Exp, scale=SCALE if h < 8 else 1.0,
                        bias=mx[:, h, t:t + 1], accum_out=sm[:, h, t:t + 1]).then_inc(S("s_exp"), 1)
                if h >= 1:
                    prob_rows(h - 1)
            prob_rows(15)
            a.wait_ge(S("pv_ps"), 16)
            for b in range(4):
                act(sqT[:, 512 * b:512 * b + 512], ps[4 + b][:, :], ACT.Square).then_inc(S("sqT"), 1)
            a.wait_ge(S("mean"), 4)
            act(tmpx[0], tmpx[0], ACT.Sqrt).then_inc(S("root"), 1)
            a.dma_start(rw, ap["rw"].rearrange("(k p) n -> p k n", p=P)).then_inc(S("in_rw"), 16)
            a.wait_ge(S("x_step"), 13)
            rms(4, [x[:, 0, :], x[:, 1, :]], junk)
            columns(3, u2T, lambda k: V("n2b", k))
            a.wait_ge(S("exp_arg"), 3)
            act(ra[0][:, :, 0:4], ra[0][:, :, 0:4], ACT.Exp)
            act(rs[:, 5, :], rs[:, 5, :], ACT.Exp).then_inc(S("exp_done"), 1)
            a.wait_ge(S("count_ready"), 1)
            npairs = a.value_load(units[0:1, NU:NU + 1], min_val=NPAIR, max_val=NU // 2)
            a.wait_ge(S("gather_ps"), 1)
            act(xsel[:, 0:4, :], tiles(ps[6][:, :], 4), ACT.Copy).then_inc(S("xsel_a"), 1)
            with a.Fori(0, npairs) as p:
                a.wait_ge(S("eg_ps"), p + 1)
                act(sg, ps[5][:, :], ACT.Silu).then_inc(S("sg"), 1)
                a.wait_ge(S("hidT_ps"), p + 1)
                act(hidT, tiles(ps[5][:, :], 4), ACT.Copy).then_inc(S("hidT_ev"), 1)
                a.wait_ge(S("gather_ps"), p + 2)
                act(xsel[:, 0:4, :], tiles(ps[6][:, :], 4), ACT.Copy).then_inc(S("xsel_a"), 1)
                a.wait_ge(S("yn_ps"), 2 * p + 1)
                act(yN[:, 0:512], ps[5][:, :], ACT.Copy).then_inc(S("yn_a"), 1)
            a.wait_ge(S("x_step"), 17)
            rms(5, [x[:, 0, :], x[:, 1, :]], junk)

        @block.vector
        def _(v):
            tt, ts, stt = nc.vector.tensor_tensor, nc.vector.tensor_scalar, nc.vector.scalar_tensor_tensor
            n = [0]

            def link(ins):
                n[0] += 1
                ins.then_inc(S("dve"), 1)
                v.wait_ge(S("dve"), n[0])

            def rms(k, width=2):
                v.wait_ge(S("rms_sq"), 4 + 2 * k)
                ts(stat[:, 0:width], stat[:, 0:width], 1.0 / D, EPS, MUL, ADD).then_inc(S("rms_mean"), 1)
                v.wait_ge(S("rms_root"), k + 1)
                link(nc.vector.reciprocal(rstd[:, 0:width], rstd[:, 0:width]))

            nc.vector.memset(csil, 0.0).then_inc(S("v_early"), 1)
            rms(0, 4)
            for t in range(4):
                ts(xn[:, t, :], x[:, t, :] if t < 2 else ctx[:, t - 2, :], rstd[:, t:t + 1], None,
                   MUL).then_inc(S("xh"), 1)
            v.wait_ge(S("one_ps"), 1)
            link(nc.vector.tensor_copy(col, ps[0][:, 0:NROWS]))
            v.wait_ge(S("fold_ps"), 4)
            link(tt(mod[:, 0:16, :], ps[1][:, 0:32].rearrange("p (j c) -> p j c", c=2),
                    wide(V("b_ada", 0, 16), 2), ADD))
            link(ts(scale1[:, :, :], mod[:, 8:16, :], 1.0, None, ADD))
            tt(scale1[:, :, :], scale1[:, :, :], wide(V("norm1", 0, 8), 2), MUL).then_inc(S("mod"), 1)
            v.wait_ge(S("mod"), 1)
            for k in range(1, KD, 2):
                v.wait_ge(S("ht_ps"), k + 1)
                for c in range(2):
                    ins = ts(hT[:, k, c * L:(c + 1) * L], ps[4 + k % 4][:, c * L:(c + 1) * L],
                             scale1[:, k, c:c + 1], mod[:, k, c:c + 1], MUL, ADD)
                ins.then_inc(S("ht_v"), 1)

            def rows_out(r):
                v.wait_ge(S("tr_ps"), r + 1)
                dest = vN[:, :, r * P:(r + 1) * P] if r < 4 else xsN[:, :, (r - 4) * P:(r - 3) * P] if r < 8 \
                    else BN[:, :, (r - 8) * P:(r - 7) * P]
                nc.vector.tensor_copy(dest, tiles(ps[6 + r % 2][:, :], 4)).then_inc(S("tr_ev"), 1)

            def kq_unit(n):
                v.wait_ge(S("kq_root"), n + 1)
                link(nc.vector.reciprocal(root[n % 2], root[n % 2]))
                tt(kq_block(n), kq_block(n), root[n % 2], MUL).then_inc(S("kq_norm"), 1)

            for i in range(20):
                w, taps, _, _ = item(i)
                segs = w // L
                v.wait_ge(S("conv_a"), i + 1)
                b = ps[4 + i % 2][:, 0:w].rearrange("p (s t) -> p s t", s=segs)
                o_ = cconv[i % 2][:, 0:w].rearrange("p (s t) -> p s t", s=segs)
                link(stt(o_[:, :, 1:L], b[:, :, 0:L - 1], col[:, taps[0]:taps[0] + 1], o_[:, :, 1:L], MUL, ADD))
                stt(o_[:, :, 0:L - 1], b[:, :, 1:L], col[:, taps[2]:taps[2] + 1], o_[:, :, 0:L - 1], MUL,
                    ADD).then_inc(S("conv_v"), 1)
                if 7 <= i < 17:
                    rows_out(i - 7)
                if i == 5:
                    v.wait_ge(S("fold_ps"), 5)
                    nc.vector.tensor_copy(gx, ps[1][:, 128:256].rearrange("p (t n) -> p t n", t=4)) \
                        .then_inc(S("v_early"), 1)
                if i in SQ_AT:
                    kq_unit(SQ_AT.index(i))
            v.wait_ge(S("v_early"), 2)
            v.wait_ge(S("in_rest"), 32)
            link(tt(gx[:, :, 0:24], gx[:, :, 0:24], each(R("dtb", 24), 4), ADD))
            link(ts(gtmp[:, :, :], gx[:, :, 0:24], -1.0, None, MUL))
            link(tt(gtmp[:, :, :], gtmp[:, :, :], gx[:, :, 0:24], ALU.min))
            ts(beta[:, :, :], gx[:, :, 24:32], -1.0, None, MUL).then_inc(S("exp_arg"), 1)
            kq_unit(4)
            kq_unit(5)
            v.wait_ge(S("exp_done"), 2)
            link(ts(gx[:, :, 0:24], gx[:, :, 0:24], 0.0, None, ALU.max))
            link(tt(dtv[:, :, :], gx[:, :, 0:24], gtmp[:, :, :], ADD))
            link(ts(nega, nega, -1.0, None, MUL))
            tt(G[:, :, :], dtv[:, :, :], each(nega, 4), MUL).then_inc(S("v_early"), 1)
            link(ts(beta[:, :, :], beta[:, :, :], 1.0, None, ADD))
            link(nc.vector.reciprocal(beta[:, :, :], beta[:, :, :]))
            link(ts(nbeta[:, :, :], beta[:, :, :], -1.0, None, MUL))
            v.wait_ge(S("one_ps"), 2)
            link(nc.vector.tensor_copy(gc[:, :, :], tiles(ps[2][:, 0:96], 4)))
            link(nc.vector.tensor_copy(etot[:, :, :], tiles(ps[2][:, 128:224], 4)))
            tt(kd[:, :, :], etot[:, :, :], gc[:, :, :], SUB).then_inc(S("exp_arg"), 1)
            v.wait_ge(S("exp_done"), 3)
            link(tt(dtkd[:, :, :], dtv[:, :, :], kd[:, :, :], MUL))
            v.wait_ge(S("one_ps"), 3)
            nc.vector.tensor_copy(CBs, pD[0][:, :].rearrange("p (t g i) -> p t g i", t=T, g=2)) \
                .then_inc(S("gates"), 1)
            v.wait_ge(S("fold_ps"), 13)
            link(tt(mod[:, 16:48, :], ps[1][:, 32:96].rearrange("p (j c) -> p j c", c=2),
                    wide(V("b_ada", 16, 32), 2), ADD))
            link(ts(scale2, mod[:, 32:40, 0], 1.0, None, ADD))
            tt(scale2, scale2, V("norm2", 0, 8), MUL).then_inc(S("mod"), 1)
            v.wait_ge(S("gates"), 1)
            v.wait_ge(S("state0"), 1)

            def piece(u, d, kind):
                t, c = tile_of(u, d), 12 * d + 4
                if kind in "ab":
                    k = 0 if kind == "a" else 4
                    m = 2 * (2 * (u - 2) + d) + (1 if kind == "b" else 0)
                    v.wait_ge(S("wg_ps"), m + 1)
                    for h in range(4):
                        ins = ts(Ws[:, k + h, :], pD[d][:, h * P:(h + 1) * P], gc[:, t, c + k + h:c + k + h + 1], 0.0,
                                 SUB, ALU.min)
                    ins.then_inc(S("ws_arg"), 1)
                elif kind == "e":
                    m = 2 * u + d
                    if u >= 2:
                        v.wait_ge(S("yo_ps"), 2 * (u - 2) + d + 1)
                        tt(heads(yoff, 8, SP_), heads(pD[d][:, :], 8, SP_), wide(egc[:, t, c:c + 8], SP_), MUL) \
                            .then_inc(S("yo_rd"), 1)
                        v.wait_ge(S("yo_rd"), 2 * (u - 2) + d + 1)
                        if first(u, d):
                            link(tt(heads(yacc[:, t, :], 8, SP_), heads(xsN[:, t, :], 8, SP_),
                                    wide(R("ssmD", 8), SP_), MUL))
                        link(tt(yacc[:, t, :], yacc[:, t, :], yoff, ADD))
                    link(tt(heads(ht[:, d, :], 8, SP_), heads(ht[:, d, :], 8, SP_), wide(etot[:, t, c:c + 8], SP_),
                            MUL))
                    v.wait_ge(S("hs_ps"), m + 1)
                    tt(ht[:, d, :], ht[:, d, :], pD[d][:, :], ADD).then_inc(S("h_ready"), 1)
                else:
                    m = 2 * (u - 2) + d
                    v.wait_ge(S("ws_mask"), m + 1)
                    for k in range(2):
                        ins = tt(Ws[:, 4 * k:4 * k + 4, :], Ws[:, 4 * k:4 * k + 4, :], each(CBs[:, t, k, :], 4), MUL)
                    ins.then_inc(S("ws_ready"), 1)
                    v.wait_ge(S("yd_ps"), m + 1)
                    tt(yacc[:, t, :], yacc[:, t, :], pD[d][:, :], ADD).then_inc(S("yd_rd"), 1)
                    v.wait_ge(S("yd_rd"), m + 1)

            def first(u, d):
                return u == 2

            for u in range(4):
                for d in range(2):
                    t = tile_of(u, d)
                    v.wait_ge(S(f"pre{d}"), u + 1)
                    for h in range(4):
                        ins = ts(E[d][:, h, :], pB[d][:, h * P:(h + 1) * P], gc[:, t, 12 * d + h:12 * d + h + 1], 0.0,
                                 SUB, ALU.min)
                    ins.then_inc(S(f"e_arg{d}"), 1)
                for d in range(2):
                    t = tile_of(u, d)
                    v.wait_ge(S(f"e_exp{d}"), u + 1)
                    if u:
                        v.wait_ge(S(f"s_ps{d}"), u)
                    if u >= 2:
                        if u == 3:
                            v.wait_ge(S(f"o_ps{d}"), 1)
                        tt(PT[d], tiles(pC[d][:, :], 4), E[d], MUL)
                    for h in range(4):
                        ins = stt(NT[d][:, h, :], pA[d][:, h * P:(h + 1) * P], nbeta[:, t, 4 * d + h:4 * d + h + 1],
                                  E[d][:, h, :], MUL, MUL)
                    ins.then_inc(S(f"nt{d}"), 1)
                for d in range(2):
                    v.wait_ge(S(f"mn{d}"), u * LEVELS + 1)
                    v.wait_ge(S(f"p_ps{d}"), u * LEVELS + 1)
                    tt(X[d], tiles(pA[d][:, :], 4), each(ident, 4), ADD)
                    tt(XT[d], Mn[d][0], each(ident, 4), ADD).then_inc(S(f"x{d}"), 1)
                for l in range(1, LEVELS):
                    for d, kind in pieces(u, l):
                        piece(u, d, kind)
                    for d in range(2):
                        v.wait_ge(S(f"x{d}"), u * LEVELS + l)
                        v.wait_ge(S(f"q_ps{d}"), u * (LEVELS - 1) + l)
                        if l < LEVELS - 1:
                            tt(X[d], X[d], tiles(pB[d][:, :], 4), ADD).then_inc(S(f"x{d}"), 1)
                        else:
                            tt(XT[d], XT[d], tiles(pC[d][:, :], 4), ADD).then_inc(S(f"x{d}"), 1)
                for d in range(2):
                    t = tile_of(u, d)
                    v.wait_ge(S(f"ks_ps{d}"), u + 1)
                    link(tt(E[d], tiles(pA[d][:, :], 4), wide(egc[:, t, 12 * d:12 * d + 4], P), MUL))
                    v.wait_ge(S(f"mn{d}"), u * LEVELS + LEVELS)
                    tt(Mn[d][1], heads(vN[:, t, :], 4, P), E[d], SUB).then_inc(S(f"r{d}"), 1)
                for d in range(2):
                    t = tile_of(u, d)
                    v.wait_ge(S(f"vn_ps{d}"), u + 1)
                    tt(vnew[d], tiles(pB[d][:, :], 4), wide(beta[:, t, 4 * d:4 * d + 4], P), MUL) \
                        .then_inc(S(f"vnew{d}"), 1)
                for d in range(2):
                    t = tile_of(u, d)
                    v.wait_ge(S(f"ks_ps{d}"), u + 1)
                    if u >= 2:
                        v.wait_ge(S(f"o_ps{d}"), u - 1)
                        link(tt(E[d], tiles(pC[d][:, :], 4), wide(egc[:, t, 12 * d:12 * d + 4], P), MUL))
                        o4 = heads(oacc[:, t, :], 4, P)
                        if first(u, d):
                            link(tt(o4, E[d], tiles(pA[d][:, :], 4), ADD))
                        else:
                            link(tt(E[d], E[d], tiles(pA[d][:, :], 4), ADD))
                            link(tt(o4, o4, E[d], ADD))
                    if u < 3:
                        link(tt(St[:, d, :, :], St[:, d, :, :], wide(etot[:, t, 12 * d:12 * d + 4], P), MUL))
                        v.wait_ge(S(f"s_ps{d}"), u + 1)
                        tt(St[:, d, :, :], St[:, d, :, :], tiles(pB[d][:, :], 4), ADD).then_inc(S(f"s{d}"), 1)
            sq = tiles(scratch(0, 1024), 2)
            v.wait_ge(S("o_ps0"), 2)
            v.wait_ge(S("o_ps1"), 2)
            for t in range(T):
                link(tt(sq[:, t, :], oacc[:, t, :], oacc[:, t, :], MUL))
            link(nc.vector.tensor_reduce(stat[:, 0:8], sq.rearrange("p t (h e) -> p (t h) e", h=4), AX, ADD))
            ts(stat[:, 0:8], stat[:, 0:8], 1.0 / P, EPS, MUL, ADD).then_inc(S("mean"), 1)
            for t in range(T):
                link(tt(yacc[:, t, :], yacc[:, t, :], Z[:, t, 512:1024], MUL))
                link(tt(sq[:, t, :], yacc[:, t, :], yacc[:, t, :], MUL))
            link(nc.vector.tensor_reduce(stat[:, 8:10], sq, AX, ADD))
            ts(stat[:, 8:10], stat[:, 8:10], 1.0 / 512, EPS, MUL, ADD).then_inc(S("mean"), 1)
            v.wait_ge(S("root"), 2)
            link(nc.vector.reciprocal(rstd[:, 0:10], rstd[:, 0:10]))
            for t in range(T):
                link(tt(heads(oacc[:, t, :], 4, P), heads(oacc[:, t, :], 4, P), wide(rstd[:, 4 * t:4 * t + 4], P), MUL))
                tt(oacc[:, t, :], oacc[:, t, :], Z[:, t, 0:512], MUL).then_inc(S("normed"), 1)
                ts(yacc[:, t, :], yacc[:, t, :], rstd[:, 8 + t:9 + t], None, MUL).then_inc(S("normed"), 1)
            for i in range(16):
                if i >= 2:
                    v.wait_ge(S("dg_ps"), i - 1)
                ts(dg[i % 2], ident, mod[:, (16 if i < 8 else 32) + i, 0:1], None, MUL).then_inc(S("dg"), 1)
            for i in range(4):
                v.wait_ge(S("dg_ps"), 4 * i + 4)
                nc.vector.tensor_copy((g1r if i < 2 else g2r)[:, 512 * (i % 2):512 * (i % 2) + 512],
                                      ps[4 + i][:, :]).then_inc(S("gain_rows"), 1)
            v.wait_ge(S("gain_rows"), 4)

            def residual(name, order, gain, done):
                for i, (bank, t, c) in enumerate(order):
                    v.wait_ge(S(name), (i + 1) if done else 6)
                    xs = x[:, t, 512 * c:512 * c + 512]
                    if gain is None:
                        tt(xs, xs, ps[bank][:, :], ADD).then_inc(S("x_step"), 1)
                    else:
                        link(tt(tmpx[i % 2], ps[bank][:, :], gain[:, 512 * c:512 * c + 512], MUL))
                        tt(xs, xs, tmpx[i % 2], ADD).then_inc(S("x_step"), 1)

            residual("wo_ps", [(4 + 2 * c + t, t, c) for c in range(2) for t in range(2)], g1r, True)
            rms(1)
            for t in range(T):
                ts(xh[:, t, :], x[:, t, :], rstd[:, t:t + 1], None, MUL).then_inc(S("xh"), 1)

            def ffn_hid(b):
                v.wait_ge(S("f_silu"), b + 1)
                v.wait_ge(S("up_ps"), b + 1)
                tt(hid[:, b, :], fs[b % 2], ps[2 + b % 2][:, 0:L], MUL).then_inc(S("f_hid"), 1)

            for b in range(KF):
                v.wait_ge(S("f_mid"), b + 1)
                src = ps[b % 2][:, 0:L].rearrange("p (r c) -> p r c", c=GRID)
                dst = fa[b % 2].rearrange("p (r c) -> p r c", c=GRID)
                nr = L // GRID
                for j in range(9):
                    if j == 4:
                        continue
                    dy, dx = j // 3 - 1, j % 3 - 1
                    r0, r1, c0, c1 = max(0, -dy), nr - max(0, dy), max(0, -dx), GRID - max(0, dx)
                    o_ = dst[:, r0:r1, c0:c1]
                    ins = stt(o_, src[:, r0 + dy:r1 + dy, c0 + dx:c1 + dx], V("fconv", j * KF + b), o_, MUL, ADD)
                    if j < 8:
                        link(ins)
                    else:
                        ins.then_inc(S("f_taps"), 1)
                if b >= 1:
                    ffn_hid(b - 1)
            ffn_hid(KF - 1)
            residual("down_ps", [(4 + 2 * t + c, t, c) for t in range(2) for c in range(2)], g2r, False)
            rms(2)
            v.wait_ge(S("x_step"), 8)
            v.wait_ge(S("in_rows"), 64)
            for t in range(T):
                link(ts(x[:, t, :], x[:, t, :], rstd[:, t:t + 1], None, MUL))
            link(tt(x[:, 0, :], x[:, 0, :], fng1, MUL))
            tt(x[:, 1, :], x[:, 1, :], fng1, MUL).then_inc(S("x_step"), 1)
            rms(3)
            v.wait_ge(S("x_step"), 9)
            for t in range(T):
                ts(xh[:, t, :], x[:, t, :], rstd[:, t:t + 1], None, MUL).then_inc(S("xh"), 1)
            v.wait_ge(S("in2_ev"), 4)
            for t in range(T):
                link(tt(rota[:, t, :], pj[:, t, 0:640], pj[:, t, 0:640], MUL))
                link(nc.vector.tensor_reduce(stat[:, 10 * t:10 * t + 10], heads(rota[:, t, :], 10, HD), AX, ADD))
            ts(stat[:, 0:20], stat[:, 0:20], 1.0 / HD, EPS, MUL, ADD).then_inc(S("mean"), 1)
            v.wait_ge(S("root"), 3)
            link(nc.vector.reciprocal(rstd[:, 0:20], rstd[:, 0:20]))
            for t in range(T):
                qa, ka = heads(pj[:, t, 0:512], 8, HD), heads(pj[:, t, 512:640], 2, HD)
                all_ = pj[:, t, 0:640]
                link(tt(heads(all_, 10, HD), heads(all_, 10, HD), wide(rstd[:, 10 * t:10 * t + 10], HD), MUL))
                link(tt(qa, qa, each(R("qn", HD), 8), MUL))
                link(tt(ka, ka, each(R("kn", HD), 2), MUL))
                s4 = all_.rearrange("p (h a e) -> p h a e", h=10, a=2)
                r4 = rota[:, t, :].rearrange("p (h a e) -> p h a e", h=10, a=2)
                cos, sin = rope(0, t)
                for a in range(2):
                    link(tt(r4[:, :, a, :], s4[:, :, 1 - a, :], each(sin[:, 32 * a:32 * a + 32], 10), MUL))
                link(tt(heads(all_, 10, HD), heads(all_, 10, HD), each(cos, 10), MUL))
                tt(all_, all_, rota[:, t, :], ADD).then_inc(S("rot_a"), 1)
            v.wait_ge(S("in_rows"), 64)
            def over_sum(h):
                v.wait_ge(S("s_exp"), 2 * h + 2)
                link(nc.vector.reciprocal(sm[:, h, :], sm[:, h, :]))
                for t in range(T):
                    ins = ts(pr[h % 2][:, t, :], pr[h % 2][:, t, :], sm[:, h, t:t + 1], None, MUL)
                ins.then_inc(S("pr"), 1)

            for h in range(16):
                v.wait_ge(S("s_ps"), h + 1)
                if h < 8:
                    link(nc.vector.tensor_reduce(mx[:, h, :], tiles(ps[h % 2][:, :], 2), AX, ALU.max, negate=True))
                    ts(mx[:, h, :], mx[:, h, :], SCALE, None, MUL).then_inc(S("s_max"), 1)
                else:
                    v.wait_ge(S("s_exp"), 2 * h - 2)
                    link(stt(sc[h % 2], tiles(ps[h % 2][:, :], 2), SCALE, bias, MUL, ADD))
                    nc.vector.tensor_reduce(mx[:, h, :], sc[h % 2], AX, ALU.max, negate=True) \
                        .then_inc(S("s_max"), 1)
                if h >= 1:
                    over_sum(h - 1)
            over_sum(15)
            v.wait_ge(S("ss_ps"), 1)
            ts(tmpx[0], ps[0][:, :], 1.0 / 512, EPS, MUL, ADD).then_inc(S("mean"), 1)
            v.wait_ge(S("root"), 4)
            link(nc.vector.reciprocal(tmpx[0], tmpx[0]))
            for k in range(KD):
                stt(uT[:, k, :], ps[4 + k // 2][:, L * (k % 2):L * (k % 2) + L], V("outab", k),
                    tmpx[0][:, L * (k // 4):L * (k // 4) + L], MUL, MUL).then_inc(S("o_norm"), 1)
            residual("wo2_ps", [(4 + 2 * c + t, t, c) for c in range(2) for t in range(2)], None, True)
            rms(4)
            v.wait_ge(S("x_step"), 13)
            for t in range(T):
                ts(xh[:, t, :], x[:, t, :], rstd[:, t:t + 1], None, MUL).then_inc(S("xh"), 1)
            v.wait_ge(S("xh"), 10)
            v.wait_ge(S("in_rows"), 64)
            for t in range(T):
                tt(u2[:, t, :], xh[:, t, :], n2row, MUL).then_inc(S("u2"), 1)
            desc = C("desc", NE)

            def one_hot(dst, src, top, w):
                e1 = ra[4][:, :, 0:w]
                link(nc.vector.tensor_reduce(top, src, AX, ALU.max))
                link(tt(e1, src, wide(top, w), ALU.is_equal))
                link(tt(e1, e1, each2(desc[:, 0:w]), MUL))
                link(nc.vector.tensor_reduce(rs[:, 7, :], e1, AX, ALU.max))
                link(tt(dst, e1, wide(rs[:, 7, :], w), ALU.is_equal))

            def each2(row):
                return row.unsqueeze(1).to_broadcast([P, 2, row.shape[1]])

            v.wait_ge(S("one_ps"), 4)
            link(tt(lg[:, :, :], tiles(ps[0][:, 0:72], 2), each2(R("rb", 36)), ADD))
            gm, el, oh1, oh2 = ra[1][:, :, 0:4], ra[2], ra[3], ra[5]
            one_hot(gm, lg[:, :, 0:4], rs[:, 0, :], 4)
            link(tt(ra[0][:, :, 0:4], lg[:, :, 0:4], wide(rs[:, 0, :], 4), SUB))
            for t in range(T):
                link(tt(heads(el[:, t, :], 4, 8), heads(lg[:, t, 4:36], 4, 8), wide(gm[:, t, :], 8), MUL))
            link(ts(gm, gm, -1.0, 1e30, ADD, MUL))
            for t in range(T):
                link(tt(heads(el[:, t, :], 4, 8), heads(el[:, t, :], 4, 8), wide(gm[:, t, :], 8), ADD))
            one_hot(oh1, el, rs[:, 1, :], NE)
            link(stt(el.rearrange("p t n -> p (t n)"), oh1.rearrange("p t n -> p (t n)"), -3e38,
                     el.rearrange("p t n -> p (t n)"), MUL, ADD))
            one_hot(oh2, el, rs[:, 2, :], NE)
            tt(rs[:, 5, :], rs[:, 2, :], rs[:, 1, :], SUB).then_inc(S("exp_arg"), 1)
            v.wait_ge(S("exp_done"), 4)
            link(nc.vector.tensor_reduce(rs[:, 3, :], ra[0][:, :, 0:4], AX, ADD))
            link(ts(rs[:, 4, :], rs[:, 5, :], 1.0, None, ADD))
            link(tt(rs[:, 3, :], rs[:, 3, :], rs[:, 4, :], MUL))
            link(nc.vector.reciprocal(rs[:, 3, :], rs[:, 3, :]))
            link(tt(rs[:, 4, :], rs[:, 3, :], rs[:, 5, :], MUL))
            flag = ra[4]
            tt(flag, oh1, oh2, ADD).then_inc(S("flag"), 1)
            link(nc.vector.memset(SL[:, :, :], -1.0))
            link(nc.vector.memset(GT[:, :, :], 0.0))
            link(tt(oh1, oh1, wide(rs[:, 3, :], NE), MUL))
            link(tt(oh2, oh2, wide(rs[:, 4, :], NE), MUL))
            v.wait_ge(S("flag"), 1)
            v.wait_ge(S("one_ps"), 5)
            link(ts(el, tiles(ps[1][:, 0:64], 2), 1.0, None, ADD))
            link(tt(el, el, flag, MUL))
            link(tt(oh1, oh1, oh2, ADD))
            link(ts(SL[:, :, 0:NE], el, -1.0, None, ADD))
            link(nc.vector.tensor_copy(GT[:, :, 0:NE], oh1))
            iota = C("iota", SLOT)
            link(nc.vector.tensor_copy(cnt[:, 0:32], ps[1][:, 64:96]))
            for r in range(3):
                link(ts(over[:, NE * r:NE * r + NE], cnt[:, 0:32], float(SLOT * (r + 1)), None, ALU.is_gt))
            link(nc.vector.tensor_reduce(cnt[:, 32:33], over, AX, ADD))
            a_, b_ = over, scanA
            for i in range(7):
                w = 2 ** i
                link(nc.vector.tensor_copy(b_[:, 0:w], a_[:, 0:w]))
                link(tt(b_[:, w:96], a_[:, w:96], a_[:, 0:96 - w], ADD))
                a_, b_ = b_, scanB if b_ is scanA else scanA
            link(ts(a_, a_, float(NE - 1), None, ADD))
            link(tt(a_, a_, over, MUL))
            p3 = place.rearrange("p (u n) -> p u n", u=EXTRA)
            link(tt(p3, each(a_, EXTRA), wide(iota[:, NE:NU], 96), ALU.is_equal))
            p4 = place.rearrange("p (u b e) -> p u b e", u=EXTRA, b=3)
            link(tt(ofexp, p4[:, :, 0, :], p4[:, :, 1, :], ADD))
            link(tt(ofexp, ofexp, p4[:, :, 2, :], ADD))
            link(nc.vector.tensor_reduce(blk.rearrange("p u b -> p (u b)"),
                                         place.rearrange("p (n e) -> p n e", e=NE), AX, ADD))
            link(ts(unitB, blk[:, :, 0], float(SLOT), None, MUL))
            link(stt(unitB, blk[:, :, 1], 2.0 * SLOT, unitB, MUL, ADD))
            link(stt(unitB, blk[:, :, 2], 3.0 * SLOT, unitB, MUL, ADD))
            link(tt(pick, ofexp, each(iota[:, 0:NE], EXTRA), MUL))
            link(nc.vector.tensor_reduce(unitE, pick, AX, ADD))
            for t in range(T):
                link(tt(pick, ofexp, each(el[:, t, :], EXTRA), MUL))
                link(nc.vector.tensor_reduce(SL[:, t, NE:NU], pick, AX, ADD))
                link(ts(SL[:, t, NE:NU], SL[:, t, NE:NU], -1.0, None, ADD))
                link(tt(SL[:, t, NE:NU], SL[:, t, NE:NU], unitB, SUB))
                link(tt(pick, ofexp, each(oh1[:, t, :], EXTRA), MUL))
                link(nc.vector.tensor_reduce(GT[:, t, NE:NU], pick, AX, ADD))
            link(nc.vector.tensor_copy(units[:, 0:NE], iota[:, 0:NE]))
            link(nc.vector.tensor_copy(units[:, NE:NU], unitE))
            for r in range(4):
                link(ts(cnt[:, 33 + r:34 + r], cnt[:, 32:33], float(2 * r), None, ALU.is_gt))
            link(nc.vector.tensor_reduce(cnt[:, 37:38], cnt[:, 33:37], AX, ADD))
            nc.vector.memset(yN[:, 0:512], 0.0).then_inc(S("yn_a"), 1)
            nc.vector.memset(yN[:, 512:1024], 0.0).then_inc(S("yn_v"), 1)
            nc.vector.memset(gselT, 0.0).then_inc(S("gt_ev"), 1)
            ts(units[:, NU:NU + 1], cnt[:, 37:38], float(NPAIR), None, ADD).then_inc(S("count_ready"), 1)

            def selection(chain, at, with_gate, name):
                chain(nc.vector.tensor_copy(cur[:, 0, :, :], SL[:, :, bass.ds(at, 2)]))
                if with_gate:
                    chain(nc.vector.tensor_copy(cur[:, 1, :, :], GT[:, :, bass.ds(at, 2)]))
                for t in range(T):
                    for e in range(2):
                        if with_gate:
                            ins = ts(gsel[:, t, e * SLOT:(e + 1) * SLOT], iota, cur[:, 0, t, e:e + 1],
                                     cur[:, 1, t, e:e + 1], ALU.is_equal, MUL)
                        else:
                            ins = ts(sel[:, t, e * SLOT:(e + 1) * SLOT], iota, cur[:, 0, t, e:e + 1], None,
                                     ALU.is_equal)
                ins.then_inc(S(name), 1)

            v.wait_ge(S("count_ready"), 1)
            npairs = v.value_load(units[0:1, NU:NU + 1], min_val=NPAIR, max_val=NU // 2)
            selection(link, 0, False, "sel")
            v.wait_ge(S("gather_ps"), 1)
            nc.vector.tensor_copy(xsel[:, 4:8, :], tiles(ps[7][:, :], 4)).then_inc(S("xsel_v"), 1)
            LINKS = 3
            with v.Fori(0, npairs) as p:
                m = [0]

                def chain(ins):
                    m[0] += 1
                    ins.then_inc(S("dve_loop"), 1)
                    v.wait_ge(S("dve_loop"), p * LINKS + m[0])

                v.wait_ge(S("sel"), p + 1)
                selection(chain, 2 * p, True, "gsel")
                v.wait_ge(S("gsel"), p + 1)
                selection(chain, 2 * p + 2, False, "sel")
                v.wait_ge(S("sg"), p + 1)
                v.wait_ge(S("eu_ps"), p + 1)
                tt(hidN, sg, ps[4][:, :], MUL).then_inc(S("hid"), 1)
                v.wait_ge(S("gather_ps"), p + 2)
                nc.vector.tensor_copy(xsel[:, 4:8, :], tiles(ps[7][:, :], 4)).then_inc(S("xsel_v"), 1)
                v.wait_ge(S("yn_ps"), 2 * p + 2)
                nc.vector.tensor_copy(yN[:, 512:1024], ps[4][:, :]).then_inc(S("yn_v"), 1)
                v.wait_ge(S("gt_ps"), p + 1)
                nc.vector.tensor_copy(gselT, ps[6][:, 0:256]).then_inc(S("gt_ev"), 1)
                assert m[0] == LINKS
            v.wait_ge(S("sc_ps"), 1)
            for t in range(T):
                for c in range(2):
                    xs = x[:, t, 512 * c:512 * c + 512]
                    tt(xs, xs, ps[2 * t + c][:, :], ADD).then_inc(S("x_step"), 1)
            rms(5)
            v.wait_ge(S("x_step"), 17)
            for t in range(T):
                link(ts(x[:, t, :], x[:, t, :], rstd[:, t:t + 1], None, MUL))
            link(tt(x[:, 0, :], x[:, 0, :], fng2, MUL))
            tt(x[:, 1, :], x[:, 1, :], fng2, MUL).then_inc(S("out_ready"), 1)

        @block.tensor
        def _(pe):
            mm, tr = nc.tensor.matmul, nc.tensor.transpose
            def rows(j, left, right):
                if j >= 2:
                    pe.wait_ge(S("rows_ev"), j - 1)
                for m in range(2):
                    for g in range(4):
                        ins = mm(ps[2 * (j % 2)][32 * g:32 * g + 32, :], left(2 * g + m), right(2 * g + m),
                                 start=(m == 0), stop=(m == 1), tile_position=(0, 32 * g))
                ins.then_inc(S("rows_ps"), 1)

            def fold(j, at, n):
                pe.wait_ge(S("rows_ev"), j + 1)
                for b in range(4):
                    ins = mm(ps[1][:, at + b * n:at + (b + 1) * n], arow[j % 2][:, b * P:(b + 1) * P],
                             C("fold", 32)[:, 0:n], start=True, stop=True)
                ins.then_inc(S("fold_ps"), 1)

            def ada(i):
                w = arrived(pe, ada_ch[i])
                j = i if i < 4 else i + 1
                rows(j, lambda k: csil[:, k, :], lambda k: w[:, k, :])
                if i == 5:
                    pe.wait_ge(S("v_early"), 2)
                if i not in (0, 4):
                    ada_fold(i - 1)

            def ada_fold(i):
                fold(i if i < 4 else i + 1, 8 * i, 2)

            def h_block(k):
                if k >= 4:
                    ht_read(k - 4)
                for t in range(4):
                    ins = tr(ps[4 + k % 4][:, t * P:(t + 1) * P], xn[:, t, k * P:(k + 1) * P], ident)
                ins.then_inc(S("ht_ps"), 1)

            def ht_read(k):
                pe.wait_ge(S("ht_v" if k % 2 else "ht_ev"), k // 2 + 1)

            pe.wait_ge(S("c_silu"), 1)
            ada(0)
            pe.wait_ge(S("in_consts"), 16)
            ada(1)
            ada(2)
            pe.wait_ge(S("xh"), 4)
            for k in range(4):
                h_block(k)
            ada(3)
            pe.wait_ge(S("in_vecs"), 16)
            pe.wait_ge(S("rows_ev"), 3)
            for i in range(3):
                ins = tr(ps[0][:, i * P:(i + 1) * P], vecs[:, i * P:(i + 1) * P], ident)
            ins.then_inc(S("one_ps"), 1)
            ada_fold(3)
            for k in range(4, KD):
                h_block(k)
            for k in range(KD - 2, KD):
                ht_read(k)
            pe.wait_ge(S("in_rest"), 32)
            rows(4, lambda k: wsm[:, k, :], lambda k: hT[:, k, :])

            def rows_in(i):
                r = i - 4
                pe.wait_ge(S("item_silu"), i + 1)
                if r >= 2:
                    pe.wait_ge(S("tr_ev"), r - 1)
                src = item(i)[3]
                for t in range(4):
                    ins = tr(ps[6 + r % 2][:, t * P:(t + 1) * P], src[:, t * P:(t + 1) * P], ident)
                ins.then_inc(S("tr_ps"), 1)

            for i in range(24):
                if i in (0, 4, 8, 12, 16, 20, 22):
                    c = PEND.index(min(e for e in PEND if e > i))
                    if i:
                        ada(3 + c)
                    if i == 4:
                        fold(4, 128, 32)
                    w = arrived(pe, proj_ch[c])
                    first_item = i
                if 2 <= i < 22:
                    pe.wait_ge(S("conv_v"), i - 1)
                elif i >= 22:
                    pe.wait_ge(S("z_ev"), i - 21)
                if i < 20:
                    n = item(i)[0]
                    j = i - first_item
                    if PROJ[c] == WBC:
                        j = i - 12
                    for k in range(KD):
                        ins = mm(ps[4 + i % 2][:, 0:n], w[:, k, j * P:(j + 1) * P], hT[:, k, 0:n],
                                 start=(k == 0), stop=(k == KD - 1))
                else:
                    t = i % 2
                    for k in range(KD):
                        ins = mm(ps[4 + i % 2][:, :], hT[:, k, t * P:(t + 1) * P], w[:, k, :],
                                 start=(k == 0), stop=(k == KD - 1))
                ins.then_inc(S("item_ps"), 1)
                if 6 <= i < 16:
                    rows_in(i - 2)
                if i in SQ_AT:
                    n = SQ_AT.index(i)
                    pe.wait_ge(S("sq_ready"), n + 1)
                    if n >= 1:
                        pe.wait_ge(S("kq_root"), n)
                    mm(ps[3][:, :], ones, sqb[n % 2], start=True, stop=True).then_inc(S("sq_ps"), 1)
                if i >= 20:
                    r = i - 20
                    pe.wait_ge(S("kq_norm"), r + 1)
                    if r < 2:
                        pe.wait_ge(S("tr_ev"), 9 + r)
                    else:
                        pe.wait_ge(S("kn_ev"), r - 1)
                    for t in range(4):
                        ins = tr(ps[6 + r % 2][:, t * P:(t + 1) * P], kT[:, r, t * P:(t + 1) * P], ident)
                    ins.then_inc(S("tr_ps"), 1)
            ada(10)
            ada(11)
            ada_fold(11)
            pe.wait_ge(S("v_early"), 3)
            pe.wait_ge(S("kq_root"), 6)
            pe.wait_ge(S("rows_ev"), 13)
            for t in range(4):
                for d in range(2):
                    mm(ps[2][:, t * 24 + d * 12:t * 24 + d * 12 + 12], mask[d], G[:, t, d * 12:d * 12 + 12],
                       start=True, stop=True)
            mm(ps[2][:, 128:224], ones, G[:, :, :].rearrange("p t n -> p (t n)"), start=True, stop=True) \
                .then_inc(S("one_ps"), 1)
            for t in range(T):
                for g in range(2):
                    ins = mm(pD[0][:, (2 * t + g) * P:(2 * t + g + 1) * P], BT[:, g, t * P:(t + 1) * P],
                             CT[:, g, t * P:(t + 1) * P], start=True, stop=True)
            ins.then_inc(S("one_ps"), 1)
            pe.wait_ge(S("gates"), 1)
            pe.wait_ge(S("mod"), 2)
            pe.wait_ge(S("state0"), 1)
            pe.wait_ge(S("kn_ev"), 4)
            pe.wait_ge(S("kq_norm"), 6)

            def sums_over(bank, t, c):
                d = 0 if c < 12 else 1
                for h in range(4):
                    ins = mm(bank[:, h * P:(h + 1) * P], G[:, t, c + h:c + h + 1].to_broadcast([P, P]), mask[d],
                             start=True, stop=True)
                return ins

            def piece(u, d, kind):
                t, c = tile_of(u, d), 12 * d + 4
                if kind in "ab":
                    m = 2 * (2 * (u - 2) + d) + (1 if kind == "b" else 0)
                    if kind == "a" and m:
                        pe.wait_ge(S("yd_rd"), 2 * (u - 2) + d)
                    if kind == "a":
                        pe.wait_ge(S("h_ready"), 2 * u + (0 if d == 0 else 1))
                    else:
                        pe.wait_ge(S("ws_arg"), m)
                    sums_over(pD[d], t, c + (4 if kind == "b" else 0)).then_inc(S("wg_ps"), 1)
                elif kind == "e":
                    m = 2 * u + d
                    if m >= 2:
                        pe.wait_ge(S("h_ready"), m - 1 if u < 2 else m)
                    if u >= 2:
                        pe.wait_ge(S("ws_arg"), 2 * (2 * (u - 2) + d + 1))
                        for g in range(2):
                            ins = mm(pD[d][:, g * L:(g + 1) * L], CT[:, g, t * P:(t + 1) * P],
                                     ht[:, d, g * L:(g + 1) * L], start=True, stop=True)
                        ins.then_inc(S("yo_ps"), 1)
                        pe.wait_ge(S("yo_rd"), 2 * (u - 2) + d + 1)
                    pe.wait_ge(S("xde_ready"), m + 1)
                    for g in range(2):
                        ins = mm(pD[d][:, g * L:(g + 1) * L], BN[:, t, g * P:(g + 1) * P],
                                 xde[:, g * L:(g + 1) * L], start=True, stop=True)
                    ins.then_inc(S("hs_ps"), 1)
                else:
                    pe.wait_ge(S("h_ready"), 2 * u + d + 1)
                    pe.wait_ge(S("ws_ready"), 2 * (u - 2) + d + 1)
                    pe.wait_ge(S("xdt_ready"), 2 * (u - 2) + d + 1)
                    for h in range(8):
                        ins = mm(pD[d][:, h * SP_:(h + 1) * SP_], Ws[:, h, :], xdt[:, h * SP_:(h + 1) * SP_],
                                 start=True, stop=True)
                    ins.then_inc(S("yd_ps"), 1)

            def four(bank, left, right):
                for h in range(4):
                    ins = mm(bank[:, h * P:(h + 1) * P], left(h), right(h), start=True, stop=True)
                return ins

            for u in range(4):
                for d in range(2):
                    t = tile_of(u, d)
                    at = slice(t * P, (t + 1) * P)
                    if u >= 1:
                        pe.wait_ge(S(f"s{d}"), u)
                    four(pA[d], lambda h: kT[:, h, at], lambda h: kT[:, h, at])
                    if u >= 2:
                        four(pC[d], lambda h: kT[:, h, at], lambda h: qT[:, h, at])
                    sums_over(pB[d], t, 12 * d).then_inc(S(f"pre{d}"), 1)
                for d in range(2):
                    pe.wait_ge(S(f"mn{d}"), u * LEVELS + 1)
                    four(pA[d], lambda h: Mn[d][0][:, h, :], lambda h: ident).then_inc(S(f"p_ps{d}"), 1)
                for l in range(1, LEVELS):
                    for d in range(2):
                        pe.wait_ge(S(f"mn{d}"), u * LEVELS + l + 1)
                        pe.wait_ge(S(f"x{d}"), u * LEVELS + l)
                        four(pA[d], lambda h: Mn[d][l % 2][:, h, :], lambda h: X[d][:, h, :]) \
                            .then_inc(S(f"p_ps{d}"), 1)
                        if l >= 2:
                            for h in range(4):
                                ins = tr(pC[d][:, h * P:(h + 1) * P], X[d][:, h, :], ident)
                            ins.then_inc(S(f"xt_ps{d}"), 1)
                    for d, kind in pieces(u, l):
                        piece(u, d, kind)
                    for d in range(2):
                        pe.wait_ge(S(f"p_ev{d}"), u * (LEVELS - 1) + l)
                        if l >= 2:
                            pe.wait_ge(S(f"xt_ev{d}"), u * (LEVELS - 2) + l - 1)
                        if l < LEVELS - 1:
                            four(pB[d], lambda h: XT[d][:, h, :], lambda h: Pv[d][:, h, :]) \
                                .then_inc(S(f"q_ps{d}"), 1)
                        else:
                            four(pC[d], lambda h: Pv[d][:, h, :], lambda h: XT[d][:, h, :]) \
                                .then_inc(S(f"q_ps{d}"), 1)
                for d in range(2):
                    t = tile_of(u, d)
                    at = slice(t * P, (t + 1) * P)
                    four(pA[d], lambda h: kT[:, h, at], lambda h: St[:, d, h, :]).then_inc(S(f"ks_ps{d}"), 1)
                for d in range(2):
                    pe.wait_ge(S(f"r{d}"), u + 1)
                    pe.wait_ge(S(f"x{d}"), LEVELS * (u + 1))
                    four(pB[d], lambda h: XT[d][:, h, :], lambda h: Mn[d][1][:, h, :]).then_inc(S(f"vn_ps{d}"), 1)
                for d in range(2):
                    t = tile_of(u, d)
                    at = slice(t * P, (t + 1) * P)
                    pe.wait_ge(S(f"vnew{d}"), u + 1)
                    if u >= 2:
                        pe.wait_ge(S(f"pt{d}"), u - 1)
                        four(pC[d], lambda h: qT[:, h, at], lambda h: St[:, d, h, :])
                        four(pA[d], lambda h: PT[d][:, h, :], lambda h: vnew[d][:, h, :]).then_inc(S(f"o_ps{d}"), 1)
                    if u < 3:
                        pe.wait_ge(S(f"kd{d}"), u + 1)
                        four(pB[d], lambda h: NT[d][:, h, :], lambda h: vnew[d][:, h, :]).then_inc(S(f"s_ps{d}"), 1)
            pe.wait_ge(S("normed"), 4)

            def columns(nth, src):
                for k in range(KD):
                    if k >= 2:
                        pe.wait_ge(S("cols_ev"), nth * KD + k - 1)
                    for t in range(T):
                        ins = tr(ps[2 + k % 2][:, t * P:(t + 1) * P], src(k, t), ident)
                    ins.then_inc(S("cols_ps"), 1)

            columns(0, lambda k, t: (oacc if k < 4 else yacc)[:, t, (k % 4) * P:(k % 4 + 1) * P])
            for i in range(16):
                pe.wait_ge(S("dg"), i + 1)
                mm(ps[4 + i // 4][:, (i % 4) * P:(i % 4 + 1) * P], ones, dg[i % 2], start=True,
                   stop=True).then_inc(S("dg_ps"), 1)
            pe.wait_ge(S("cols_ev"), 8)
            pe.wait_ge(S("gain_rows"), 4)

            def token_rows(bank, w, src, t, n, name):
                for k in range(KD):
                    ins = mm(ps[bank][:, 0:n], src[:, k, t * P:(t + 1) * P], w[:, k, :], start=(k == 0),
                             stop=(k == KD - 1))
                ins.then_inc(S(name), 1)

            for c in range(2):
                w = arrived(pe, wo_ch[c])
                for t in range(T):
                    token_rows(4 + 2 * c + t, w, mixT, t, 512, "wo_ps")
            pe.wait_ge(S("xh"), 6)
            columns(1, lambda k, t: xh[:, t, k * P:(k + 1) * P])
            pe.wait_ge(S("cols_ev"), 16)
            for b in range(KF):
                if b % 4 == 0:
                    wg = arrived(pe, ga_ch[b // 4])
                at = slice((b % 4) * P, (b % 4 + 1) * P)
                if b >= 2:
                    pe.wait_ge(S("f_taps"), b - 1)
                for k in range(KD):
                    ins = mm(ps[b % 2][:, 0:L], wg[:, k, at], hT2[:, k, :], start=(k == 0), stop=(k == KD - 1))
                ins.then_inc(S("gate_ps"), 1)
                if b % 4 == 0:
                    wu = arrived(pe, up_ch[b // 4])
                if b >= 2:
                    pe.wait_ge(S("f_hid"), b - 1)
                for k in range(KD):
                    ins = mm(ps[2 + b % 2][:, 0:L], wu[:, k, at], hT2[:, k, :], start=(k == 0), stop=(k == KD - 1))
                ins.then_inc(S("up_ps"), 1)
            pe.wait_ge(S("x_step"), 4)
            for c in range(6):
                w = arrived(pe, dn_ch[c])
                for kk in range(min(4, KF - 4 * c)):
                    k = 4 * c + kk
                    if c == 5 or kk == 0:
                        pe.wait_ge(S("f_hid"), min(k + 4, KF))
                    for t in range(T):
                        for h in range(2):
                            ins = mm(ps[4 + 2 * t + h][:, :], hid[:, k, t * P:(t + 1) * P],
                                     w[:, kk, 512 * h:512 * h + 512], start=(k == 0), stop=(k == KF - 1))
                ins.then_inc(S("down_ps"), 1)
            pe.wait_ge(S("xh"), 8)
            columns(2, lambda k, t: xh[:, t, k * P:(k + 1) * P])
            pe.wait_ge(S("cols_ev"), 24)
            for i, (c0, n) in enumerate(IN2):
                w = arrived(pe, in2_ch[i])
                for t in range(T):
                    j = 2 * i + t
                    if j >= 4:
                        pe.wait_ge(S("in2_ev"), j - 3)
                    token_rows(4 + j % 4, w, uT, t, n, "in2_ps")
            for i in range(13):
                if i == 0:
                    pe.wait_ge(S("rot_a"), 2)
                if i == 5:
                    pe.wait_ge(S("rot_b"), 2)
                if i >= 2:
                    pe.wait_ge(S("qt_ev"), i - 1)
                for hh in range(2):
                    head = 2 * i + hh
                    c0 = head * HD if head < 10 else 768 + (head - 10) * HD
                    for t in range(T):
                        ins = tr(ps[i % 2][0:HD, hh * L + t * P:hh * L + (t + 1) * P], pj[:, t, c0:c0 + HD], ident)
                ins.then_inc(S("qt_ps"), 1)
            pe.wait_ge(S("qt_ev"), 13)
            pe.wait_ge(S("in2_ev"), 10)

            def scores(h):
                qi, ki = (h, 8 + h // 4) if h < 8 else (2 + h, 10 + h)
                if h >= 2:
                    pe.wait_ge(S("s_exp"), 2 * (h - 1))
                for t in range(T):
                    ins = mm(ps[h % 2][:, t * L:(t + 1) * L], qkT[0:HD, qi, t * P:(t + 1) * P], qkT[0:HD, ki, :],
                             start=True, stop=True)
                ins.then_inc(S("s_ps"), 1)

            def prob_rows(h):
                pe.wait_ge(S("pr"), h + 1)
                if h >= 2:
                    pe.wait_ge(S("pt_ev"), h - 1)
                for kt in range(2):
                    for t in range(T):
                        ins = tr(ps[2 + h % 2][:, (2 * kt + t) * P:(2 * kt + t + 1) * P],
                                 pr[h % 2][:, t, kt * P:(kt + 1) * P], ident)
                ins.then_inc(S("pt_ps"), 1)

            def values(h):
                vc = 640 + HD * (h // 4) if h < 8 else 1792 + HD * (h - 8)
                pe.wait_ge(S("pt_ev"), h + 1)
                e0, c0 = HD * (h % 2), L * (h // 2 % 2)
                for kt in range(2):
                    ins = mm(ps[4 + h // 4][e0:e0 + HD, c0:c0 + L], pj[:, kt, vc:vc + HD],
                             prT[h % 2][:, kt, :, :].rearrange("p t q -> p (t q)"), start=(kt == 0), stop=(kt == 1))
                ins.then_inc(S("pv_ps"), 1)

            for h in range(18):
                if h < 16:
                    scores(h)
                if 1 <= h < 17:
                    prob_rows(h - 1)
                if h >= 2:
                    values(h - 2)
            for k in range(KD):
                pe.wait_ge(S("sqT"), k // 2 + 1)
                ins = mm(ps[0][:, L * (k // 4):L * (k // 4) + L], ones, sqT[:, L * k:L * k + L], start=(k % 4 == 0),
                         stop=(k % 4 == 3))
            ins.then_inc(S("ss_ps"), 1)
            pe.wait_ge(S("o_norm"), KD)
            for c in range(2):
                w = arrived(pe, wo2_ch[c])
                for t in range(T):
                    token_rows(4 + 2 * c + t, w, uT, t, 512, "wo2_ps")
            pe.wait_ge(S("xh"), 10)
            columns(3, lambda k, t: xh[:, t, k * P:(k + 1) * P])
            pe.wait_ge(S("cols_ev"), 32)
            pe.wait_ge(S("in_rw"), 16)
            for t in range(T):
                for k in range(KD):
                    ins = mm(ps[0][:, t * 36:(t + 1) * 36], u2T[:, k, t * P:(t + 1) * P], rw[:, k, :],
                             start=(k == 0), stop=(k == KD - 1))
            ins.then_inc(S("one_ps"), 1)
            pe.wait_ge(S("flag"), 1)
            flag = ra[4]
            mm(ps[1][:, 0:NE], C("strict", P), flag[:, 0, :], start=True, stop=True)
            mm(ps[1][:, NE:2 * NE], ones, flag[:, 0, :], start=True, stop=False)
            mm(ps[1][:, NE:2 * NE], C("strict", P), flag[:, 1, :], start=False, stop=True)
            mm(ps[1][:, 2 * NE:3 * NE], ones, flag[:, 0, :], start=True, stop=False)
            mm(ps[1][:, 2 * NE:3 * NE], ones, flag[:, 1, :], start=False, stop=True).then_inc(S("one_ps"), 1)
            pe.wait_ge(S("count_ready"), 1)
            npairs = pe.value_load(units[0:1, NU:NU + 1], min_val=NPAIR, max_val=NU // 2)

            def gather(n):
                pe.wait_ge(S("sel"), n)
                for k in range(KD):
                    for t in range(T):
                        ins = mm(ps[6 + k // 4][:, (k % 4) * P:(k % 4 + 1) * P], u2[:, t, k * P:(k + 1) * P],
                                 sel[:, t, :], start=(t == 0), stop=(t == 1))
                ins.then_inc(S("gather_ps"), 1)

            def product(p, bank, s, left, nk, c0, name):
                for j in range(2):
                    if c0 == 0:
                        pe.wait_ge(S(f"loaded{s + j}"), p * 16 + 16 * (base[s + j] + 1))
                w = [slot(s + j).rearrange("p (k n) -> p k n", k=nk) for j in range(2)]
                for k in range(nk):
                    for j in range(2):
                        ins = mm(ps[bank][j * SLOT:(j + 1) * SLOT, :], left[:, k, j * SLOT:(j + 1) * SLOT],
                                 w[j][:, k, c0:c0 + 512], start=(k == 0), stop=(k == nk - 1))
                ins.then_inc(S(name), 1)

            def scatter(p, last):
                pe.wait_ge(S("yn_a"), p + 1)
                pe.wait_ge(S("yn_v"), p + 1)
                pe.wait_ge(S("gt_ev"), p + 1)
                for t in range(T):
                    for c in range(2):
                        ins = mm(ps[2 * t + c][:, :], gselT[:, t * P:(t + 1) * P], yN[:, 512 * c:512 * c + 512],
                                 start=False, stop=last)
                if last:
                    ins.then_inc(S("sc_ps"), 1)

            for t in range(T):
                for c in range(2):
                    mm(ps[2 * t + c][:, :], yN[:, 0:P], u2[:, 0, 0:512], start=True, stop=False)
            gather(1)
            with pe.Fori(0, npairs) as p:
                pe.wait_ge(S("xsel_a"), p + 1)
                pe.wait_ge(S("xsel_v"), p + 1)
                pe.wait_ge(S("yn_a"), p + 1)
                product(p, 5, 0, xsel, KD, 0, "eg_ps")
                pe.wait_ge(S("yn_v"), p + 1)
                product(p, 4, 2, xsel, KD, 0, "eu_ps")
                scatter(p, False)
                pe.wait_ge(S("hid"), p + 1)
                for f in range(4):
                    ins = tr(ps[5][:, f * P:(f + 1) * P], hidN[:, f * P:(f + 1) * P], ident)
                ins.then_inc(S("hidT_ps"), 1)
                gather(p + 2)
                pe.wait_ge(S("hidT_ev"), p + 1)
                product(p, 5, 4, hidT, 4, 0, "yn_ps")
                product(p, 4, 4, hidT, 4, 512, "yn_ps")
                pe.wait_ge(S("gsel"), p + 1)
                pe.wait_ge(S("xsel_a"), p + 2)
                for t in range(T):
                    ins = tr(ps[6][:, t * P:(t + 1) * P], gsel[:, t, :], ident)
                ins.then_inc(S("gt_ps"), 1)
            scatter(npairs, True)


def constants():
    import numpy as np
    c = np.zeros((P, NCO), np.float32)
    j, i = np.arange(P)[:, None], np.arange(P)[None, :]
    c[:, CO["ident"]:CO["ident"] + P] = i == j
    c[:, CO["ones"]:CO["ones"] + P] = 1
    c[:, CO["mf"]:CO["mf"] + P] = i >= j
    c[:, CO["mb"]:CO["mb"] + P] = i <= j
    c[:, CO["strict"]:CO["strict"] + P] = i > j
    for lv in range(LEVELS):
        s = 2 ** lv
        m = (i // (2 * s) == j // (2 * s)) & (j % (2 * s) < s) & (i % (2 * s) >= s)
        c[:, CO["lvl"] + lv * P:CO["lvl"] + (lv + 1) * P] = m
        c[:, CO["lvl"] + (LEVELS + lv) * P:CO["lvl"] + (LEVELS + lv + 1) * P] = m.T
    c[:, CO["iota"]:CO["iota"] + SLOT] = np.arange(SLOT)
    c[:, CO["desc"]:CO["desc"] + NE] = NE - np.arange(NE)
    c[:, CO["fold"]:CO["fold"] + 32] = j % 32 == i[:, 0:32]
    c[:, CO["eps"]:CO["eps"] + 4] = (EPS, EPS * P, 1.0, 0.0)

    def inv(dim):
        e = np.arange(0, dim, 2, dtype=np.float32) / np.float32(dim)
        return (np.float32(1.0) / (np.float32(10000.0) ** e)).astype(np.float32)

    tok = np.arange(L)
    row, colm = (tok // GRID).astype(np.float32), (tok % GRID).astype(np.float32)
    axial = np.concatenate([row[:, None] * inv(HD // 2), colm[:, None] * inv(HD // 2)], axis=1)
    linear = tok.astype(np.float32)[:, None] * inv(HD)
    for kind, ang in enumerate((axial, linear)):
        cos, sin = np.cos(ang.astype(np.float64)), np.sin(ang.astype(np.float64))
        tab = np.concatenate([cos, cos, -sin, sin], axis=1).astype(np.float32)
        for t in range(T):
            at = CO["rope"] + (kind * T + t) * 2 * HD
            c[:, at:at + 2 * HD] = tab[t * P:(t + 1) * P]
    q, k = tok[:, None], tok[None, :]
    count = np.zeros((L, L))
    for window, dil in ((128, 1), (512, 4), (2048, 16)):
        count += (q % dil == k % dil) & (np.abs(q // dil - k // dil) <= window // (2 * dil))
    bias = np.where(count > 0, np.log(np.maximum(count, 1)), -1e30).astype(np.float32)
    return c, bias


def kernel(**inputs):
    import numpy as np
    import concourse.bacc as _bacc
    from concourse.bass_utils import run_bass_kernel_spmd as _run

    v = {n: np.asarray(a) for n, a in inputs.items()}
    r = lambda n: v[n].reshape(-1, P)
    w_in = v["w_in"][0]
    vec = np.concatenate([
        r("b_ada"), r("norm1_g"), r("norm2_g"), r("gdn_conv_w"), r("ssm_conv_w"), r("ssm_conv_b"),
        np.repeat(r("gdn_norm_g"), 4, axis=0), r("ssm_norm_g"), r("norm1_g_2"), r("out_norm_a_g_2"),
        r("out_norm_b_g_2"), r("norm2_g_2"), r("ffn_conv_w"), r("ffn_conv_b")], axis=0)
    vec = np.concatenate([vec, np.zeros((NROWS - vec.shape[0], P), np.float32)], axis=0)
    both = lambda a, b: np.concatenate([a[0, 0], b[0, 0], a[0, 1], b[0, 1]])
    rowv = np.concatenate([
        both(v["gdn_dt_bias"], v["ssm_dt_bias"]), both(v["gdn_A_log"], v["ssm_A_log"]), v["ssm_D"][0],
        v["q_norm_g_2"][0], v["k_norm_g_2"][0], v["router_group_b_2"][0], v["router_expert_b_2"][0]])
    small = np.concatenate([w_in[:, 2048:2052], w_in[:, 3600:3608], w_in[:, 2052:2056], w_in[:, 3608:3616],
                            w_in[:, 2056:2064]], axis=1)
    consts, bias = constants()
    cc = np.stack([v["c"].reshape(KD, P).T, v["c_ctx"].reshape(KD, P).T], axis=2)
    arrays = {
        "x": v["x"][0], "ctx": v["ctx"][0], "cc": cc, "vec_rows": vec, "rowv": rowv[None, :], "w_small": small,
        "consts": consts, "bias": bias, "w_ada": v["w_ada"][0], "w_in": w_in, "w_out": v["w_out"][0],
        "w_gate": v["ffn_w_gate"][0], "w_up": v["ffn_w_up"][0], "w_down": v["ffn_w_down"][0],
        "fng": v["final_norm_g"][None, :], "fng2": v["final_norm_g_2"][None, :], "n2row": v["norm2_g_2"],
        "w_in2": v["w_in_2"][0], "w_out2": v["w_out_2"][0],
        "rw": np.concatenate([v["router_group_w_2"][0], v["router_expert_w_2"][0]], axis=1),
        "e_gate": v["w_gate_2"][0], "e_up": v["w_up_2"][0], "e_down": v["w_down_2"][0],
    }
    arrays = {n: np.ascontiguousarray(a) for n, a in arrays.items()}
    nc = _bacc.Bacc("TRN2", target_bir_lowering=False, num_devices=1)
    ap = {n: nc.dram_tensor("in_" + n, a.shape, mybir.dt.from_np(a.dtype), kind="ExternalInput").ap()
          for n, a in arrays.items()}
    out = nc.dram_tensor("out", (L, D), mybir.dt.float32, kind="ExternalOutput").ap()
    build(nc, ap, out)
    got = _run(nc, [{"in_" + n: a for n, a in arrays.items()}], core_ids=[0])
    return got.results[0]["out"].reshape(1, L, D)
```

```python
import math
from contextlib import ExitStack

import concourse.bass as bass
from concourse import mybir

P = 128
D = 1024
L = 256
T = L // P
KD = D // P
EPS = 1e-6
GH, SH, SG, SP_ = 4, 8, 2, 64
FF = 2816
KF = FF // P
ARENA = 28560
NE, DE, SLOT = 32, 512, 64
NPAIR = NE // 2
EXTRA = 8
NU = NE + EXTRA
HD = 64
SCALE = HD ** -0.5
LEVELS = 7
GRID = 64

WQ, WK, WV, WZG = 0, 512, 1024, 1536
WZS, WXS, WBC = 2064, 2576, 3088
ROWS = {}
_at = 0
for _name, _n in (("b_ada", 48), ("norm1", 8), ("norm2", 8), ("gconv", 36), ("sconv", 24), ("sconvb", 8),
                  ("mixg", 8), ("n1b", 8), ("outab", 8), ("n2b", 8), ("fconv", 9 * KF), ("fconvb", KF)):
    ROWS[_name] = _at
    _at += _n
NROWS = 3 * P
assert _at <= NROWS
RV = {}
_at = 0
for _name, _n in (("dtb", 24), ("alog", 24), ("ssmD", 8), ("qn", 64), ("kn", 64), ("rb", 36)):
    RV[_name] = _at
    _at += _n
NRV = _at
CO = {}
_at = 0
for _name, _n in (("ident", P), ("ones", P), ("mf", P), ("mb", P), ("lvl", 2 * LEVELS * P), ("strict", P),
                  ("iota", SLOT), ("desc", NE), ("eps", 4), ("fold", 32), ("rope", 2 * T * 2 * HD)):
    CO[_name] = _at
    _at += _n
NCO = _at


def build(nc, ap, out):
    f32, i32 = mybir.dt.float32, mybir.dt.int32
    ACT, ALU, AX = mybir.ActivationFunctionType, mybir.AluOpType, mybir.AxisListType.X
    MUL, ADD, SUB = ALU.mult, ALU.add, ALU.subtract
    stack = ExitStack()
    with stack:
        sems = {}

        def S(name):
            if name not in sems:
                sems[name] = stack.enter_context(nc.semaphore(name))
            return sems[name]

        ring = stack.enter_context(nc.sbuf_tensor("ring", [P, 6 * 4096], f32))
        A = stack.enter_context(nc.sbuf_tensor("arena", [P, ARENA], f32))
        units = stack.enter_context(nc.sbuf_tensor("units", [P, NU + 2], i32))
        ps = [stack.enter_context(nc.psum_tensor(f"bank{i}", [P, 512], f32)) for i in range(8)]

        top = [0]

        def take(n, at=None):
            a = top[0] if at is None else at
            if at is None:
                top[0] += n
            assert a + n <= ARENA, (a, n)
            return A[:, a:a + n]

        co = take(NCO)
        C = lambda k, n: co[:, CO[k]:CO[k] + n]
        ident, ones = C("ident", P), C("ones", P)
        mask = [C("mf", P), C("mb", P)]
        lvl = [[co[:, CO["lvl"] + (d * LEVELS + l) * P:CO["lvl"] + (d * LEVELS + l + 1) * P] for l in range(LEVELS)]
               for d in range(2)]
        col = take(NROWS)
        V = lambda k, i, n=1: col[:, ROWS[k] + i:ROWS[k] + i + n]
        rowv = take(NRV)
        R = lambda k, n: rowv[:, RV[k]:RV[k] + n]
        mod = take(96).rearrange("p (j c) -> p j c", c=2)
        scale1 = take(16).rearrange("p (j c) -> p j c", c=2)
        scale2 = take(8)
        stat = take(32)
        rstd = take(32)
        yoff = take(512)
        x = take(T * D).rearrange("p (t n) -> p t n", t=T)
        F0 = top[0]

        def lay(at, n):
            assert F0 + at + n <= ARENA, (at, n)
            return A[:, F0 + at:F0 + at + n]

        def tiles(v, t):
            return v.rearrange("p (t n) -> p t n", t=t)

        kT, BT = tiles(lay(0, 2048), 4), tiles(lay(2048, 1024), 2)
        CT, qT = tiles(lay(3072, 512), 2), tiles(lay(3584, 1024), 4)
        vN, kN, xsN = tiles(lay(4608, 2048), 4), tiles(lay(6656, 2048), 4), tiles(lay(8704, 2048), 4)
        BN, Z = tiles(lay(10752, 1024), 4), tiles(lay(11776, 2048), 2)
        hT, ctx = tiles(lay(13824, 4096), KD), tiles(lay(17920, 2048), 2)
        St = lay(13824, 1024).rearrange("p (d h e) -> p d h e", d=2, h=4)
        ht = tiles(lay(14848, 1024), 2)
        vnew = [tiles(lay(15872 + 512 * d, 512), 4) for d in range(2)]
        xdt, xde = lay(16896, 512), lay(17408, 512)
        Ws = tiles(lay(17920, 1024), 8)
        CBs = lay(18944, 512).rearrange("p (t g i) -> p t g i", t=T, g=2)
        gx = tiles(lay(19968, 128), 4)
        G, dtv, gtmp, gc, egc, kd, etot, dtkd = (tiles(lay(20096 + 96 * i, 96), 4) for i in range(8))
        beta, nbeta, nega = tiles(lay(20864, 32), 4), tiles(lay(20896, 32), 4), lay(20928, 24)
        oacc, yacc = kN[:, 2:4, :], vN[:, 2:4, :]

        def scratch(at, n):
            return ring[:, 4 * 4096 + at:4 * 4096 + at + n]

        xn = tiles(scratch(0, 4096), 4)
        cconv = [scratch(4096 + 512 * i, 512) for i in range(2)]
        csilu = [scratch(5120 + 512 * i, 512) for i in range(3)]
        sqb = [scratch(6656 + 512 * i, 512) for i in range(2)]
        root = [scratch(512 * i, 512) for i in range(2)]
        vecs = scratch(6656, 3 * P)
        craw = scratch(7680, 16).rearrange("p (k c) -> p k c", c=2)
        csil = tiles(scratch(7696, 256), KD)
        wsm = tiles(lay(20960, 256), KD)
        arow = [lay(21216, 512), yoff]
        junk0 = scratch(4096, 1024)
        E, NT, PT, Pv, X, XT, Mn0, Mn1 = ([tiles(scratch(4096 * d + 512 * i, 512), 4) for d in range(2)]
                                          for i in range(8))
        Mn = [[Mn0[d], Mn1[d]] for d in range(2)]
        NTu = [NT, [tiles(lay(20960 + 512 * d, 512), 4) for d in range(2)]]
        PTu = [PT, [kT[:, :, L + P * d:L + P * d + P] for d in range(2)]]
        pA, pB, pC, pD = [ps[0], ps[4]], [ps[1], ps[5]], [ps[2], ps[6]], [ps[3], ps[7]]

        mixT, g1r, g2r = tiles(lay(0, 2048), KD), lay(2048, D), lay(3072, D)
        dg = [lay(8704 + P * i, P) for i in range(16)]
        hid = tiles(lay(4608, KF * L), KF)
        tmpx = [lay(12288 + 512 * i, 512) for i in range(2)]
        xh, hT2 = tiles(lay(13824, 2048), 2), tiles(lay(15872, 2048), KD)
        fa, fs = [lay(17920 + L * i, L) for i in range(2)], [lay(18432 + L * i, L) for i in range(2)]
        junk = lay(18944, 1024)
        n2row = lay(19968, D)
        fng2 = lay(20992, D)
        fng1 = lay(10240, D)

        pj = tiles(lay(0, 4608), 2)
        rotb = tiles(lay(4608, 2048), 2)
        rota = tiles(lay(6656, 1280), 2)
        sqT = lay(4608, 2048)
        sc = [tiles(lay(7936 + 512 * i, 512), 2) for i in range(2)]
        pr = [tiles(lay(8960 + 512 * i, 512), 2) for i in range(2)]
        mx, sm = (lay(9984 + 32 * i, 32).rearrange("p (h t) -> p h t", t=2) for i in range(2))
        prT = [lay(12288 + 512 * i, 512).rearrange("p (k t q) -> p k t q", k=2, t=2) for i in range(2)]
        bias = tiles(lay(13312, 512), 2)
        qkT = tiles(scratch(0, 26 * L), 26)
        uT = hT2

        u2, u2T = tiles(lay(0, 2048), 2), hT2
        rw, lg = tiles(lay(2048, 288), KD), tiles(lay(2336, 72), 2)
        ra = [tiles(lay(2408 + 64 * i, 64), 2) for i in range(6)]
        rs = lay(2792, 32).rearrange("p (j t) -> p j t", t=2)
        SL, GT = tiles(lay(2824, 2 * (NU + 2)), 2), tiles(lay(2912, 2 * (NU + 2)), 2)
        cur = lay(3352, 8).rearrange("p (c t e) -> p c t e", c=2, t=2)
        sel, gsel = tiles(lay(3360, 256), 2), tiles(lay(3616, 256), 2)
        gselT = lay(4128, 256)
        xsel, hidN, sg, hidT = tiles(lay(4608, 1024), KD), lay(5632, 512), lay(6144, 512), tiles(lay(6656, 512), 4)
        yN = lay(7168, D)
        over, scanA, scanB = (lay(8192 + 96 * i, 96) for i in range(3))
        cnt = lay(8480, 40)
        blk, unitE, unitB = tiles(lay(8520, 24), EXTRA), lay(8544, EXTRA), lay(8552, EXTRA)
        place = lay(12288, EXTRA * 96)
        ofexp, pick = tiles(lay(13056, EXTRA * NE), EXTRA), tiles(lay(8576, EXTRA * NE), EXTRA)

        def item(i):
            g, s = ROWS["gconv"], ROWS["sconv"]
            if i < 4:
                return 512, [g + 12 * a + 4 + i for a in range(3)], None, kT[:, i, :]
            if i < 8:
                return 512, [g + 12 * a + 4 + i for a in range(3)], None, csilu[i % 3]
            if i < 12:
                return 512, [s + 8 * a + i - 8 for a in range(3)], ROWS["sconvb"] + i - 8, csilu[i % 3]
            if i < 14:
                return 512, [s + 8 * a + i - 8 for a in range(3)], ROWS["sconvb"] + i - 8, BT[:, i - 12, :]
            if i < 16:
                return L, [s + 8 * a + i - 8 for a in range(3)], ROWS["sconvb"] + i - 8, CT[:, i - 14, :]
            return L, [g + 12 * a + i - 16 for a in range(3)], None, qT[:, i - 16, :]

        SQ_AT = (5, 7, 9, 11, 20, 21)

        def kq_block(n):
            return kT[:, n, :] if n < 4 else qT[:, 2 * n - 8:2 * n - 6, :].rearrange("p h t -> p (h t)")

        def tile_of(u, d):
            step = u % 2
            return (step if d == 0 else 1 - step) + (2 if u < 2 else 0)

        def pieces(u, l):
            if u < 2:
                return {1: [(0, "e")], 5: [(1, "e")]}.get(l, [])
            return {1: [(0, "a")], 2: [(0, "b")], 3: [(0, "e"), (0, "c")], 4: [(1, "a")], 5: [(1, "b")],
                    6: [(1, "e"), (1, "c")]}.get(l, [])

        def prepare(u, l):
            if u >= 4 or (u < 2 and l in (3, 6)):
                return []
            return [(u, 1 if l < 4 else 0, "gnk"[(l - 1) % 3])]

        STEPS = [(0, 1, "g"), (0, 0, "g"), (0, 1, "n"), (0, 0, "n")] + \
                [st for u in range(1, 4) for l in range(1, LEVELS) for st in prepare(u, l)]

        def step(u, d, kind):
            return STEPS.index((u, d, kind)) + 1

        def prep_bank(u, d, kind):
            return pA[d] if (u, kind) == (0, "n") else pD[d]

        def last_step(u, d):
            return step(u, d, "k" if u >= 2 else "n")

        def heads(v, n, e):
            return v.rearrange("p (h e) -> p h e", h=n, e=e)

        def wide(v, n):
            return v.unsqueeze(2).to_broadcast([P, v.shape[1], n])

        def each(v, h):
            return v.unsqueeze(1).to_broadcast([P, h, v.shape[1]])

        def rope(kind, t):
            at = CO["rope"] + (kind * T + t) * 2 * HD
            return co[:, at:at + HD], co[:, at + HD:at + 2 * HD]

        def slot(s):
            return ring[:, s * 4096:(s + 1) * 4096]

        chunks = []

        def cols(w, c0, n):
            return (lambda s: slot(s)[:, 0:KD * n].rearrange("p (k n) -> p k n", k=KD),
                    w[:, c0:c0 + n].rearrange("(k p) n -> p k n", p=P))

        def rows(w, k0, nk):
            return (lambda s: slot(s)[:, 0:nk * D].rearrange("p (k n) -> p k n", k=nk),
                    w[k0 * P:(k0 + nk) * P, :].rearrange("(k p) n -> p k n", p=P))

        def add(view, done, value):
            chunks.append((view, done, value))
            return len(chunks) - 1

        ada_ch = [add(cols(ap["w_ada"], 512 * i, 512), "rows_ps", i + 1) for i in range(4)]
        proj_ch = []
        PROJ = (WK, WV, WXS, WBC, WQ, WZG, WZS)
        PEND = (4, 8, 12, 16, 20, 22, 24)
        for i, c0 in enumerate(PROJ):
            proj_ch.append(add(cols(ap["w_in"], c0, 512), "item_ps", PEND[i]))
            ada_ch.append(add(cols(ap["w_ada"], 512 * (4 + i), 512), "rows_ps", 6 + i))
        ada_ch.append(add(cols(ap["w_ada"], 512 * 11, 512), "rows_ps", 13))
        wo_ch = [add(cols(ap["w_out"], 512 * c, 512), "wo_ps", 2 * c + 2) for c in range(2)]
        ga_ch, up_ch = [], []
        for c in range(6):
            n = min(512, FF - 512 * c)
            ga_ch.append(add(cols(ap["w_gate"], 512 * c, n), "gate_ps", min(4 * c + 4, KF)))
            up_ch.append(add(cols(ap["w_up"], 512 * c, n), "up_ps", min(4 * c + 4, KF)))
        dn_ch = [add(rows(ap["w_down"], 4 * c, min(4, KF - 4 * c)), "down_ps", c + 1 if c < 5 else 9) for c in range(6)]
        IN2 = ((0, 512), (512, 256), (768, 512), (1280, 512), (1792, 512))
        in2_ch = [add(cols(ap["w_in2"], c0, n), "in2_ps", 2 * i + 2) for i, (c0, n) in enumerate(IN2)]
        wo2_ch = [add(cols(ap["w_out2"], 512 * c, 512), "wo2_ps", 2 * c + 2) for c in range(2)]
        NCH = len(chunks)
        base = [len(range(s, NCH, 4)) for s in range(4)] + [0, 0]

        def arrived(pe, n):
            pe.wait_ge(S(f"loaded{n % 4}"), 16 * (n // 4 + 1))
            return chunks[n][0][0](n % 4)

        block = stack.enter_context(nc.Block())

        @block.sync
        def _(sp):
            for n, ((view, dram), done, value) in enumerate(chunks):
                if n >= 4:
                    sp.wait_ge(S(chunks[n - 4][1]), chunks[n - 4][2])
                sp.dma_start(view(n % 4), dram).then_inc(S(f"loaded{n % 4}"), 16)
                if n == 2:
                    sp.dma_start(ctx, ap["ctx"].rearrange("(t p) n -> p t n", p=P)).then_inc(S("in_ctx"), 16)

            ORDER = (("e_gate", 0), ("e_gate", 1), ("e_up", 0), ("e_up", 1), ("e_down", 0), ("e_down", 1))

            def expert(e, s):
                name = ORDER[s][0]
                nk = 4 if name == "e_down" else KD
                sp.dma_start(slot(s).rearrange("p (o k n) -> p o k n", o=1, k=nk),
                             ap[name][bass.ds(e, 1), :, :].rearrange("o (k p) n -> p o k n", p=P)) \
                    .then_inc(S(f"loaded{s}"), 16)

            sp.wait_ge(S("pv_ps"), 16)
            expert(0, 4)
            expert(1, 5)
            for last in range(NCH - 4, NCH):
                sp.wait_ge(S(chunks[last][1]), chunks[last][2])
                expert(ORDER[last % 4][1], last % 4)
            def load_pair(p, e):
                for s, (sem, n) in enumerate((("eg_ps", 1), ("eg_ps", 1), ("eu_ps", 1), ("eu_ps", 1),
                                              ("yn_ps", 2), ("yn_ps", 2))):
                    sp.wait_ge(S(sem), n * p)
                    expert(e[ORDER[s][1]], s)

            load_pair(1, (2, 3))
            sp.wait_ge(S("count_ready"), 1)
            npairs = sp.value_load(units[0:1, NU:NU + 1], min_val=NPAIR, max_val=NU // 2)
            with sp.Fori(2, npairs) as p:
                e = [sp.value_load(units[0:1, bass.ds(2 * p + j, 1)], min_val=0, max_val=NE - 1) for j in range(2)]
                load_pair(p, e)
            for t in range(T):
                sp.wait_ge(S("out_ready"), t + 1)
                sp.dma_start(out[t * P:(t + 1) * P, :], x[:, t, :]).then_inc(S("out_done"), 16)
            sp.wait_ge(S("out_done"), 16 * T)

        @block.gpsimd
        def _(g):
            def mul(o_, a, b):
                return nc.gpsimd.tensor_tensor(o_, a, b, MUL)

            for n in range(6):
                g.wait_ge(S("item_silu"), n + 1 if n < 4 else 20)
                if n >= 2:
                    g.wait_ge(S("sq_ps"), n - 1)
                mul(sqb[n % 2], kq_block(n), kq_block(n)).then_inc(S("sq_ready"), 1)
            g.wait_ge(S("item_ps"), 24)
            nc.gpsimd.memset(St[:, :, :, :], 0.0)
            nc.gpsimd.memset(ht[:, :, :], 0.0).then_inc(S("state0"), 1)
            g.wait_ge(S("gates"), 1)

            def piece(u, d, kind):
                t = tile_of(u, d)
                if kind == "c":
                    n = 2 * (u - 2) + d + 1
                    g.wait_ge(S("ws_exp"), n)
                    mul(Ws[:, :, :], Ws[:, :, :], each(mask[d], 8)).then_inc(S("ws_mask"), 1)
                    if n > 1:
                        g.wait_ge(S("yd_ps"), n - 1)
                    mul(heads(xdt, 8, SP_), heads(xsN[:, t, :], 8, SP_),
                        wide(dtv[:, t, 12 * d + 4:12 * d + 12], SP_)).then_inc(S("xdt_ready"), 1)
                if kind == "e":
                    n = 2 * u + d + 1
                    if n > 1:
                        g.wait_ge(S("hs_ps"), n - 1)
                    mul(heads(xde, 8, SP_), heads(xsN[:, t, :], 8, SP_),
                        wide(dtkd[:, t, 12 * d + 4:12 * d + 12], SP_)).then_inc(S("xde_ready"), 1)

            def strip(u, d, l):
                mul(Mn[d][l % 2], NTu[u % 2][d], each(lvl[d][l], 4)).then_inc(S(f"mn{d}"), 1)

            for d in range(2):
                g.wait_ge(S("prep"), step(0, d, "n"))
                strip(0, d, 0)
            for d in range(2):
                strip(0, d, 1)
            for u in range(4):
                for l in range(1, LEVELS):
                    if l + 1 < LEVELS:
                        for d in range(2):
                            g.wait_ge(S(f"p_ps{d}"), u * LEVELS + l)
                            if l == 1:
                                g.wait_ge(S(f"x{d}"), u * LEVELS + 1)
                            strip(u, d, l + 1)
                    for d, kind in pieces(u, l):
                        piece(u, d, kind)
                if u < 3:
                    for d in range(2):
                        g.wait_ge(S(f"p_ps{d}"), (u + 1) * LEVELS)
                        g.wait_ge(S("prep"), step(u + 1, d, "n"))
                        strip(u + 1, d, 0)
                    for d in range(2):
                        t = tile_of(u, d)
                        g.wait_ge(S(f"mn{d}"), LEVELS * (u + 1))
                        mul(NTu[u % 2][d], heads(kN[:, t, :], 4, P), wide(kd[:, t, 12 * d:12 * d + 4], P)) \
                            .then_inc(S(f"kd{d}"), 1)
                    for d in range(2):
                        strip(u + 1, d, 1)
                        if u >= 1:
                            g.wait_ge(S("prep"), step(u + 1, d, "k"))
                            mul(PTu[(u + 1) % 2][d], PTu[(u + 1) % 2][d], each(mask[d], 4)).then_inc(S(f"pt{d}"), 1)
            g.wait_ge(S("yd_rd"), 4)
            for t in range(T):
                mul(yacc[:, t, :], yacc[:, t, :], Z[:, t, 512:1024]).then_inc(S("y_gated"), 1)
            for i in range(16):
                mul(dg[i], ident, mod[:, (16 if i < 8 else 32) + i, 0:1].to_broadcast([P, P])).then_inc(S("dg"), 1)
            for t in range(T):
                g.wait_ge(S("in2_ev"), 8 + t + 1)
            link_n = 0
            for t in range(T):
                src = pj[:, t, 768:1792]
                s4, r4 = src.rearrange("p (h a e) -> p h a e", h=16, a=2), \
                    rotb[:, t, :].rearrange("p (h a e) -> p h a e", h=16, a=2)
                cos, sin = rope(1, t)
                for a in range(2):
                    mul(r4[:, :, a, :], s4[:, :, 1 - a, :], each(sin[:, 32 * a:32 * a + 32], 16)) \
                        .then_inc(S("pool_rot"), 1)
                link_n += 2
                g.wait_ge(S("pool_rot"), link_n)
                mul(heads(src, 16, HD), heads(src, 16, HD), each(cos, 16)).then_inc(S("pool_rot"), 1)
                link_n += 1
                g.wait_ge(S("pool_rot"), link_n)
                nc.gpsimd.tensor_tensor(src, src, rotb[:, t, :], ADD).then_inc(S("rot_b"), 1)
            g.wait_ge(S("pv_ps"), 16)
            g.wait_ge(S("s_exp"), 32)
            g.wait_ge(S("s_max"), 16)
            nc.gpsimd.memset(yN[:, 0:512], 0.0).then_inc(S("yn_a"), 1)
            nc.gpsimd.memset(yN[:, 512:1024], 0.0).then_inc(S("yn_v"), 1)
            nc.gpsimd.memset(gselT, 0.0).then_inc(S("gt_ev"), 1)

        @block.scalar
        def _(a):
            act = nc.scalar.activation
            a.dma_start(craw, ap["cc"]).then_inc(S("in_c"), 16)
            a.dma_start(co, ap["consts"]).then_inc(S("in_consts"), 16)
            a.dma_start(x, ap["x"].rearrange("(t p) n -> p t n", p=P)).then_inc(S("in_x"), 16)
            a.dma_start(tiles(vecs, 3), ap["vec_rows"].rearrange("(i p) n -> p i n", p=P)).then_inc(S("in_vecs"), 16)
            a.dma_start(wsm, ap["w_small"].rearrange("(k p) n -> p k n", p=P)).then_inc(S("in_rest"), 16)
            a.dma_start(rowv, ap["rowv"].to_broadcast([P, NRV])).then_inc(S("in_rest"), 16)
            a.wait_ge(S("in_c"), 16)
            a.wait_ge(S("v_early"), 1)
            act(csil[:, :, 0:2], craw, ACT.Silu).then_inc(S("c_silu"), 1)

            def rows_copy(j):
                a.wait_ge(S("rows_ps"), j + 1)
                if j >= 2:
                    a.wait_ge(S("fold_ps"), j - 1)
                act(arow[j % 2], ps[2 * (j % 2)][:, :], ACT.Copy).then_inc(S("rows_ev"), 1)

            for j in range(3):
                rows_copy(j)

            def rms(k, srcs, space, ready=None):
                for i, s in enumerate(srcs):
                    if k == 0 and i in (0, 2):
                        a.wait_ge(S("in_ctx" if i else "in_x"), 16)
                    if k or i:
                        a.wait_ge(S("rms_sq"), (2 + 2 * k if k else 0) + i)
                    if ready:
                        a.wait_ge(S("x_step"), ready[i])
                    act(space, s, ACT.Square, accum_out=stat[:, i:i + 1]).then_inc(S("rms_sq"), 1)
                a.wait_ge(S("rms_mean"), k + 1)
                act(rstd[:, 0:len(srcs)], stat[:, 0:len(srcs)], ACT.Sqrt).then_inc(S("rms_root"), 1)

            rms(0, [x[:, 0, :], x[:, 1, :], ctx[:, 0, :], ctx[:, 1, :]], junk0)
            rows_copy(3)
            a.wait_ge(S("mod"), 1)
            for k in range(0, KD, 2):
                a.wait_ge(S("ht_ps"), k + 1)
                b = ps[4 + k % 4]
                act(hT[:, k, 0:L], b[:, 0:L], ACT.Identity, scale=scale1[:, k, 0:1], bias=mod[:, k, 0:1])
                act(hT[:, k, L:2 * L], b[:, L:2 * L], ACT.Identity, scale=scale1[:, k, 1:2],
                    bias=mod[:, k, 1:2]).then_inc(S("ht_ev"), 1)

            def silu_item(i):
                n, _, _, dest = item(i)
                a.wait_ge(S("conv_v"), i + 1)
                if 7 <= i < 12:
                    a.wait_ge(S("tr_ps"), i - 6)
                act(dest, cconv[i % 2][:, 0:n], ACT.Silu).then_inc(S("item_silu"), 1)

            def k_rows(i):
                a.wait_ge(S("tr_ps"), 10 + i + 1)
                act(kN[:, :, i * P:(i + 1) * P], tiles(ps[6 + i % 2][:, :], 4), ACT.Copy).then_inc(S("kn_ev"), 1)

            rows_copy(4)
            for i in range(24):
                b = ps[4 + i % 2]
                if i in (4, 8, 12, 16, 20, 22):
                    rows_copy(4 + (4, 8, 12, 16, 20, 22).index(i) + 1)
                if i < 20:
                    n, taps, wb, _ = item(i)
                    if i >= 2:
                        a.wait_ge(S("item_silu"), i - 1)
                    a.wait_ge(S("item_ps"), i + 1)
                    act(cconv[i % 2][:, 0:n], b[:, 0:n], ACT.Identity, scale=col[:, taps[1]:taps[1] + 1],
                        bias=0.0 if wb is None else col[:, wb:wb + 1]).then_inc(S("conv_a"), 1)
                    if i >= 1:
                        silu_item(i - 1)
                    if i == 19:
                        silu_item(19)
                else:
                    j = i - 20
                    a.wait_ge(S("item_ps"), i + 1)
                    act(Z[:, j % 2, 512 * (j // 2):512 * (j // 2) + 512], b[:, :], ACT.Silu).then_inc(S("z_ev"), 1)
                    k_rows(j)
                if i in SQ_AT:
                    n = SQ_AT.index(i)
                    a.wait_ge(S("sq_ps"), n + 1)
                    if n >= 2:
                        a.wait_ge(S("kq_norm"), n - 1)
                    act(root[n % 2], ps[3][:, :], ACT.Sqrt, scale=1.0 if n < 4 else float(P),
                        bias=C("eps", 4)[:, 0:1] if n < 4 else C("eps", 4)[:, 1:2]).then_inc(S("kq_root"), 1)
                if i == 21:
                    a.wait_ge(S("exp_arg"), 1)
                    act(gtmp[:, :, :], gtmp[:, :, :], ACT.Exp).then_inc(S("exp_done"), 1)
                    a.wait_ge(S("exp_done"), 1)
                    act(beta[:, :, :], beta[:, :, :], ACT.Exp)
                    act(nega, R("alog", 24), ACT.Exp)
                    act(gtmp[:, :, :], gtmp[:, :, :], ACT.Ln, bias=C("eps", 4)[:, 2:3]).then_inc(S("exp_done"), 1)

            rows_copy(11)
            rows_copy(12)
            a.wait_ge(S("exp_arg"), 2)
            act(egc[:, :, :], gc[:, :, :], ACT.Exp)
            act(etot[:, :, :], etot[:, :, :], ACT.Exp)
            act(kd[:, :, :], kd[:, :, :], ACT.Exp).then_inc(S("exp_done"), 1)
            def decays(u, d, kind):
                if kind == "g":
                    a.wait_ge(S("prep"), step(u, d, "g"))
                    act(E[d], E[d], ACT.Exp).then_inc(S(f"e_exp{d}"), 1)

            for st in STEPS[:2]:
                decays(*st)
            for u in range(4):
                for l in range(1, LEVELS):
                    for d in range(2):
                        a.wait_ge(S(f"p_ps{d}"), u * LEVELS + l + 1)
                        act(Pv[d], tiles(pA[d][:, :], 4), ACT.Copy).then_inc(S(f"p_ev{d}"), 1)
                        if l >= 2:
                            a.wait_ge(S(f"xt_ps{d}"), u * (LEVELS - 2) + l - 1)
                            act(XT[d], tiles(pC[d][:, :], 4), ACT.Copy).then_inc(S(f"xt_ev{d}"), 1)
                    for d, kind in pieces(u, l):
                        if kind == "c":
                            a.wait_ge(S("ws_arg"), 2 * (2 * (u - 2) + d + 1))
                            act(Ws[:, :, :], Ws[:, :, :], ACT.Exp).then_inc(S("ws_exp"), 1)
                    for st in prepare(u + 1, l):
                        decays(*st)
            for t in range(T):
                a.wait_ge(S("y_gated"), t + 1)
                act((xdt, xde)[t], yacc[:, t, :], ACT.Square, accum_out=stat[:, 8 + t:9 + t]).then_inc(S("y_sq"), 1)
            for n, (c0, c1) in enumerate(((8, 10), (0, 8))):
                a.wait_ge(S("mean"), n + 1)
                act(rstd[:, c0:c1], stat[:, c0:c1], ACT.Sqrt).then_inc(S("root"), 1)

            def columns(nth, dest, scale, bias=None):
                for k in range(KD):
                    a.wait_ge(S("cols_ps"), nth * KD + k + 1)
                    act(dest[:, k, :], ps[2 + k % 2][:, 0:L], ACT.Identity, scale=scale(k),
                        bias=0.0 if bias is None else bias(k)).then_inc(S("cols_ev"), 1)

            columns(0, mixT, lambda k: V("mixg", k))
            rms(1, [x[:, 0, :], x[:, 1, :]], junk, (3, 4))
            columns(1, hT2, lambda k: scale2[:, k:k + 1], lambda k: mod[:, 24 + k, 0:1])
            a.dma_start(fng1, ap["fng"].to_broadcast([P, D])).then_inc(S("in_rows"), 16)
            a.dma_start(fng2, ap["fng2"].to_broadcast([P, D])).then_inc(S("in_rows"), 16)
            a.dma_start(n2row, ap["n2row"].to_broadcast([P, D])).then_inc(S("in_rows"), 16)
            a.dma_start(bias, ap["bias"].rearrange("(t p) n -> p t n", p=P)).then_inc(S("in_rows"), 16)

            def ffn_silu(b):
                a.wait_ge(S("f_taps"), b + 1)
                if b >= 2:
                    a.wait_ge(S("f_hid"), b - 1)
                act(fs[b % 2], fa[b % 2], ACT.Silu).then_inc(S("f_silu"), 1)

            for b in range(KF):
                if b >= 2:
                    a.wait_ge(S("f_silu"), b - 1)
                a.wait_ge(S("gate_ps"), b + 1)
                act(fa[b % 2], ps[b % 2][:, 0:L], ACT.Identity, scale=V("fconv", 4 * KF + b),
                    bias=V("fconvb", b)).then_inc(S("f_mid"), 1)
                if b >= 1:
                    ffn_silu(b - 1)
            ffn_silu(KF - 1)
            rms(2, [x[:, 0, :], x[:, 1, :]], junk, (6, 8))
            rms(3, [x[:, 0, :], x[:, 1, :]], junk, (9, 10))
            columns(2, uT, lambda k: V("n1b", k))
            for i, (c0, n) in enumerate(IN2):
                for t in range(T):
                    j = 2 * i + t
                    a.wait_ge(S("in2_ps"), j + 1)
                    act(pj[:, t, c0:c0 + n], ps[4 + j % 4][:, 0:n], ACT.Copy).then_inc(S("in2_ev"), 1)
            a.wait_ge(S("mean"), 3)
            act(rstd[:, 0:20], stat[:, 0:20], ACT.Sqrt).then_inc(S("root"), 1)
            for i in range(13):
                a.wait_ge(S("qt_ps"), i + 1)
                act(qkT[0:HD, 2 * i:2 * i + 2, :], ps[i % 2][0:HD, :].rearrange("p (h t) -> p h t", h=2),
                    ACT.Copy).then_inc(S("qt_ev"), 1)

            def prob_rows(h):
                a.wait_ge(S("pt_ps"), h + 1)
                if h >= 2:
                    a.wait_ge(S("pv_ps"), h - 1)
                act(prT[h % 2], ps[2 + h % 2][:, :].rearrange("p (k t q) -> p k t q", k=2, t=2),
                    ACT.Copy).then_inc(S("pt_ev"), 1)

            for h in range(16):
                a.wait_ge(S("s_max"), h + 1)
                if h >= 2:
                    a.wait_ge(S("pt_ps"), h - 1)
                for t in range(T):
                    src = ps[h % 2][:, t * L:(t + 1) * L] if h < 8 else sc[h % 2][:, t, :]
                    act(pr[h % 2][:, t, :], src, ACT.Exp, scale=SCALE if h < 8 else 1.0,
                        bias=mx[:, h, t:t + 1], accum_out=sm[:, h, t:t + 1]).then_inc(S("s_exp"), 1)
                if h >= 2:
                    prob_rows(h - 2)
            prob_rows(14)
            prob_rows(15)
            a.wait_ge(S("pv_ps"), 16)
            for b in range(4):
                act(sqT[:, 512 * b:512 * b + 512], ps[4 + b][:, :], ACT.Square).then_inc(S("sqT"), 1)
            a.wait_ge(S("mean"), 4)
            act(tmpx[0], tmpx[0], ACT.Sqrt).then_inc(S("root"), 1)
            a.dma_start(rw, ap["rw"].rearrange("(k p) n -> p k n", p=P)).then_inc(S("in_rw"), 16)
            rms(4, [x[:, 0, :], x[:, 1, :]], junk, (13, 14))
            columns(3, u2T, lambda k: V("n2b", k))
            a.wait_ge(S("exp_arg"), 3)
            act(ra[0][:, :, 0:4], ra[0][:, :, 0:4], ACT.Exp)
            act(rs[:, 5, :], rs[:, 5, :], ACT.Exp).then_inc(S("exp_done"), 1)
            a.wait_ge(S("gather_ps"), 1)
            act(xsel[:, 0:4, :], tiles(ps[6][:, :], 4), ACT.Copy).then_inc(S("xsel_a"), 1)
            act(xsel[:, 4:8, :], tiles(ps[7][:, :], 4), ACT.Copy).then_inc(S("xsel_v"), 1)

            def pair(p):
                a.wait_ge(S("eg_ps"), p + 1)
                act(sg, ps[5][:, :], ACT.Silu).then_inc(S("sg"), 1)
                a.wait_ge(S("hidT_ps"), p + 1)
                act(hidT, tiles(ps[5][:, :], 4), ACT.Copy).then_inc(S("hidT_ev"), 1)
                a.wait_ge(S("gather_ps"), p + 2)
                act(xsel[:, 0:4, :], tiles(ps[6][:, :], 4), ACT.Copy).then_inc(S("xsel_a"), 1)
                a.wait_ge(S("yn_ps"), 2 * p + 1)
                act(yN[:, 0:512], ps[5][:, :], ACT.Copy).then_inc(S("yn_a"), 1)

            pair(0)
            a.wait_ge(S("count_ready"), 1)
            npairs = a.value_load(units[0:1, NU:NU + 1], min_val=NPAIR, max_val=NU // 2)
            with a.Fori(1, npairs) as p:
                pair(p)
            rms(5, [x[:, 0, :], x[:, 1, :]], junk, (16, 18))

        @block.vector
        def _(v):
            tt, ts, stt = nc.vector.tensor_tensor, nc.vector.tensor_scalar, nc.vector.scalar_tensor_tensor
            n = [0]

            def link(ins):
                n[0] += 1
                ins.then_inc(S("dve"), 1)
                v.wait_ge(S("dve"), n[0])

            def rms(k, width=2):
                v.wait_ge(S("rms_sq"), 4 + 2 * k)
                ts(stat[:, 0:width], stat[:, 0:width], 1.0 / D, EPS, MUL, ADD).then_inc(S("rms_mean"), 1)
                v.wait_ge(S("rms_root"), k + 1)
                link(nc.vector.reciprocal(rstd[:, 0:width], rstd[:, 0:width]))

            nc.vector.memset(csil, 0.0).then_inc(S("v_early"), 1)
            rms(0, 4)
            for t in range(4):
                ts(xn[:, t, :], x[:, t, :] if t < 2 else ctx[:, t - 2, :], rstd[:, t:t + 1], None,
                   MUL).then_inc(S("xh"), 1)
            v.wait_ge(S("one_ps"), 1)
            link(nc.vector.tensor_copy(col, ps[0][:, 0:NROWS]))
            v.wait_ge(S("fold_ps"), 4)
            link(tt(mod[:, 0:16, :], ps[1][:, 0:32].rearrange("p (j c) -> p j c", c=2),
                    wide(V("b_ada", 0, 16), 2), ADD))
            link(ts(scale1[:, :, :], mod[:, 8:16, :], 1.0, None, ADD))
            tt(scale1[:, :, :], scale1[:, :, :], wide(V("norm1", 0, 8), 2), MUL).then_inc(S("mod"), 1)
            v.wait_ge(S("mod"), 1)
            for k in range(1, KD, 2):
                v.wait_ge(S("ht_ps"), k + 1)
                for c in range(2):
                    ins = ts(hT[:, k, c * L:(c + 1) * L], ps[4 + k % 4][:, c * L:(c + 1) * L],
                             scale1[:, k, c:c + 1], mod[:, k, c:c + 1], MUL, ADD)
                ins.then_inc(S("ht_v"), 1)

            def rows_out(r):
                v.wait_ge(S("tr_ps"), r + 1)
                dest = vN[:, :, r * P:(r + 1) * P] if r < 4 else xsN[:, :, (r - 4) * P:(r - 3) * P] if r < 8 \
                    else BN[:, :, (r - 8) * P:(r - 7) * P]
                nc.vector.tensor_copy(dest, tiles(ps[6 + r % 2][:, :], 4)).then_inc(S("tr_ev"), 1)

            def kq_unit(n):
                v.wait_ge(S("kq_root"), n + 1)
                link(nc.vector.reciprocal(root[n % 2], root[n % 2]))
                tt(kq_block(n), kq_block(n), root[n % 2], MUL).then_inc(S("kq_norm"), 1)

            for i in range(20):
                w, taps, _, _ = item(i)
                segs = w // L
                v.wait_ge(S("conv_a"), i + 1)
                b = ps[4 + i % 2][:, 0:w].rearrange("p (s t) -> p s t", s=segs)
                o_ = cconv[i % 2][:, 0:w].rearrange("p (s t) -> p s t", s=segs)
                link(stt(o_[:, :, 1:L], b[:, :, 0:L - 1], col[:, taps[0]:taps[0] + 1], o_[:, :, 1:L], MUL, ADD))
                stt(o_[:, :, 0:L - 1], b[:, :, 1:L], col[:, taps[2]:taps[2] + 1], o_[:, :, 0:L - 1], MUL,
                    ADD).then_inc(S("conv_v"), 1)
                if 7 <= i < 17:
                    rows_out(i - 7)
                if i == 5:
                    v.wait_ge(S("fold_ps"), 5)
                    nc.vector.tensor_copy(gx, ps[1][:, 128:256].rearrange("p (t n) -> p t n", t=4)) \
                        .then_inc(S("v_early"), 1)
                if i in SQ_AT:
                    kq_unit(SQ_AT.index(i))
            v.wait_ge(S("v_early"), 2)
            v.wait_ge(S("in_rest"), 32)
            link(tt(gx[:, :, 0:24], gx[:, :, 0:24], each(R("dtb", 24), 4), ADD))
            link(ts(gtmp[:, :, :], gx[:, :, 0:24], -1.0, None, MUL))
            link(tt(gtmp[:, :, :], gtmp[:, :, :], gx[:, :, 0:24], ALU.min))
            ts(beta[:, :, :], gx[:, :, 24:32], -1.0, None, MUL).then_inc(S("exp_arg"), 1)
            kq_unit(4)
            kq_unit(5)
            v.wait_ge(S("exp_done"), 2)
            link(ts(gx[:, :, 0:24], gx[:, :, 0:24], 0.0, None, ALU.max))
            link(tt(dtv[:, :, :], gx[:, :, 0:24], gtmp[:, :, :], ADD))
            link(ts(nega, nega, -1.0, None, MUL))
            tt(G[:, :, :], dtv[:, :, :], each(nega, 4), MUL).then_inc(S("v_early"), 1)
            link(ts(beta[:, :, :], beta[:, :, :], 1.0, None, ADD))
            link(nc.vector.reciprocal(beta[:, :, :], beta[:, :, :]))
            link(ts(nbeta[:, :, :], beta[:, :, :], -1.0, None, MUL))
            v.wait_ge(S("one_ps"), 2)
            link(nc.vector.tensor_copy(gc[:, :, :], tiles(ps[2][:, 0:96], 4)))
            link(nc.vector.tensor_copy(etot[:, :, :], tiles(ps[2][:, 128:224], 4)))
            tt(kd[:, :, :], etot[:, :, :], gc[:, :, :], SUB).then_inc(S("exp_arg"), 1)
            v.wait_ge(S("exp_done"), 3)
            link(tt(dtkd[:, :, :], dtv[:, :, :], kd[:, :, :], MUL))
            v.wait_ge(S("one_ps"), 3)
            nc.vector.tensor_copy(CBs, pD[0][:, :].rearrange("p (t g i) -> p t g i", t=T, g=2)) \
                .then_inc(S("gates"), 1)
            v.wait_ge(S("fold_ps"), 13)
            link(tt(mod[:, 16:48, :], ps[1][:, 32:96].rearrange("p (j c) -> p j c", c=2),
                    wide(V("b_ada", 16, 32), 2), ADD))
            link(ts(scale2, mod[:, 32:40, 0], 1.0, None, ADD))
            tt(scale2, scale2, V("norm2", 0, 8), MUL).then_inc(S("mod"), 1)
            v.wait_ge(S("gates"), 1)
            v.wait_ge(S("state0"), 1)

            def piece(u, d, kind):
                t, c = tile_of(u, d), 12 * d + 4
                if kind in "ab":
                    k = 0 if kind == "a" else 4
                    m = 2 * (2 * (u - 2) + d) + (1 if kind == "b" else 0)
                    v.wait_ge(S("wg_ps"), m + 1)
                    for h in range(4):
                        ins = ts(Ws[:, k + h, :], pD[d][:, h * P:(h + 1) * P], gc[:, t, c + k + h:c + k + h + 1], 0.0,
                                 SUB, ALU.min)
                    ins.then_inc(S("ws_arg"), 1)
                elif kind == "e":
                    m = 2 * u + d
                    if u >= 2:
                        v.wait_ge(S("yo_ps"), 2 * (u - 2) + d + 1)
                        tt(heads(yoff, 8, SP_), heads(pD[d][:, :], 8, SP_), wide(egc[:, t, c:c + 8], SP_), MUL) \
                            .then_inc(S("yo_rd"), 1)
                        v.wait_ge(S("yo_rd"), 2 * (u - 2) + d + 1)
                        if first(u, d):
                            link(tt(heads(yacc[:, t, :], 8, SP_), heads(xsN[:, t, :], 8, SP_),
                                    wide(R("ssmD", 8), SP_), MUL))
                        link(tt(yacc[:, t, :], yacc[:, t, :], yoff, ADD))
                    link(tt(heads(ht[:, d, :], 8, SP_), heads(ht[:, d, :], 8, SP_), wide(etot[:, t, c:c + 8], SP_),
                            MUL))
                    v.wait_ge(S("hs_ps"), m + 1)
                    tt(ht[:, d, :], ht[:, d, :], pD[d][:, :], ADD).then_inc(S("h_ready"), 1)
                else:
                    m = 2 * (u - 2) + d
                    v.wait_ge(S("ws_mask"), m + 1)
                    for k in range(2):
                        ins = tt(Ws[:, 4 * k:4 * k + 4, :], Ws[:, 4 * k:4 * k + 4, :], each(CBs[:, t, k, :], 4), MUL)
                    ins.then_inc(S("ws_ready"), 1)
                    v.wait_ge(S("yd_ps"), m + 1)
                    tt(yacc[:, t, :], yacc[:, t, :], pD[d][:, :], ADD).then_inc(S("yd_rd"), 1)
                    v.wait_ge(S("yd_rd"), m + 1)

            def first(u, d):
                return u == 2

            def make(u, d, kind):
                t = tile_of(u, d)
                bank = prep_bank(u, d, kind)
                v.wait_ge(S("prep_ps"), step(u, d, kind))
                if kind == "g":
                    for h in range(4):
                        ins = ts(E[d][:, h, :], bank[:, h * P:(h + 1) * P], gc[:, t, 12 * d + h:12 * d + h + 1], 0.0,
                                 SUB, ALU.min)
                    ins.then_inc(S("prep"), 1)
                elif kind == "n":
                    v.wait_ge(S(f"e_exp{d}"), u + 1)
                    for h in range(4):
                        ins = stt(NTu[u % 2][d][:, h, :], bank[:, h * P:(h + 1) * P],
                                  nbeta[:, t, 4 * d + h:4 * d + h + 1], E[d][:, h, :], MUL, MUL)
                    ins.then_inc(S("prep"), 1)
                else:
                    tt(PTu[u % 2][d], tiles(bank[:, :], 4), E[d], MUL).then_inc(S("prep"), 1)

            def level0(u):
                for d in range(2):
                    v.wait_ge(S(f"mn{d}"), u * LEVELS + 1)
                    v.wait_ge(S(f"p_ps{d}"), u * LEVELS + 1)
                    tt(X[d], tiles(pD[d][:, :], 4), each(ident, 4), ADD)
                    tt(XT[d], Mn[d][0], each(ident, 4), ADD).then_inc(S(f"x{d}"), 1)

            for st in STEPS[:4]:
                make(*st)
            level0(0)
            for u in range(4):
                for l in range(1, LEVELS):
                    for d, kind in pieces(u, l):
                        piece(u, d, kind)
                    for st in prepare(u + 1, l):
                        make(*st)
                    for d in range(2):
                        v.wait_ge(S(f"x{d}"), u * LEVELS + l)
                        v.wait_ge(S(f"q_ps{d}"), u * (LEVELS - 1) + l)
                        if l < LEVELS - 1:
                            tt(X[d], X[d], tiles(pB[d][:, :], 4), ADD).then_inc(S(f"x{d}"), 1)
                        else:
                            tt(XT[d], XT[d], tiles(pC[d][:, :], 4), ADD).then_inc(S(f"x{d}"), 1)
                for d in range(2):
                    t = tile_of(u, d)
                    v.wait_ge(S(f"ks_ps{d}"), u + 1)
                    if u < 3:
                        v.wait_ge(S("prep"), last_step(u + 1, d))
                    link(tt(E[d], tiles(pA[d][:, :], 4), wide(egc[:, t, 12 * d:12 * d + 4], P), MUL))
                    tt(E[d], heads(vN[:, t, :], 4, P), E[d], SUB).then_inc(S(f"r{d}"), 1)

                def decay_state(d):
                    link(tt(St[:, d, :, :], St[:, d, :, :], wide(etot[:, tile_of(u, d), 12 * d:12 * d + 4], P), MUL))

                if u < 2:
                    for d in range(2):
                        decay_state(d)
                for d in range(2):
                    t = tile_of(u, d)
                    v.wait_ge(S(f"vn_ps{d}"), u + 1)
                    tt(vnew[d], tiles(pB[d][:, :], 4), wide(beta[:, t, 4 * d:4 * d + 4], P), MUL) \
                        .then_inc(S(f"vnew{d}"), 1)
                if u < 3:
                    level0(u + 1)
                for d in range(2):
                    t = tile_of(u, d)
                    if u >= 2:
                        v.wait_ge(S(f"o_ps{d}"), u - 1)
                        link(tt(E[d], tiles(pC[d][:, :], 4), wide(egc[:, t, 12 * d:12 * d + 4], P), MUL))
                        o4 = heads(oacc[:, t, :], 4, P)
                        if first(u, d):
                            tt(o4, E[d], tiles(pA[d][:, :], 4), ADD).then_inc(S(f"s{d}"), 1)
                            decay_state(d)
                        else:
                            link(tt(E[d], E[d], tiles(pA[d][:, :], 4), ADD))
                            link(tt(o4, o4, E[d], ADD))
                    if u < 3:
                        v.wait_ge(S(f"s_ps{d}"), u + 1)
                        tt(St[:, d, :, :], St[:, d, :, :], tiles(pB[d][:, :], 4), ADD).then_inc(S(f"s{d}"), 1)
            sq = tiles(scratch(0, 1024), 2)
            v.wait_ge(S("o_ps0"), 2)
            v.wait_ge(S("o_ps1"), 2)
            v.wait_ge(S("y_sq"), 2)
            ts(stat[:, 8:10], stat[:, 8:10], 1.0 / 512, EPS, MUL, ADD).then_inc(S("mean"), 1)
            for t in range(T):
                link(tt(sq[:, t, :], oacc[:, t, :], oacc[:, t, :], MUL))
            link(nc.vector.tensor_reduce(stat[:, 0:8], sq.rearrange("p t (h e) -> p (t h) e", h=4), AX, ADD))
            ts(stat[:, 0:8], stat[:, 0:8], 1.0 / P, EPS, MUL, ADD).then_inc(S("mean"), 1)
            v.wait_ge(S("root"), 1)
            link(nc.vector.reciprocal(rstd[:, 8:10], rstd[:, 8:10]))
            for t in range(T):
                ts(yacc[:, t, :], yacc[:, t, :], rstd[:, 8 + t:9 + t], None, MUL).then_inc(S("normed"), 1)
            v.wait_ge(S("root"), 2)
            link(nc.vector.reciprocal(rstd[:, 0:8], rstd[:, 0:8]))
            for t in range(T):
                link(tt(heads(oacc[:, t, :], 4, P), heads(oacc[:, t, :], 4, P), wide(rstd[:, 4 * t:4 * t + 4], P), MUL))
                tt(oacc[:, t, :], oacc[:, t, :], Z[:, t, 0:512], MUL).then_inc(S("normed"), 1)
            for i in range(4):
                v.wait_ge(S("dg_ps"), i + 1)
                nc.vector.tensor_copy((g1r if i < 2 else g2r)[:, 512 * (i % 2):512 * (i % 2) + 512],
                                      ps[(0, 1, 6, 7)[i]][:, :]).then_inc(S("gain_rows"), 1)
            v.wait_ge(S("gain_rows"), 4)

            def residual(name, order, gain, before):
                for i, (bank, t, c) in enumerate(order):
                    v.wait_ge(S(name), before + i + 1)
                    xs = x[:, t, 512 * c:512 * c + 512]
                    if gain is None:
                        tt(xs, xs, ps[bank][:, :], ADD).then_inc(S("x_step"), 1)
                    else:
                        link(tt(tmpx[i % 2], ps[bank][:, :], gain[:, 512 * c:512 * c + 512], MUL))
                        tt(xs, xs, tmpx[i % 2], ADD).then_inc(S("x_step"), 1)

            residual("wo_ps", [(4 + 2 * c + t, t, c) for c in range(2) for t in range(2)], g1r, 0)
            rms(1)
            for t in range(T):
                ts(xh[:, t, :], x[:, t, :], rstd[:, t:t + 1], None, MUL).then_inc(S("xh"), 1)

            def ffn_hid(b):
                v.wait_ge(S("f_silu"), b + 1)
                v.wait_ge(S("up_ps"), b + 1)
                tt(hid[:, b, :], fs[b % 2], ps[2 + b % 2][:, 0:L], MUL).then_inc(S("f_hid"), 1)

            for b in range(KF):
                v.wait_ge(S("f_mid"), b + 1)
                src = ps[b % 2][:, 0:L].rearrange("p (r c) -> p r c", c=GRID)
                dst = fa[b % 2].rearrange("p (r c) -> p r c", c=GRID)
                nr = L // GRID
                for j in range(9):
                    if j == 4:
                        continue
                    dy, dx = j // 3 - 1, j % 3 - 1
                    r0, r1, c0, c1 = max(0, -dy), nr - max(0, dy), max(0, -dx), GRID - max(0, dx)
                    o_ = dst[:, r0:r1, c0:c1]
                    ins = stt(o_, src[:, r0 + dy:r1 + dy, c0 + dx:c1 + dx], V("fconv", j * KF + b), o_, MUL, ADD)
                    if j < 8:
                        link(ins)
                    else:
                        ins.then_inc(S("f_taps"), 1)
                if b >= 1:
                    ffn_hid(b - 1)
            ffn_hid(KF - 1)
            residual("down_ps", [(4 + 2 * t + c, t, c) for t in range(2) for c in range(2)], g2r, 5)
            rms(2)
            v.wait_ge(S("x_step"), 8)
            v.wait_ge(S("in_rows"), 64)
            for t in range(T):
                stt(x[:, t, :], x[:, t, :], rstd[:, t:t + 1], fng1, MUL, MUL).then_inc(S("x_step"), 1)
            rms(3)
            v.wait_ge(S("x_step"), 10)
            for t in range(T):
                ts(xh[:, t, :], x[:, t, :], rstd[:, t:t + 1], None, MUL).then_inc(S("xh"), 1)
            v.wait_ge(S("in2_ev"), 4)
            for t in range(T):
                link(tt(rota[:, t, :], pj[:, t, 0:640], pj[:, t, 0:640], MUL))
                link(nc.vector.tensor_reduce(stat[:, 10 * t:10 * t + 10], heads(rota[:, t, :], 10, HD), AX, ADD))
            ts(stat[:, 0:20], stat[:, 0:20], 1.0 / HD, EPS, MUL, ADD).then_inc(S("mean"), 1)
            v.wait_ge(S("root"), 3)
            link(nc.vector.reciprocal(rstd[:, 0:20], rstd[:, 0:20]))
            for t in range(T):
                qa, ka = heads(pj[:, t, 0:512], 8, HD), heads(pj[:, t, 512:640], 2, HD)
                all_ = pj[:, t, 0:640]
                link(tt(heads(all_, 10, HD), heads(all_, 10, HD), wide(rstd[:, 10 * t:10 * t + 10], HD), MUL))
                link(tt(qa, qa, each(R("qn", HD), 8), MUL))
                link(tt(ka, ka, each(R("kn", HD), 2), MUL))
                s4 = all_.rearrange("p (h a e) -> p h a e", h=10, a=2)
                r4 = rota[:, t, :].rearrange("p (h a e) -> p h a e", h=10, a=2)
                cos, sin = rope(0, t)
                for a in range(2):
                    link(tt(r4[:, :, a, :], s4[:, :, 1 - a, :], each(sin[:, 32 * a:32 * a + 32], 10), MUL))
                link(tt(heads(all_, 10, HD), heads(all_, 10, HD), each(cos, 10), MUL))
                tt(all_, all_, rota[:, t, :], ADD).then_inc(S("rot_a"), 1)
            v.wait_ge(S("in_rows"), 64)
            def over_sum(h):
                v.wait_ge(S("s_exp"), 2 * h + 2)
                link(nc.vector.reciprocal(sm[:, h, :], sm[:, h, :]))
                for t in range(T):
                    ins = ts(pr[h % 2][:, t, :], pr[h % 2][:, t, :], sm[:, h, t:t + 1], None, MUL)
                ins.then_inc(S("pr"), 1)

            for h in range(16):
                v.wait_ge(S("s_ps"), h + 1)
                if h < 8:
                    link(nc.vector.tensor_reduce(mx[:, h, :], tiles(ps[h % 2][:, :], 2), AX, ALU.max, negate=True))
                    ts(mx[:, h, :], mx[:, h, :], SCALE, None, MUL).then_inc(S("s_max"), 1)
                else:
                    v.wait_ge(S("s_exp"), 2 * h - 2)
                    link(stt(sc[h % 2], tiles(ps[h % 2][:, :], 2), SCALE, bias, MUL, ADD))
                    nc.vector.tensor_reduce(mx[:, h, :], sc[h % 2], AX, ALU.max, negate=True) \
                        .then_inc(S("s_max"), 1)
                if h >= 1:
                    over_sum(h - 1)
            over_sum(15)
            v.wait_ge(S("ss_ps"), 1)
            ts(tmpx[0], ps[0][:, :], 1.0 / 512, EPS, MUL, ADD).then_inc(S("mean"), 1)
            v.wait_ge(S("root"), 4)
            for k in range(KD):
                if k % 4 == 0:
                    half = tmpx[0][:, L * (k // 4):L * (k // 4) + L]
                    link(nc.vector.reciprocal(half, half))
                stt(uT[:, k, :], ps[4 + k // 2][:, L * (k % 2):L * (k % 2) + L], V("outab", k),
                    tmpx[0][:, L * (k // 4):L * (k // 4) + L], MUL, MUL).then_inc(S("o_norm"), 1)
            residual("wo2_ps", [(2 * c + t, t, c) for c in range(2) for t in range(2)], None, 0)
            rms(4)
            v.wait_ge(S("x_step"), 14)
            for t in range(T):
                ts(xh[:, t, :], x[:, t, :], rstd[:, t:t + 1], None, MUL).then_inc(S("xh"), 1)
            v.wait_ge(S("xh"), 10)
            v.wait_ge(S("in_rows"), 64)
            for t in range(T):
                tt(u2[:, t, :], xh[:, t, :], n2row, MUL).then_inc(S("u2"), 1)
            desc, iota = C("desc", NE), C("iota", SLOT)

            def one_hot(dst, src, top, w):
                e1 = ra[4][:, :, 0:w]
                link(nc.vector.tensor_reduce(top, src, AX, ALU.max))
                link(tt(e1, src, wide(top, w), ALU.is_equal))
                link(tt(e1, e1, each2(desc[:, 0:w]), MUL))
                link(nc.vector.tensor_reduce(rs[:, 7, :], e1, AX, ALU.max))
                link(tt(dst, e1, wide(rs[:, 7, :], w), ALU.is_equal))

            def each2(row):
                return row.unsqueeze(1).to_broadcast([P, 2, row.shape[1]])

            v.wait_ge(S("one_ps"), 4)
            link(tt(lg[:, :, :], tiles(ps[0][:, 0:72], 2), each2(R("rb", 36)), ADD))
            gm, el, oh1, oh2 = ra[1][:, :, 0:4], ra[2], ra[3], ra[5]
            one_hot(gm, lg[:, :, 0:4], rs[:, 0, :], 4)
            link(tt(ra[0][:, :, 0:4], lg[:, :, 0:4], wide(rs[:, 0, :], 4), SUB))
            for t in range(T):
                link(tt(heads(el[:, t, :], 4, 8), heads(lg[:, t, 4:36], 4, 8), wide(gm[:, t, :], 8), MUL))
            link(ts(gm, gm, -1.0, 1e30, ADD, MUL))
            for t in range(T):
                link(tt(heads(el[:, t, :], 4, 8), heads(el[:, t, :], 4, 8), wide(gm[:, t, :], 8), ADD))
            one_hot(oh1, el, rs[:, 1, :], NE)
            link(stt(el.rearrange("p t n -> p (t n)"), oh1.rearrange("p t n -> p (t n)"), -3e38,
                     el.rearrange("p t n -> p (t n)"), MUL, ADD))
            one_hot(oh2, el, rs[:, 2, :], NE)
            tt(rs[:, 5, :], rs[:, 2, :], rs[:, 1, :], SUB).then_inc(S("exp_arg"), 1)
            v.wait_ge(S("exp_done"), 4)
            link(nc.vector.tensor_reduce(rs[:, 3, :], ra[0][:, :, 0:4], AX, ADD))
            link(ts(rs[:, 4, :], rs[:, 5, :], 1.0, None, ADD))
            link(tt(rs[:, 3, :], rs[:, 3, :], rs[:, 4, :], MUL))
            link(nc.vector.reciprocal(rs[:, 3, :], rs[:, 3, :]))
            link(tt(rs[:, 4, :], rs[:, 3, :], rs[:, 5, :], MUL))
            flag = ra[4]
            tt(flag, oh1, oh2, ADD).then_inc(S("flag"), 1)
            link(nc.vector.memset(SL[:, :, :], -1.0))
            link(nc.vector.memset(GT[:, :, :], 0.0))
            link(tt(oh1, oh1, wide(rs[:, 3, :], NE), MUL))
            link(tt(oh2, oh2, wide(rs[:, 4, :], NE), MUL))
            v.wait_ge(S("flag"), 1)
            v.wait_ge(S("one_ps"), 5)
            link(ts(el, tiles(ps[1][:, 0:64], 2), 1.0, None, ADD))
            link(tt(el, el, flag, MUL))
            link(tt(oh1, oh1, oh2, ADD))
            link(ts(SL[:, :, 0:NE], el, -1.0, None, ADD))
            link(nc.vector.tensor_copy(GT[:, :, 0:NE], oh1))
            def selection(chain, at, with_gate, name):
                chain(nc.vector.tensor_copy(cur[:, 0, :, :], SL[:, :, bass.ds(at, 2)]))
                if with_gate:
                    chain(nc.vector.tensor_copy(cur[:, 1, :, :], GT[:, :, bass.ds(at, 2)]))
                for t in range(T):
                    for e in range(2):
                        if with_gate:
                            ins = ts(gsel[:, t, e * SLOT:(e + 1) * SLOT], iota, cur[:, 0, t, e:e + 1],
                                     cur[:, 1, t, e:e + 1], ALU.is_equal, MUL)
                        else:
                            ins = ts(sel[:, t, e * SLOT:(e + 1) * SLOT], iota, cur[:, 0, t, e:e + 1], None,
                                     ALU.is_equal)
                ins.then_inc(S(name), 1)

            link(nc.vector.tensor_copy(cnt[:, 0:32], ps[1][:, 64:96]))
            LINKS = 3
            m = [0]

            def chain(ins, p=0):
                m[0] += 1
                ins.then_inc(S("dve_loop"), 1)
                v.wait_ge(S("dve_loop"), p * LINKS + m[0])

            selection(link, 0, False, "sel")
            v.wait_ge(S("sel"), 1)
            selection(chain, 0, True, "gsel")
            for r in range(3):
                link(ts(over[:, NE * r:NE * r + NE], cnt[:, 0:32], float(SLOT * (r + 1)), None, ALU.is_gt))
            link(nc.vector.tensor_reduce(cnt[:, 32:33], over, AX, ADD))
            a_, b_ = over, scanA
            for i in range(7):
                w = 2 ** i
                link(nc.vector.tensor_copy(b_[:, 0:w], a_[:, 0:w]))
                link(tt(b_[:, w:96], a_[:, w:96], a_[:, 0:96 - w], ADD))
                a_, b_ = b_, scanB if b_ is scanA else scanA
            link(ts(a_, a_, float(NE - 1), None, ADD))
            link(tt(a_, a_, over, MUL))
            p3 = place.rearrange("p (u n) -> p u n", u=EXTRA)
            link(tt(p3, each(a_, EXTRA), wide(iota[:, NE:NU], 96), ALU.is_equal))
            p4 = place.rearrange("p (u b e) -> p u b e", u=EXTRA, b=3)
            link(tt(ofexp, p4[:, :, 0, :], p4[:, :, 1, :], ADD))
            link(tt(ofexp, ofexp, p4[:, :, 2, :], ADD))
            link(nc.vector.tensor_reduce(blk.rearrange("p u b -> p (u b)"),
                                         place.rearrange("p (n e) -> p n e", e=NE), AX, ADD))
            link(ts(unitB, blk[:, :, 0], float(SLOT), None, MUL))
            link(stt(unitB, blk[:, :, 1], 2.0 * SLOT, unitB, MUL, ADD))
            link(stt(unitB, blk[:, :, 2], 3.0 * SLOT, unitB, MUL, ADD))
            link(tt(pick, ofexp, each(iota[:, 0:NE], EXTRA), MUL))
            link(nc.vector.tensor_reduce(unitE, pick, AX, ADD))
            for t in range(T):
                link(tt(pick, ofexp, each(el[:, t, :], EXTRA), MUL))
                link(nc.vector.tensor_reduce(SL[:, t, NE:NU], pick, AX, ADD))
                link(ts(SL[:, t, NE:NU], SL[:, t, NE:NU], -1.0, None, ADD))
                link(tt(SL[:, t, NE:NU], SL[:, t, NE:NU], unitB, SUB))
                link(tt(pick, ofexp, each(oh1[:, t, :], EXTRA), MUL))
                link(nc.vector.tensor_reduce(GT[:, t, NE:NU], pick, AX, ADD))
            link(nc.vector.tensor_copy(units[:, 0:NE], iota[:, 0:NE]))
            link(nc.vector.tensor_copy(units[:, NE:NU], unitE))
            for r in range(4):
                link(ts(cnt[:, 33 + r:34 + r], cnt[:, 32:33], float(2 * r), None, ALU.is_gt))
            link(nc.vector.tensor_reduce(cnt[:, 37:38], cnt[:, 33:37], AX, ADD))
            ts(units[:, NU:NU + 1], cnt[:, 37:38], float(NPAIR), None, ADD).then_inc(S("count_ready"), 1)

            def pair(p):
                v.wait_ge(S("sg"), p + 1)
                v.wait_ge(S("eu_ps"), p + 1)
                tt(hidN, sg, ps[4][:, :], MUL).then_inc(S("hid"), 1)
                v.wait_ge(S("gather_ps"), p + 2)
                nc.vector.tensor_copy(xsel[:, 4:8, :], tiles(ps[7][:, :], 4)).then_inc(S("xsel_v"), 1)
                v.wait_ge(S("yn_ps"), 2 * p + 2)
                nc.vector.tensor_copy(yN[:, 512:1024], ps[4][:, :]).then_inc(S("yn_v"), 1)
                v.wait_ge(S("gt_ps"), p + 1)
                nc.vector.tensor_copy(gselT, ps[6][:, 0:256]).then_inc(S("gt_ev"), 1)

            v.wait_ge(S("gsel"), 1)
            v.wait_ge(S("gather_ps"), 1)
            selection(chain, 2, False, "sel")
            assert m[0] == LINKS
            pair(0)
            v.wait_ge(S("count_ready"), 1)
            npairs = v.value_load(units[0:1, NU:NU + 1], min_val=NPAIR, max_val=NU // 2)
            with v.Fori(1, npairs) as p:
                m[0] = 0
                v.wait_ge(S("sel"), p + 1)
                selection(lambda ins: chain(ins, p), 2 * p, True, "gsel")
                v.wait_ge(S("gsel"), p + 1)
                selection(lambda ins: chain(ins, p), 2 * p + 2, False, "sel")
                assert m[0] == LINKS
                pair(p)
            for t in range(T):
                for c in range(2):
                    v.wait_ge(S("sc_ps"), 2 * t + c + 1)
                    xs = x[:, t, 512 * c:512 * c + 512]
                    tt(xs, xs, ps[2 * t + c][:, :], ADD).then_inc(S("x_step"), 1)
            rms(5)
            v.wait_ge(S("x_step"), 18)
            for t in range(T):
                stt(x[:, t, :], x[:, t, :], rstd[:, t:t + 1], fng2, MUL, MUL).then_inc(S("out_ready"), 1)

        @block.tensor
        def _(pe):
            mm, tr = nc.tensor.matmul, nc.tensor.transpose

            def rows(j, left, right):
                if j >= 2:
                    pe.wait_ge(S("rows_ev"), j - 1)
                for m in range(2):
                    for g in range(4):
                        ins = mm(ps[2 * (j % 2)][32 * g:32 * g + 32, :], left(2 * g + m), right(2 * g + m),
                                 start=(m == 0), stop=(m == 1), tile_position=(0, 32 * g))
                ins.then_inc(S("rows_ps"), 1)

            def fold(j, at, n):
                pe.wait_ge(S("rows_ev"), j + 1)
                for b in range(4):
                    ins = mm(ps[1][:, at + b * n:at + (b + 1) * n], arow[j % 2][:, b * P:(b + 1) * P],
                             C("fold", 32)[:, 0:n], start=True, stop=True)
                ins.then_inc(S("fold_ps"), 1)

            def ada(i):
                w = arrived(pe, ada_ch[i])
                j = i if i < 4 else i + 1
                rows(j, lambda k: csil[:, k, :], lambda k: w[:, k, :])
                if i == 5:
                    pe.wait_ge(S("v_early"), 2)
                if i not in (0, 4):
                    ada_fold(i - 1)

            def ada_fold(i):
                fold(i if i < 4 else i + 1, 8 * i, 2)

            def h_block(k):
                if k >= 4:
                    ht_read(k - 4)
                for t in range(4):
                    ins = tr(ps[4 + k % 4][:, t * P:(t + 1) * P], xn[:, t, k * P:(k + 1) * P], ident)
                ins.then_inc(S("ht_ps"), 1)

            def ht_read(k):
                pe.wait_ge(S("ht_v" if k % 2 else "ht_ev"), k // 2 + 1)

            pe.wait_ge(S("c_silu"), 1)
            ada(0)
            pe.wait_ge(S("in_consts"), 16)
            ada(1)
            ada(2)
            pe.wait_ge(S("xh"), 4)
            for k in range(4):
                h_block(k)
            ada(3)
            pe.wait_ge(S("in_vecs"), 16)
            pe.wait_ge(S("rows_ev"), 3)
            for i in range(3):
                ins = tr(ps[0][:, i * P:(i + 1) * P], vecs[:, i * P:(i + 1) * P], ident)
            ins.then_inc(S("one_ps"), 1)
            ada_fold(3)
            for k in range(4, KD):
                h_block(k)
            for k in range(KD - 2, KD):
                ht_read(k)
            pe.wait_ge(S("in_rest"), 32)
            rows(4, lambda k: wsm[:, k, :], lambda k: hT[:, k, :])

            def rows_in(i):
                r = i - 4
                pe.wait_ge(S("item_silu"), i + 1)
                if r >= 2:
                    pe.wait_ge(S("tr_ev"), r - 1)
                src = item(i)[3]
                for t in range(4):
                    ins = tr(ps[6 + r % 2][:, t * P:(t + 1) * P], src[:, t * P:(t + 1) * P], ident)
                ins.then_inc(S("tr_ps"), 1)

            for i in range(24):
                if i in (0, 4, 8, 12, 16, 20, 22):
                    c = PEND.index(min(e for e in PEND if e > i))
                    if i:
                        ada(3 + c)
                    if i == 4:
                        fold(4, 128, 32)
                    w = arrived(pe, proj_ch[c])
                    first_item = i
                if 2 <= i < 22:
                    pe.wait_ge(S("conv_v"), i - 1)
                elif i >= 22:
                    pe.wait_ge(S("z_ev"), i - 21)
                if i < 20:
                    n = item(i)[0]
                    j = i - first_item
                    if PROJ[c] == WBC:
                        j = i - 12
                    for k in range(KD):
                        ins = mm(ps[4 + i % 2][:, 0:n], w[:, k, j * P:(j + 1) * P], hT[:, k, 0:n],
                                 start=(k == 0), stop=(k == KD - 1))
                else:
                    t = i % 2
                    for k in range(KD):
                        ins = mm(ps[4 + i % 2][:, :], hT[:, k, t * P:(t + 1) * P], w[:, k, :],
                                 start=(k == 0), stop=(k == KD - 1))
                ins.then_inc(S("item_ps"), 1)
                if 6 <= i < 16:
                    rows_in(i - 2)
                if i in SQ_AT:
                    n = SQ_AT.index(i)
                    pe.wait_ge(S("sq_ready"), n + 1)
                    if n >= 1:
                        pe.wait_ge(S("kq_root"), n)
                    mm(ps[3][:, :], ones, sqb[n % 2], start=True, stop=True).then_inc(S("sq_ps"), 1)
                if i >= 20:
                    r = i - 20
                    pe.wait_ge(S("kq_norm"), r + 1)
                    if r < 2:
                        pe.wait_ge(S("tr_ev"), 9 + r)
                    else:
                        pe.wait_ge(S("kn_ev"), r - 1)
                    for t in range(4):
                        ins = tr(ps[6 + r % 2][:, t * P:(t + 1) * P], kT[:, r, t * P:(t + 1) * P], ident)
                    ins.then_inc(S("tr_ps"), 1)
            ada(10)
            ada(11)
            ada_fold(11)
            pe.wait_ge(S("v_early"), 3)
            pe.wait_ge(S("kq_root"), 6)
            pe.wait_ge(S("rows_ev"), 13)
            for t in range(4):
                for d in range(2):
                    mm(ps[2][:, t * 24 + d * 12:t * 24 + d * 12 + 12], mask[d], G[:, t, d * 12:d * 12 + 12],
                       start=True, stop=True)
            mm(ps[2][:, 128:224], ones, G[:, :, :].rearrange("p t n -> p (t n)"), start=True, stop=True) \
                .then_inc(S("one_ps"), 1)
            for t in range(T):
                for g in range(2):
                    ins = mm(pD[0][:, (2 * t + g) * P:(2 * t + g + 1) * P], BT[:, g, t * P:(t + 1) * P],
                             CT[:, g, t * P:(t + 1) * P], start=True, stop=True)
            ins.then_inc(S("one_ps"), 1)
            pe.wait_ge(S("gates"), 1)
            pe.wait_ge(S("mod"), 2)
            pe.wait_ge(S("state0"), 1)
            pe.wait_ge(S("kn_ev"), 4)
            pe.wait_ge(S("kq_norm"), 6)

            def sums_over(bank, t, c):
                d = 0 if c < 12 else 1
                for h in range(4):
                    ins = mm(bank[:, h * P:(h + 1) * P], G[:, t, c + h:c + h + 1].to_broadcast([P, P]), mask[d],
                             start=True, stop=True)
                return ins

            def piece(u, d, kind):
                t, c = tile_of(u, d), 12 * d + 4
                if kind in "ab":
                    m = 2 * (2 * (u - 2) + d) + (1 if kind == "b" else 0)
                    if kind == "a" and d == 1 and u < 3:
                        pe.wait_ge(S("prep"), last_step(u + 1, 1))
                    if kind == "a" and m:
                        pe.wait_ge(S("yd_rd"), 2 * (u - 2) + d)
                    if kind == "a":
                        pe.wait_ge(S("h_ready"), 2 * u + (0 if d == 0 else 1))
                    else:
                        pe.wait_ge(S("ws_arg"), m)
                    sums_over(pD[d], t, c + (4 if kind == "b" else 0)).then_inc(S("wg_ps"), 1)
                elif kind == "e":
                    m = 2 * u + d
                    if u < 2 and d == 1:
                        pe.wait_ge(S("prep"), last_step(u + 1, 1))
                    if m >= 2:
                        pe.wait_ge(S("h_ready"), m - 1 if u < 2 else m)
                    if u >= 2:
                        pe.wait_ge(S("ws_arg"), 2 * (2 * (u - 2) + d + 1))
                        for g in range(2):
                            ins = mm(pD[d][:, g * L:(g + 1) * L], CT[:, g, t * P:(t + 1) * P],
                                     ht[:, d, g * L:(g + 1) * L], start=True, stop=True)
                        ins.then_inc(S("yo_ps"), 1)
                        pe.wait_ge(S("yo_rd"), 2 * (u - 2) + d + 1)
                    pe.wait_ge(S("xde_ready"), m + 1)
                    for g in range(2):
                        ins = mm(pD[d][:, g * L:(g + 1) * L], BN[:, t, g * P:(g + 1) * P],
                                 xde[:, g * L:(g + 1) * L], start=True, stop=True)
                    ins.then_inc(S("hs_ps"), 1)
                else:
                    pe.wait_ge(S("h_ready"), 2 * u + d + 1)
                    pe.wait_ge(S("ws_ready"), 2 * (u - 2) + d + 1)
                    pe.wait_ge(S("xdt_ready"), 2 * (u - 2) + d + 1)
                    for h in range(8):
                        ins = mm(pD[d][:, h * SP_:(h + 1) * SP_], Ws[:, h, :], xdt[:, h * SP_:(h + 1) * SP_],
                                 start=True, stop=True)
                    ins.then_inc(S("yd_ps"), 1)

            def four(bank, left, right):
                for h in range(4):
                    ins = mm(bank[:, h * P:(h + 1) * P], left(h), right(h), start=True, stop=True)
                return ins

            def make(u, d, kind):
                t = tile_of(u, d)
                at = slice(t * P, (t + 1) * P)
                bank = prep_bank(u, d, kind)
                if u >= 1:
                    if kind != "g":
                        pe.wait_ge(S("prep"), step(u, d, kind) - 1)
                    elif d == 0 and u < 3:
                        pe.wait_ge(S("h_ready"), 2 * (u - 1) + 1)
                    elif d == 0:
                        pe.wait_ge(S("yd_rd"), 1)
                if kind == "g":
                    ins = sums_over(bank, t, 12 * d)
                else:
                    ins = four(bank, lambda h: kT[:, h, at], lambda h: (kT if kind == "n" else qT)[:, h, at])
                ins.then_inc(S("prep_ps"), 1)

            def level0(u):
                for d in range(2):
                    pe.wait_ge(S(f"mn{d}"), u * LEVELS + 1)
                    pe.wait_ge(S("prep"), last_step(u, d))
                    if u in (1, 2) and d == 1:
                        pe.wait_ge(S("h_ready"), 2 * u)
                    if u == 3 and d == 1:
                        pe.wait_ge(S("yd_rd"), 2)
                    four(pD[d], lambda h: Mn[d][0][:, h, :], lambda h: ident).then_inc(S(f"p_ps{d}"), 1)

            for st in STEPS[:4]:
                make(*st)
            level0(0)
            for u in range(4):
                for l in range(1, LEVELS):
                    for d in range(2):
                        pe.wait_ge(S(f"mn{d}"), u * LEVELS + l + 1)
                        pe.wait_ge(S(f"x{d}"), u * LEVELS + l)
                        if u == 3 and l == 1:
                            pe.wait_ge(S(f"s{d}"), 3)
                        four(pA[d], lambda h: Mn[d][l % 2][:, h, :], lambda h: X[d][:, h, :]) \
                            .then_inc(S(f"p_ps{d}"), 1)
                        if l >= 2:
                            for h in range(4):
                                ins = tr(pC[d][:, h * P:(h + 1) * P], X[d][:, h, :], ident)
                            ins.then_inc(S(f"xt_ps{d}"), 1)
                    for d, kind in pieces(u, l):
                        piece(u, d, kind)
                    for st in prepare(u + 1, l):
                        make(*st)
                    for d in range(2):
                        pe.wait_ge(S(f"p_ev{d}"), u * (LEVELS - 1) + l)
                        if u and l == 1:
                            pe.wait_ge(S(f"s{d}"), u if u < 3 else 4)
                        if l >= 2:
                            pe.wait_ge(S(f"xt_ev{d}"), u * (LEVELS - 2) + l - 1)
                        if l < LEVELS - 1:
                            four(pB[d], lambda h: XT[d][:, h, :], lambda h: Pv[d][:, h, :]) \
                                .then_inc(S(f"q_ps{d}"), 1)
                        else:
                            four(pC[d], lambda h: Pv[d][:, h, :], lambda h: XT[d][:, h, :]) \
                                .then_inc(S(f"q_ps{d}"), 1)
                for d in range(2):
                    t = tile_of(u, d)
                    at = slice(t * P, (t + 1) * P)
                    four(pA[d], lambda h: kT[:, h, at], lambda h: St[:, d, h, :]).then_inc(S(f"ks_ps{d}"), 1)
                for d in range(2):
                    pe.wait_ge(S(f"r{d}"), u + 1)
                    pe.wait_ge(S(f"x{d}"), LEVELS * (u + 1))
                    four(pB[d], lambda h: XT[d][:, h, :], lambda h: E[d][:, h, :]).then_inc(S(f"vn_ps{d}"), 1)
                if u < 3:
                    level0(u + 1)
                for d in range(2):
                    t = tile_of(u, d)
                    at = slice(t * P, (t + 1) * P)
                    pe.wait_ge(S(f"vnew{d}"), u + 1)
                    if u >= 2:
                        pe.wait_ge(S(f"pt{d}"), u - 1)
                        four(pC[d], lambda h: qT[:, h, at], lambda h: St[:, d, h, :])
                        four(pA[d], lambda h: PTu[u % 2][d][:, h, :], lambda h: vnew[d][:, h, :]).then_inc(S(f"o_ps{d}"), 1)
                    if u < 3:
                        pe.wait_ge(S(f"kd{d}"), u + 1)
                        four(pB[d], lambda h: NTu[u % 2][d][:, h, :], lambda h: vnew[d][:, h, :]).then_inc(S(f"s_ps{d}"), 1)
            pe.wait_ge(S("normed"), 4)

            def columns(nth, src):
                for k in range(KD):
                    if k >= 2:
                        pe.wait_ge(S("cols_ev"), nth * KD + k - 1)
                    for t in range(T):
                        ins = tr(ps[2 + k % 2][:, t * P:(t + 1) * P], src(k, t), ident)
                    ins.then_inc(S("cols_ps"), 1)

            columns(0, lambda k, t: (oacc if k < 4 else yacc)[:, t, (k % 4) * P:(k % 4 + 1) * P])
            pe.wait_ge(S("dg"), 16)
            for i in range(16):
                ins = mm(ps[(0, 1, 6, 7)[i // 4]][:, (i % 4) * P:(i % 4 + 1) * P], ones, dg[i], start=True, stop=True)
                if i % 4 == 3:
                    ins.then_inc(S("dg_ps"), 1)
            pe.wait_ge(S("cols_ev"), 8)

            def token_rows(bank, w, src, t, n, name, as_normed=False):
                for k in range(KD):
                    if as_normed:
                        pe.wait_ge(S("o_norm"), k + 1)
                    ins = mm(ps[bank][:, 0:n], src[:, k, t * P:(t + 1) * P], w[:, k, :], start=(k == 0),
                             stop=(k == KD - 1))
                ins.then_inc(S(name), 1)

            for c in range(2):
                w = arrived(pe, wo_ch[c])
                if c == 1:
                    pe.wait_ge(S("gain_rows"), 4)
                for t in range(T):
                    token_rows(4 + 2 * c + t, w, mixT, t, 512, "wo_ps")
            pe.wait_ge(S("xh"), 6)
            columns(1, lambda k, t: xh[:, t, k * P:(k + 1) * P])
            pe.wait_ge(S("cols_ev"), 16)
            for b in range(KF):
                if b % 4 == 0:
                    wg = arrived(pe, ga_ch[b // 4])
                at = slice((b % 4) * P, (b % 4 + 1) * P)
                if b >= 2:
                    pe.wait_ge(S("f_taps"), b - 1)
                for k in range(KD):
                    ins = mm(ps[b % 2][:, 0:L], wg[:, k, at], hT2[:, k, :], start=(k == 0), stop=(k == KD - 1))
                ins.then_inc(S("gate_ps"), 1)
                if b % 4 == 0:
                    wu = arrived(pe, up_ch[b // 4])
                if b >= 2:
                    pe.wait_ge(S("f_hid"), b - 1)
                for k in range(KD):
                    ins = mm(ps[2 + b % 2][:, 0:L], wu[:, k, at], hT2[:, k, :], start=(k == 0), stop=(k == KD - 1))
                ins.then_inc(S("up_ps"), 1)
            pe.wait_ge(S("x_step"), 4)
            for c in range(6):
                w = arrived(pe, dn_ch[c])
                if c == 5:
                    pe.wait_ge(S("f_hid"), KF)
                    for t in range(T):
                        for h in range(2):
                            for k in range(4 * c, KF):
                                ins = mm(ps[4 + 2 * t + h][:, :], hid[:, k, t * P:(t + 1) * P],
                                         w[:, k - 4 * c, 512 * h:512 * h + 512], start=False, stop=(k == KF - 1))
                            ins.then_inc(S("down_ps"), 1)
                    continue
                for kk in range(4):
                    k = 4 * c + kk
                    if kk == 0:
                        pe.wait_ge(S("f_hid"), min(k + 4, KF))
                    for t in range(T):
                        for h in range(2):
                            ins = mm(ps[4 + 2 * t + h][:, :], hid[:, k, t * P:(t + 1) * P],
                                     w[:, kk, 512 * h:512 * h + 512], start=(k == 0), stop=False)
                ins.then_inc(S("down_ps"), 1)
            pe.wait_ge(S("xh"), 8)
            columns(2, lambda k, t: xh[:, t, k * P:(k + 1) * P])
            pe.wait_ge(S("cols_ev"), 24)
            for i, (c0, n) in enumerate(IN2):
                w = arrived(pe, in2_ch[i])
                for t in range(T):
                    j = 2 * i + t
                    if j >= 4:
                        pe.wait_ge(S("in2_ev"), j - 3)
                    token_rows(4 + j % 4, w, uT, t, n, "in2_ps")
            for i in range(13):
                if i == 0:
                    pe.wait_ge(S("rot_a"), 2)
                if i == 5:
                    pe.wait_ge(S("rot_b"), 2)
                if i >= 2:
                    pe.wait_ge(S("qt_ev"), i - 1)
                for hh in range(2):
                    head = 2 * i + hh
                    c0 = head * HD if head < 10 else 768 + (head - 10) * HD
                    for t in range(T):
                        ins = tr(ps[i % 2][0:HD, hh * L + t * P:hh * L + (t + 1) * P], pj[:, t, c0:c0 + HD], ident)
                ins.then_inc(S("qt_ps"), 1)
            pe.wait_ge(S("qt_ev"), 13)
            pe.wait_ge(S("in2_ev"), 10)

            def scores(h):
                qi, ki = (h, 8 + h // 4) if h < 8 else (2 + h, 10 + h)
                if h >= 2:
                    pe.wait_ge(S("s_exp"), 2 * (h - 1))
                for t in range(T):
                    ins = mm(ps[h % 2][:, t * L:(t + 1) * L], qkT[0:HD, qi, t * P:(t + 1) * P], qkT[0:HD, ki, :],
                             start=True, stop=True)
                ins.then_inc(S("s_ps"), 1)

            def prob_rows(h):
                pe.wait_ge(S("pr"), h + 1)
                if h >= 2:
                    pe.wait_ge(S("pt_ev"), h - 1)
                for kt in range(2):
                    for t in range(T):
                        ins = tr(ps[2 + h % 2][:, (2 * kt + t) * P:(2 * kt + t + 1) * P],
                                 pr[h % 2][:, t, kt * P:(kt + 1) * P], ident)
                ins.then_inc(S("pt_ps"), 1)

            def values(h):
                vc = 640 + HD * (h // 4) if h < 8 else 1792 + HD * (h - 8)
                pe.wait_ge(S("pt_ev"), h + 1)
                e0, c0 = HD * (h % 2), L * (h // 2 % 2)
                for kt in range(2):
                    ins = mm(ps[4 + h // 4][e0:e0 + HD, c0:c0 + L], pj[:, kt, vc:vc + HD],
                             prT[h % 2][:, kt, :, :].rearrange("p t q -> p (t q)"), start=(kt == 0), stop=(kt == 1))
                ins.then_inc(S("pv_ps"), 1)

            for h in range(19):
                if h < 16:
                    scores(h)
                if 2 <= h < 18:
                    prob_rows(h - 2)
                if h >= 3:
                    values(h - 3)
            for k in range(KD):
                pe.wait_ge(S("sqT"), k // 2 + 1)
                ins = mm(ps[0][:, L * (k // 4):L * (k // 4) + L], ones, sqT[:, L * k:L * k + L], start=(k % 4 == 0),
                         stop=(k % 4 == 3))
            ins.then_inc(S("ss_ps"), 1)
            for c in range(2):
                w = arrived(pe, wo2_ch[c])
                for t in range(T):
                    token_rows(2 * c + t, w, uT, t, 512, "wo2_ps", c == t == 0)
            pe.wait_ge(S("xh"), 10)
            columns(3, lambda k, t: xh[:, t, k * P:(k + 1) * P])
            pe.wait_ge(S("cols_ev"), 32)
            pe.wait_ge(S("in_rw"), 16)
            for t in range(T):
                for k in range(KD):
                    ins = mm(ps[0][:, t * 36:(t + 1) * 36], u2T[:, k, t * P:(t + 1) * P], rw[:, k, :],
                             start=(k == 0), stop=(k == KD - 1))
            ins.then_inc(S("one_ps"), 1)
            pe.wait_ge(S("flag"), 1)
            flag = ra[4]
            mm(ps[1][:, 0:NE], C("strict", P), flag[:, 0, :], start=True, stop=True)
            mm(ps[1][:, NE:2 * NE], ones, flag[:, 0, :], start=True, stop=False)
            mm(ps[1][:, NE:2 * NE], C("strict", P), flag[:, 1, :], start=False, stop=True)
            mm(ps[1][:, 2 * NE:3 * NE], ones, flag[:, 0, :], start=True, stop=False)
            mm(ps[1][:, 2 * NE:3 * NE], ones, flag[:, 1, :], start=False, stop=True).then_inc(S("one_ps"), 1)
            def gather(n):
                pe.wait_ge(S("sel"), n)
                for k in range(KD):
                    for t in range(T):
                        ins = mm(ps[6 + k // 4][:, (k % 4) * P:(k % 4 + 1) * P], u2[:, t, k * P:(k + 1) * P],
                                 sel[:, t, :], start=(t == 0), stop=(t == 1))
                ins.then_inc(S("gather_ps"), 1)

            def product(p, bank, s, left, nk, c0, name):
                for j in range(2):
                    if c0 == 0:
                        pe.wait_ge(S(f"loaded{s + j}"), p * 16 + 16 * (base[s + j] + 1))
                w = [slot(s + j).rearrange("p (k n) -> p k n", k=nk) for j in range(2)]
                for k in range(nk):
                    for j in range(2):
                        ins = mm(ps[bank][j * SLOT:(j + 1) * SLOT, :], left[:, k, j * SLOT:(j + 1) * SLOT],
                                 w[j][:, k, c0:c0 + 512], start=(k == 0), stop=(k == nk - 1))
                ins.then_inc(S(name), 1)

            def scatter(p, last):
                pe.wait_ge(S("yn_a"), p + 1)
                pe.wait_ge(S("yn_v"), p + 1)
                pe.wait_ge(S("gt_ev"), p + 1)
                for t in range(T):
                    for c in range(2):
                        ins = mm(ps[2 * t + c][:, :], gselT[:, t * P:(t + 1) * P], yN[:, 512 * c:512 * c + 512],
                                 start=False, stop=last)
                        if last:
                            ins.then_inc(S("sc_ps"), 1)

            gather(1)
            pe.wait_ge(S("yn_a"), 1)
            for t in range(T):
                for c in range(2):
                    mm(ps[2 * t + c][:, :], yN[:, 0:P], u2[:, 0, 0:512], start=True, stop=False)

            def pair(p):
                pe.wait_ge(S("xsel_a"), p + 1)
                pe.wait_ge(S("xsel_v"), p + 1)
                pe.wait_ge(S("yn_a"), p + 1)
                product(p, 5, 0, xsel, KD, 0, "eg_ps")
                pe.wait_ge(S("yn_v"), p + 1)
                product(p, 4, 2, xsel, KD, 0, "eu_ps")
                scatter(p, False)
                pe.wait_ge(S("hid"), p + 1)
                for f in range(4):
                    ins = tr(ps[5][:, f * P:(f + 1) * P], hidN[:, f * P:(f + 1) * P], ident)
                ins.then_inc(S("hidT_ps"), 1)
                gather(p + 2)
                pe.wait_ge(S("hidT_ev"), p + 1)
                product(p, 5, 4, hidT, 4, 0, "yn_ps")
                product(p, 4, 4, hidT, 4, 512, "yn_ps")
                pe.wait_ge(S("gsel"), p + 1)
                pe.wait_ge(S("xsel_a"), p + 2)
                for t in range(T):
                    ins = tr(ps[6][:, t * P:(t + 1) * P], gsel[:, t, :], ident)
                ins.then_inc(S("gt_ps"), 1)

            pair(0)
            pe.wait_ge(S("count_ready"), 1)
            npairs = pe.value_load(units[0:1, NU:NU + 1], min_val=NPAIR, max_val=NU // 2)
            with pe.Fori(1, npairs) as p:
                pair(p)
            scatter(npairs, True)


def constants():
    import numpy as np
    c = np.zeros((P, NCO), np.float32)
    j, i = np.arange(P)[:, None], np.arange(P)[None, :]
    c[:, CO["ident"]:CO["ident"] + P] = i == j
    c[:, CO["ones"]:CO["ones"] + P] = 1
    c[:, CO["mf"]:CO["mf"] + P] = i >= j
    c[:, CO["mb"]:CO["mb"] + P] = i <= j
    c[:, CO["strict"]:CO["strict"] + P] = i > j
    for lv in range(LEVELS):
        s = 2 ** lv
        m = (i // (2 * s) == j // (2 * s)) & (j % (2 * s) < s) & (i % (2 * s) >= s)
        c[:, CO["lvl"] + lv * P:CO["lvl"] + (lv + 1) * P] = m
        c[:, CO["lvl"] + (LEVELS + lv) * P:CO["lvl"] + (LEVELS + lv + 1) * P] = m.T
    c[:, CO["iota"]:CO["iota"] + SLOT] = np.arange(SLOT)
    c[:, CO["desc"]:CO["desc"] + NE] = NE - np.arange(NE)
    c[:, CO["fold"]:CO["fold"] + 32] = j % 32 == i[:, 0:32]
    c[:, CO["eps"]:CO["eps"] + 4] = (EPS, EPS * P, 1.0, 0.0)

    def inv(dim):
        e = np.arange(0, dim, 2, dtype=np.float32) / np.float32(dim)
        return (np.float32(1.0) / (np.float32(10000.0) ** e)).astype(np.float32)

    tok = np.arange(L)
    row, colm = (tok // GRID).astype(np.float32), (tok % GRID).astype(np.float32)
    axial = np.concatenate([row[:, None] * inv(HD // 2), colm[:, None] * inv(HD // 2)], axis=1)
    linear = tok.astype(np.float32)[:, None] * inv(HD)
    for kind, ang in enumerate((axial, linear)):
        cos, sin = np.cos(ang.astype(np.float64)), np.sin(ang.astype(np.float64))
        tab = np.concatenate([cos, cos, -sin, sin], axis=1).astype(np.float32)
        for t in range(T):
            at = CO["rope"] + (kind * T + t) * 2 * HD
            c[:, at:at + 2 * HD] = tab[t * P:(t + 1) * P]
    q, k = tok[:, None], tok[None, :]
    count = np.zeros((L, L))
    for window, dil in ((128, 1), (512, 4), (2048, 16)):
        count += (q % dil == k % dil) & (np.abs(q // dil - k // dil) <= window // (2 * dil))
    bias = np.where(count > 0, np.log(np.maximum(count, 1)), -1e30).astype(np.float32)
    return c, bias


def kernel(**inputs):
    import numpy as np
    import concourse.bacc as _bacc
    from concourse.bass_utils import run_bass_kernel_spmd as _run

    v = {n: np.asarray(a) for n, a in inputs.items()}
    r = lambda n: v[n].reshape(-1, P)
    w_in = v["w_in"][0]
    vec = np.concatenate([
        r("b_ada"), r("norm1_g"), r("norm2_g"), r("gdn_conv_w"), r("ssm_conv_w"), r("ssm_conv_b"),
        np.repeat(r("gdn_norm_g"), 4, axis=0), r("ssm_norm_g"), r("norm1_g_2"), r("out_norm_a_g_2"),
        r("out_norm_b_g_2"), r("norm2_g_2"), r("ffn_conv_w"), r("ffn_conv_b")], axis=0)
    vec = np.concatenate([vec, np.zeros((NROWS - vec.shape[0], P), np.float32)], axis=0)
    both = lambda a, b: np.concatenate([a[0, 0], b[0, 0], a[0, 1], b[0, 1]])
    rowv = np.concatenate([
        both(v["gdn_dt_bias"], v["ssm_dt_bias"]), both(v["gdn_A_log"], v["ssm_A_log"]), v["ssm_D"][0],
        v["q_norm_g_2"][0], v["k_norm_g_2"][0], v["router_group_b_2"][0], v["router_expert_b_2"][0]])
    small = np.concatenate([w_in[:, 2048:2052], w_in[:, 3600:3608], w_in[:, 2052:2056], w_in[:, 3608:3616],
                            w_in[:, 2056:2064]], axis=1)
    consts, bias = constants()
    cc = np.stack([v["c"].reshape(KD, P).T, v["c_ctx"].reshape(KD, P).T], axis=2)
    arrays = {
        "x": v["x"][0], "ctx": v["ctx"][0], "cc": cc, "vec_rows": vec, "rowv": rowv[None, :], "w_small": small,
        "consts": consts, "bias": bias, "w_ada": v["w_ada"][0], "w_in": w_in, "w_out": v["w_out"][0],
        "w_gate": v["ffn_w_gate"][0], "w_up": v["ffn_w_up"][0], "w_down": v["ffn_w_down"][0],
        "fng": v["final_norm_g"][None, :], "fng2": v["final_norm_g_2"][None, :], "n2row": v["norm2_g_2"],
        "w_in2": v["w_in_2"][0], "w_out2": v["w_out_2"][0],
        "rw": np.concatenate([v["router_group_w_2"][0], v["router_expert_w_2"][0]], axis=1),
        "e_gate": v["w_gate_2"][0], "e_up": v["w_up_2"][0], "e_down": v["w_down_2"][0],
    }
    arrays = {n: np.ascontiguousarray(a) for n, a in arrays.items()}
    nc = _bacc.Bacc("TRN2", target_bir_lowering=False, num_devices=1)
    ap = {n: nc.dram_tensor("in_" + n, a.shape, mybir.dt.from_np(a.dtype), kind="ExternalInput").ap()
          for n, a in arrays.items()}
    out = nc.dram_tensor("out", (L, D), mybir.dt.float32, kind="ExternalOutput").ap()
    build(nc, ap, out)
    got = _run(nc, [{"in_" + n: a for n, a in arrays.items()}], core_ids=[0])
    return got.results[0]["out"].reshape(1, L, D)
```
